# Optimizing a Trainium2 kernel written in Bass

```python
import math
import jax
import jax.numpy as jnp
from jax import lax
import numpy as np
import jax, jax.numpy as jnp

D_MODEL = 1024
BATCH = 1
SEQ = 512
DEPTH = 1

EPS = 1e-6
D_MIX = D_MODEL

GLA_HEADS = 4
GLA_DK = 64
GLA_DV = 128
GLA_WIDTH = GLA_HEADS * GLA_DV
GLA_QK_WIDTH = GLA_HEADS * GLA_DK
GLA_GATE_RANK = 16
GLA_GATE_NORMALIZER = 16.0
GLA_CHUNK = 64

SSD_HEADS = 8
SSD_HEAD_DIM = 64
SSD_WIDTH = SSD_HEADS * SSD_HEAD_DIM
SSD_GROUPS = 2
SSD_STATE = 64
SSD_CONV = 4
SSD_CHUNK = 128
SSD_BC_WIDTH = SSD_GROUPS * SSD_STATE
SSD_CONV_DIM = SSD_WIDTH + 2 * SSD_BC_WIDTH

IN_SIZES = (GLA_QK_WIDTH, GLA_QK_WIDTH, GLA_WIDTH, GLA_GATE_RANK, GLA_WIDTH,
            SSD_WIDTH, SSD_CONV_DIM, SSD_HEADS)
IN_TOTAL = (2 * GLA_QK_WIDTH + 2 * GLA_WIDTH + GLA_GATE_RANK
            + SSD_WIDTH + SSD_CONV_DIM + SSD_HEADS)

PEER_HEADS = 8
PEER_KEYS = 128
PEER_EXPERTS = PEER_KEYS * PEER_KEYS
PEER_TOPK = 16
PEER_DQ = 256
PEER_HALF = PEER_DQ // 2
PEER_BLOCK = 128


def rmsnorm(x, w):
    xf = x.astype(jnp.float32)
    xf = xf * lax.rsqrt(jnp.mean(xf * xf, axis=-1, keepdims=True) + EPS)
    return xf * w.astype(jnp.float32)

def split_cols(proj):
    out, start = [], 0
    for size in IN_SIZES:
        out.append(proj[..., start:start + size])
        start += size
    return out

def gla_mixer(q, k, v, gate_lr, g_out, w_gate2, b_gate, norm_w):
    f32 = jnp.float32
    b, l, _ = q.shape
    nc, C, H = l // GLA_CHUNK, GLA_CHUNK, GLA_HEADS
    q = q.astype(f32).reshape(b, nc, C, H, GLA_DK) * (GLA_DK ** -0.5)
    k = k.astype(f32).reshape(b, nc, C, H, GLA_DK)
    v = v.astype(f32).reshape(b, nc, C, H, GLA_DV)
    log_a = jax.nn.log_sigmoid((gate_lr.astype(f32) @ w_gate2.astype(f32)
                                + b_gate.astype(f32))) / GLA_GATE_NORMALIZER
    log_a = log_a.reshape(b, nc, C, H, GLA_DK)
    G = jnp.cumsum(log_a, axis=2)
    G_last = G[:, :, -1:]
    q_in = q * jnp.exp(G)
    k_in = k * jnp.exp(-G)
    k_end = k * jnp.exp(G_last - G)
    causal = jnp.tril(jnp.ones((C, C), dtype=bool))
    att = jnp.einsum('bcihd,bcjhd->bchij', q_in, k_in)
    att = jnp.where(causal, att, 0.0)
    o_intra = jnp.einsum('bchij,bcjhv->bcihv', att, v)
    chunk_state = jnp.einsum('bcjhd,bcjhv->bchdv', k_end, v)
    chunk_decay = jnp.exp(G_last[:, :, 0])

    def step(S, inp):
        dec, st = inp
        return dec[..., None] * S + st, S

    S0 = jnp.zeros((b, H, GLA_DK, GLA_DV), f32)
    _, S_prev = lax.scan(step, S0, (jnp.moveaxis(chunk_decay, 1, 0),
                                    jnp.moveaxis(chunk_state, 1, 0)))
    S_prev = jnp.moveaxis(S_prev, 0, 1)
    o_inter = jnp.einsum('bcihd,bchdv->bcihv', q_in, S_prev)
    o = (o_intra + o_inter).reshape(b, l, H, GLA_DV)
    o = rmsnorm(o, norm_w)
    return o.reshape(b, l, GLA_WIDTH) * jax.nn.silu(g_out.astype(f32))

def causal_depthwise_conv(x, w, bias):
    c = x.shape[-1]
    out = lax.conv_general_dilated(
        x, w.astype(x.dtype)[:, None, :], window_strides=(1,),
        padding=[(SSD_CONV - 1, 0)], dimension_numbers=('NWC', 'WIO', 'NWC'),
        feature_group_count=c)
    return out + bias.astype(x.dtype)

def ssd_mixer(z, xbc, dt_raw, conv_w, conv_b, dt_bias, a_log, d_skip, norm_w):
    f32 = jnp.float32
    b, l, _ = z.shape
    nc, C = l // SSD_CHUNK, SSD_CHUNK
    G, J, P, N = SSD_GROUPS, SSD_HEADS // SSD_GROUPS, SSD_HEAD_DIM, SSD_STATE
    xbc = jax.nn.silu(causal_depthwise_conv(xbc.astype(f32), conv_w, conv_b))
    xs = xbc[..., :SSD_WIDTH]
    Bm = xbc[..., SSD_WIDTH:SSD_WIDTH + SSD_BC_WIDTH].reshape(b, nc, C, G, N)
    Cm = xbc[..., SSD_WIDTH + SSD_BC_WIDTH:].reshape(b, nc, C, G, N)
    X = xs.reshape(b, nc, C, G, J, P)
    dt = jax.nn.softplus(dt_raw.astype(f32) + dt_bias.astype(f32)).reshape(b, nc, C, G, J)
    A = -jnp.exp(a_log.astype(f32)).reshape(G, J)
    a = dt * A
    a_cum = jnp.cumsum(a, axis=2)
    seg = a_cum[:, :, :, None] - a_cum[:, :, None]
    causal = jnp.tril(jnp.ones((C, C), dtype=bool))[:, :, None, None]
    Lmat = jnp.exp(jnp.where(causal, seg, -jnp.inf))
    Xdt = X * dt[..., None]
    scores = jnp.einsum('bclgn,bcsgn->bclsg', Cm, Bm)
    y_diag = jnp.einsum('bclsg,bclsgj,bcsgjp->bclgjp', scores, Lmat, Xdt)
    decay_to_end = jnp.exp(a_cum[:, :, -1:] - a_cum)
    states = jnp.einsum('bclgn,bclgj,bclgjp->bcgjpn', Bm, decay_to_end, Xdt)
    chunk_decay = jnp.exp(a_cum[:, :, -1])

    def step(S, inp):
        dec, st = inp
        return dec[..., None, None] * S + st, S

    S0 = jnp.zeros((b, G, J, P, N), f32)
    _, S_prev = lax.scan(step, S0, (jnp.moveaxis(chunk_decay, 1, 0),
                                    jnp.moveaxis(states, 1, 0)))
    S_prev = jnp.moveaxis(S_prev, 0, 1)
    y_off = jnp.einsum('bclgn,bcgjpn,bclgj->bclgjp', Cm, S_prev, jnp.exp(a_cum))
    y = y_diag + y_off + X * d_skip.astype(f32).reshape(G, J)[..., None]
    y = y.reshape(b, l, SSD_WIDTH) * jax.nn.silu(z.astype(f32))
    y = y.reshape(b, l, G, SSD_WIDTH // G)
    y = y * lax.rsqrt(jnp.mean(y * y, axis=-1, keepdims=True) + EPS)
    return y.reshape(b, l, SSD_WIDTH) * norm_w.astype(f32)

def peer_ffn(xn, w_query, sub_keys, u, v):
    f32 = jnp.float32
    b, l, d = xn.shape
    T = b * l
    H, K = PEER_HEADS, PEER_TOPK
    xt = xn.reshape(T, d).astype(u.dtype)
    q = (xt @ w_query).reshape(T, H, 2, PEER_HALF)
    s = jnp.einsum('thpd,hpkd->thpk', q, sub_keys).astype(f32)
    top_s, top_i = lax.top_k(s, K)
    cand_s = (top_s[:, :, 0, :, None] + top_s[:, :, 1, None, :]).reshape(T, H, K * K)
    cand_i = (top_i[:, :, 0, :, None] * PEER_KEYS + top_i[:, :, 1, None, :]).reshape(T, H, K * K)
    best_s, best_pos = lax.top_k(cand_s, K)
    expert_idx = jnp.take_along_axis(cand_i, best_pos, axis=-1)
    gate = jax.nn.softmax(best_s, axis=-1)
    nb = T // PEER_BLOCK
    xb = xt.reshape(nb, PEER_BLOCK, d)
    ib = expert_idx.reshape(nb, PEER_BLOCK, H * K)
    gb = gate.reshape(nb, PEER_BLOCK, H * K)

    def block(args):
        x_blk, i_blk, g_blk = args
        act = jnp.einsum('td,ted->te', x_blk, u[i_blk]).astype(f32)
        hid = jax.nn.gelu(act, approximate=False) * g_blk
        return jnp.einsum('te,ted->td', hid.astype(v.dtype), v[i_blk])

    out = lax.map(block, (xb, ib, gb))
    return out.reshape(b, l, d)

def first_inputs(seed: int = 0) -> dict:
    key = jax.random.key(seed)
    ks = jax.random.split(key, 24)
    f32 = jnp.float32
    nrm = lambda k, shape, scale: jax.random.normal(k, shape, f32) * scale
    dt0 = jnp.exp(jax.random.uniform(ks[10], (DEPTH, SSD_HEADS), f32,
                                     math.log(1e-3), math.log(1e-1)))
    return {
        "x": jax.random.normal(ks[0], (BATCH, SEQ, D_MODEL), f32),
        "norm_mix_w": 1.0 + nrm(ks[1], (DEPTH, D_MODEL), 0.02),
        "w_in": nrm(ks[2], (DEPTH, D_MODEL, IN_TOTAL), D_MODEL ** -0.5),
        "gla_w_gate2": nrm(ks[3], (DEPTH, GLA_GATE_RANK, GLA_QK_WIDTH), GLA_GATE_RANK ** -0.5),
        "gla_b_gate": nrm(ks[4], (DEPTH, GLA_QK_WIDTH), 0.1),
        "gla_norm_w": 1.0 + nrm(ks[5], (DEPTH, GLA_DV), 0.02),
        "ssd_conv_w": nrm(ks[6], (DEPTH, SSD_CONV, SSD_CONV_DIM), SSD_CONV ** -0.5),
        "ssd_conv_b": nrm(ks[7], (DEPTH, SSD_CONV_DIM), 0.02),
        "ssd_dt_bias": dt0 + jnp.log(-jnp.expm1(-dt0)),
        "ssd_a_log": jnp.log(jax.random.uniform(ks[8], (DEPTH, SSD_HEADS), f32, 1.0, 16.0)),
        "ssd_d": 1.0 + nrm(ks[9], (DEPTH, SSD_HEADS), 0.1),
        "ssd_norm_w": 1.0 + nrm(ks[11], (DEPTH, SSD_WIDTH), 0.02),
        "w_out": nrm(ks[12], (DEPTH, D_MIX, D_MODEL), D_MIX ** -0.5),
        "norm_ffn_w": 1.0 + nrm(ks[13], (DEPTH, D_MODEL), 0.02),
        "peer_w_query": nrm(ks[14], (DEPTH, D_MODEL, PEER_HEADS * PEER_DQ), D_MODEL ** -0.5),
        "peer_sub_keys": nrm(ks[15], (DEPTH, PEER_HEADS, 2, PEER_KEYS, PEER_HALF), PEER_HALF ** -0.5),
        "peer_u": nrm(ks[16], (DEPTH, PEER_EXPERTS, D_MODEL), D_MODEL ** -0.5),
        "peer_v": nrm(ks[17], (DEPTH, PEER_EXPERTS, D_MODEL), PEER_HEADS ** -0.5),
        "norm_final_w": 1.0 + nrm(ks[18], (D_MODEL,), 0.02),
    }

def first_block(x, norm_mix_w, w_in, gla_w_gate2, gla_b_gate, gla_norm_w,
              ssd_conv_w, ssd_conv_b, ssd_dt_bias, ssd_a_log, ssd_d, ssd_norm_w,
              w_out, norm_ffn_w, peer_w_query, peer_sub_keys, peer_u, peer_v,
              norm_final_w):
    h = x
    for i in range(DEPTH):
        n = rmsnorm(h, norm_mix_w[i]).astype(w_in.dtype)
        proj = n @ w_in[i]
        q, k, v, gate_lr, g_out, z, xbc, dt_raw = split_cols(proj)
        o_gla = gla_mixer(q, k, v, gate_lr, g_out, gla_w_gate2[i], gla_b_gate[i], gla_norm_w[i])
        o_ssd = ssd_mixer(z, xbc, dt_raw, ssd_conv_w[i], ssd_conv_b[i], ssd_dt_bias[i],
                          ssd_a_log[i], ssd_d[i], ssd_norm_w[i])
        mixed = jnp.concatenate([o_gla, o_ssd], axis=-1).astype(w_out.dtype)
        h = h + (mixed @ w_out[i]).astype(h.dtype)
        n2 = rmsnorm(h, norm_ffn_w[i])
        h = h + peer_ffn(n2, peer_w_query[i], peer_sub_keys[i], peer_u[i], peer_v[i]).astype(h.dtype)
    return rmsnorm(h, norm_final_w).astype(x.dtype)


CHUNK = 64
D_CONV = 1024
CONV_WIDTH = 3
HEAD_DIM = 64
N_HEADS = 16
D_ATT = N_HEADS * HEAD_DIM
Q_BLOCK = 128
N_GROUPS = 4
EXPERTS_PER_GROUP = 8
N_EXPERTS = N_GROUPS * EXPERTS_PER_GROUP
TOP_K = 2
D_EXPERT = 512
MOE_BLOCK = 256

SPLITS = (D_CONV, D_CONV, D_CONV, D_ATT, D_ATT, D_ATT, N_HEADS, D_MODEL, D_MODEL)
D_IN_PROJ = sum(SPLITS)


def rmsnorm_2(x, g):
    xf = x.astype(jnp.float32)
    y = xf * lax.rsqrt(jnp.mean(xf * xf, axis=-1, keepdims=True) + EPS)
    return (y * g.astype(jnp.float32)).astype(x.dtype)

def split_cols_2(p):
    idx = np.cumsum(np.array(SPLITS))[:-1].tolist()
    return jnp.split(p, idx, axis=-1)

def short_conv(b, c, u, conv_w, conv_b):
    S = u.shape[1]
    z = c * u
    zp = jnp.pad(z, ((0, 0), (CONV_WIDTH - 1, 0), (0, 0)))
    acc = conv_b
    for i in range(CONV_WIDTH):
        acc = acc + conv_w[i] * zp[:, i:i + S]
    return b * acc

def forgetting_attention(q, k, v, f_logit, b_forget):
    B, S, H, dh = q.shape
    log_f = jax.nn.log_sigmoid(f_logit.astype(jnp.float32) + b_forget.astype(jnp.float32))
    cum = jnp.transpose(jnp.cumsum(log_f, axis=1), (0, 2, 1))
    scale = 1.0 / math.sqrt(dh)
    outs = []
    for qb in range(S // Q_BLOCK):
        qs, qe = qb * Q_BLOCK, (qb + 1) * Q_BLOCK
        qblk = q[:, qs:qe]
        kp, vp = k[:, :qe], v[:, :qe]
        s = jnp.einsum('bqhd,bkhd->bhqk', qblk, kp).astype(jnp.float32) * scale
        s = s + (cum[:, :, qs:qe, None] - cum[:, :, None, :qe])
        t_pos = jnp.arange(qs, qe)[:, None]
        s_pos = jnp.arange(qe)[None, :]
        s = jnp.where(s_pos <= t_pos, s, -jnp.inf)
        p = jax.nn.softmax(s, axis=-1).astype(v.dtype)
        outs.append(jnp.einsum('bhqk,bkhd->bqhd', p, vp))
    return jnp.concatenate(outs, axis=1)

def token_mixer(h, w_in, conv_w, conv_b, b_forget, w_conv_out, w_att_out, w_out):
    B, S, _ = h.shape
    proj = h @ w_in
    cb, cc, cu, q, k, v, f_logit, g_conv, g_att = split_cols_2(proj)
    y_conv = short_conv(cb, cc, cu, conv_w, conv_b) @ w_conv_out
    o = forgetting_attention(q.reshape(B, S, N_HEADS, HEAD_DIM),
                             k.reshape(B, S, N_HEADS, HEAD_DIM),
                             v.reshape(B, S, N_HEADS, HEAD_DIM),
                             f_logit, b_forget)
    y_att = o.reshape(B, S, D_ATT) @ w_att_out
    m = jax.nn.sigmoid(g_conv) * y_conv + jax.nn.sigmoid(g_att) * y_att
    return m @ w_out

def hier_moe(h, w_router_group, w_router_expert, w_e_gate, w_e_up, w_e_down):
    B, S, D = h.shape
    T = B * S
    hf = h.reshape(T, D)
    pg = jax.nn.softmax((hf @ w_router_group).astype(jnp.float32), axis=-1)
    g_val, g_idx = lax.top_k(pg, 1)
    le = jnp.einsum('td,gde->tge', hf, w_router_expert).astype(jnp.float32)
    le_sel = jnp.take_along_axis(le, g_idx[:, :, None], axis=1)[:, 0]
    pe = jax.nn.softmax(le_sel, axis=-1)
    e_val, e_idx = lax.top_k(pe, TOP_K)
    e_val = e_val / jnp.sum(e_val, axis=-1, keepdims=True)
    w_tok = (g_val * e_val).astype(h.dtype)
    expert = (g_idx * EXPERTS_PER_GROUP + e_idx).astype(jnp.int32)

    A = T * TOP_K
    flat_e = expert.reshape(A)
    flat_w = w_tok.reshape(A)
    flat_tok = jnp.arange(A, dtype=jnp.int32) // TOP_K
    order = jnp.argsort(flat_e)
    sorted_e = flat_e[order]
    counts = jnp.bincount(flat_e, length=N_EXPERTS)
    padded = (counts + MOE_BLOCK - 1) // MOE_BLOCK * MOE_BLOCK
    start_sorted = jnp.cumsum(counts) - counts
    end_padded = jnp.cumsum(padded)
    start_padded = end_padded - padded
    rank = jnp.arange(A, dtype=jnp.int32) - start_sorted[sorted_e]
    dest = start_padded[sorted_e] + rank
    n_rows = A + N_EXPERTS * MOE_BLOCK
    n_blocks = n_rows // MOE_BLOCK
    row_tok = jnp.zeros((n_rows,), jnp.int32).at[dest].set(flat_tok[order])
    row_w = jnp.zeros((n_rows,), h.dtype).at[dest].set(flat_w[order])
    block_e = jnp.minimum(
        jnp.searchsorted(end_padded, jnp.arange(n_blocks) * MOE_BLOCK, side='right'),
        N_EXPERTS - 1).astype(jnp.int32)
    x_rows = hf[row_tok].reshape(n_blocks, MOE_BLOCK, D)

    def expert_block(args):
        xb, e = args
        a = xb @ w_e_gate[e]
        u = xb @ w_e_up[e]
        return (jax.nn.silu(a) * u) @ w_e_down[e]

    y_rows = lax.map(expert_block, (x_rows, block_e)).reshape(n_rows, D)
    y = jax.ops.segment_sum(y_rows * row_w[:, None], row_tok, num_segments=T)
    return y.reshape(B, S, D)

def second_inputs(seed: int = 0) -> dict:
    key = jax.random.key(seed)
    ks = jax.random.split(key, 20)
    f32 = jnp.float32
    nrm = lambda k, shape, fan: jax.random.normal(k, shape, f32) * (fan ** -0.5)
    return {
        "x": jax.random.normal(ks[0], (BATCH, SEQ, D_MODEL), f32),
        "norm_mix_g": 1.0 + 0.02 * jax.random.normal(ks[1], (D_MODEL,), f32),
        "w_in": nrm(ks[2], (D_MODEL, D_IN_PROJ), D_MODEL),
        "conv_w": nrm(ks[3], (CONV_WIDTH, D_CONV), CONV_WIDTH),
        "conv_b": 0.01 * jax.random.normal(ks[4], (D_CONV,), f32),
        "b_forget": jax.random.uniform(ks[5], (N_HEADS,), f32, 1.0, 6.0),
        "w_conv_out": nrm(ks[6], (D_CONV, D_MODEL), D_CONV),
        "w_att_out": nrm(ks[7], (D_ATT, D_MODEL), D_ATT),
        "w_out": nrm(ks[8], (D_MODEL, D_MODEL), D_MODEL),
        "norm_ffn_g": 1.0 + 0.02 * jax.random.normal(ks[9], (D_MODEL,), f32),
        "w_router_group": nrm(ks[10], (D_MODEL, N_GROUPS), D_MODEL),
        "w_router_expert": nrm(ks[11], (N_GROUPS, D_MODEL, EXPERTS_PER_GROUP), D_MODEL),
        "w_e_gate": nrm(ks[12], (N_EXPERTS, D_MODEL, D_EXPERT), D_MODEL),
        "w_e_up": nrm(ks[13], (N_EXPERTS, D_MODEL, D_EXPERT), D_MODEL),
        "w_e_down": nrm(ks[14], (N_EXPERTS, D_EXPERT, D_MODEL), D_EXPERT),
        "norm_final_g": 1.0 + 0.02 * jax.random.normal(ks[15], (D_MODEL,), f32),
    }

def second_block(x, norm_mix_g, w_in, conv_w, conv_b, b_forget, w_conv_out, w_att_out, w_out,
              norm_ffn_g, w_router_group, w_router_expert, w_e_gate, w_e_up, w_e_down,
              norm_final_g):
    for _ in range(DEPTH):
        x = x + token_mixer(rmsnorm_2(x, norm_mix_g), w_in, conv_w, conv_b, b_forget,
                            w_conv_out, w_att_out, w_out)
        x = x + hier_moe(rmsnorm_2(x, norm_ffn_g), w_router_group, w_router_expert,
                         w_e_gate, w_e_up, w_e_down)
    return rmsnorm_2(x, norm_final_g)


def setup_inputs(seed=0):
    out = dict(first_inputs(seed))
    for name, value in second_inputs(seed + 1).items():
        if name != "x":
            out[name + "_2"] = value
    return out


def reference(
    x, norm_mix_w, w_in, gla_w_gate2, gla_b_gate, gla_norm_w, ssd_conv_w, ssd_conv_b,
    ssd_dt_bias, ssd_a_log, ssd_d, ssd_norm_w, w_out, norm_ffn_w, peer_w_query, peer_sub_keys,
    peer_u, peer_v, norm_final_w, norm_mix_g_2, w_in_2, conv_w_2, conv_b_2, b_forget_2,
    w_conv_out_2, w_att_out_2, w_out_2, norm_ffn_g_2, w_router_group_2, w_router_expert_2,
    w_e_gate_2, w_e_up_2, w_e_down_2, norm_final_g_2,
):
    x = first_block(
        x, norm_mix_w, w_in, gla_w_gate2, gla_b_gate, gla_norm_w, ssd_conv_w, ssd_conv_b,
        ssd_dt_bias, ssd_a_log, ssd_d, ssd_norm_w, w_out, norm_ffn_w, peer_w_query,
        peer_sub_keys, peer_u, peer_v, norm_final_w,
    )
    return second_block(
        x, norm_mix_g_2, w_in_2, conv_w_2, conv_b_2, b_forget_2, w_conv_out_2, w_att_out_2,
        w_out_2, norm_ffn_g_2, w_router_group_2, w_router_expert_2, w_e_gate_2, w_e_up_2,
        w_e_down_2, norm_final_g_2,
    )


_drawn_inputs = setup_inputs


def setup_inputs(seed=0):
    import zlib

    import numpy as np

    out = dict(_drawn_inputs(seed))
    spreads = {}
    factors = {'conv_b_2': 4.179, 'norm_final_g_2': 2.887}
    for name, (base, spread) in spreads.items():
        noise = np.random.default_rng([zlib.crc32(name.encode()), seed]).standard_normal(out[name].shape)
        drawn = base * np.exp(spread * noise) if base else spread * noise
        out[name] = jnp.asarray(drawn.astype(out[name].dtype))
    for name, factor in factors.items():
        out[name] = (out[name] * factor).astype(out[name].dtype)
    return out
```

```python
from contextlib import ExitStack

import numpy as np

import concourse.bass as bass
from concourse import mybir

F32 = mybir.dt.float32
BF16 = mybir.dt.bfloat16
I32 = mybir.dt.int32
U32 = mybir.dt.uint32
ALU = mybir.AluOpType
ACT = mybir.ActivationFunctionType
AX_X = mybir.AxisListType.X

P = 128
T = 512
TB = T // P
D = 1024
KT = D // P
EPS = 1e-6
NEG = -1.0e30
LOWEST = -3.4e38

GH, GDK, GDV, GC = 4, 64, 128, 64
GQK, GW, GRANK = GH * GDK, GH * GDV, 16
NGC = T // GC
GATE_NORM = 16.0
SH, SP_, SG, SN, SCONV = 8, 64, 2, 64, 4
SJ = SH // SG
SW = SH * SP_
XBC = SW + 2 * SG * SN
PH, PK, PTOP = 8, 128, 16
PE_N = PK * PK
SLOTS = PH * PTOP
CONVW = 3
AH, ADH = 16, 64
EG, EPG, DE = 4, 8, 512
NE = EG * EPG
CAP = 64
PASSES = T // CAP

CW = 2048
RING = 4
AHEAD = 3
N_P1F = (2 * GQK + XBC) // P // 2
N_P1T = 3 * 2
N_WOUT = 4
N_QUERY = 2 * PH // 2
N_KEYS = 1
N_U = PK // 2
N_V = PK // 2
N_CONV = 3 * KT // 2
N_CO = KT
N_V2 = 4
N_QK = KT
N_AO = KT
N_WO2 = 4
N_MOE = NE * 6
C_P1F = 0
C_P1T = C_P1F + N_P1F
C_WOUT = C_P1T + N_P1T
C_QUERY = C_WOUT + N_WOUT
C_KEYS = C_QUERY + N_QUERY
C_U = C_KEYS + N_KEYS
C_V = C_U + N_U
C_CONV = C_V + N_V
C_CO = C_CONV + N_CONV
C_V2 = C_CO + N_CO
C_QK = C_V2 + N_V2
C_AO = C_QK + N_QK
C_WO2 = C_AO + N_AO
C_MOE = C_WO2 + N_WO2
N_CHUNKS = C_MOE + N_MOE

_cols = {}
_at = 0
for _name, _n in (("norm_mix", KT), ("gla_b", 2), ("gla_norm", 1), ("conv_w", 6 * SCONV), ("conv_b", 6),
                  ("dt_b", 1), ("a_log", 1), ("d_skip", SH), ("ssd_norm", 4), ("norm_ffn", KT),
                  ("norm_mix2", KT), ("conv_w2", KT * CONVW), ("conv_b2", KT), ("b_forget", 1)):
    _cols[_name] = _at
    _at += _n
N_COLS = _at
SM_IN, SM_F, SM_R = 40, 16, EG + NE
O_IN, O_F, O_R = 0, KT * SM_IN, KT * (SM_IN + SM_F)
N_SPLIT = KT * (SM_IN + SM_F + SM_R)
O_G2 = N_SPLIT
N_SMALL = N_SPLIT + GQK
DT0 = 32


def MOE_GATE(e):
    return C_MOE + (0 if e == 0 else 4 + (e - 1) * 6)


def MOE_UP(e):
    return C_MOE + (2 if e == 0 else 4 + (e - 1) * 6 + 4)


def MOE_DOWN(e):
    return C_MOE + 4 + e * 6 + (2 if e < NE - 1 else 0)



def build_program(nc, w_all, x_in, cols_in, small_in, row_final, row_ffn2, row_final2, out):
    ctx = ExitStack()
    with ctx:
        def sb(name, shape, dt=F32):
            return ctx.enter_context(nc.sbuf_tensor(name, shape, dt))

        def sem(name):
            return ctx.enter_context(nc.semaphore(name))

        w_st = sb("w_st", [P, RING, CW])
        w_hi = sb("w_hi", [P, RING, CW], BF16)
        w_lo = sb("w_lo", [P, RING, CW], BF16)
        res = sb("res", [P, TB, D])
        a_hi = sb("a_hi", [P, KT, T], BF16)
        a_lo = sb("a_lo", [P, KT, T], BF16)
        xn = sb("xn", [P, TB, D])
        cols = sb("cols", [P, N_COLS])
        small = sb("small", [P, N_SMALL])
        small_hi = sb("small_hi", [P, N_SPLIT], BF16)
        small_lo = sb("small_lo", [P, N_SPLIT], BF16)
        ident = sb("ident", [P, P])
        ident_b = sb("ident_b", [P, P], BF16)
        tri_le = sb("tri_le", [P, P])
        tri_gt = sb("tri_gt", [P, P])
        tri_neg = sb("tri_neg", [P, P])
        neg_gt = sb("neg_gt", [P, P])
        ones = sb("ones", [P, P])
        mask64 = sb("mask64", [P, GC])
        eps = sb("eps", [P, 1])
        iota_i = sb("iota_i", [P, P], I32)
        ss = sb("ss", [P, 16])
        sd = sb("sd", [P, 16])
        rstd = sb("rstd", [P, 16])
        ARENA = 19712
        arena = sb("arena", [P, ARENA])
        ps = ctx.enter_context(nc.psum_tensor("ps", [P, 8, 512], F32))

        def col(name, i=0, n=1):
            return cols[:, _cols[name] + i:_cols[name] + i + n]

        def view(at, *shape, dt=F32):
            n = int(np.prod(shape)) * (2 if dt == BF16 else 4) // 4
            assert at + n <= ARENA, (at, n)
            v = arena[:, at:at + n]
            if dt != F32:
                v = v.bitcast(dt)
            names = "abcd"[:len(shape)]
            return v.rearrange(f"p ({' '.join(names)}) -> p {' '.join(names)}",
                               **{c: s for c, s in zip(names, shape)}) if len(shape) > 1 else v

        o = 0
        qk = view(o, 4, T); xdte = view(o, TB, T); o += 4 * T
        xbc = view(o, 6, T + 4); o += 6 * (T + 4)
        xt = view(o - 6 * (T + 4), TB, T); bt = view(o - 6 * (T + 4) + 4 * T, TB, P)
        sm = view(o, T); o += T
        vT = view(o, TB, GW); o += TB * GW
        lg = view(o, 2, T); att_s = view(o, 2, 8, GC); l_s = view(o, 2, 4 * P); o += 2 * T
        g_cum = view(o, 2, T); e_neg = view(o + 2 * T, 2, T); s_gla = view(o, 2, NGC, GDV); xdt = view(o, TB, T); o += 4 * T
        e_pos = view(o, 2, T); y_t = view(o, 2, T); o += 2 * T
        k_end = view(o, 2, T); o_s = view(o, 2, T); w_s = view(o, 2, 4 * P); o += 2 * T
        k_endT = view(o, 2, TB, P); s_ssd = view(o, TB, SJ * SP_); o += 2 * T
        xc = view(o, 6, T); o += 6 * T
        reset = view(o, T); o += T
        dtm = view(o, 4, T); o += 4 * T
        dta = view(o, TB, 2, SH); o += TB * 2 * SH
        ecum = view(o, 3, TB, SH); o += 3 * TB * SH
        ea = view(o, 2); o += 2

        q_hi = view(0, 2 * PH, T, dt=BF16)
        q_lo = view(4 * 1024, 2 * PH, T, dt=BF16)
        keys_hi = view(8 * 1024, 2 * PH, PK, dt=BF16)
        keys_lo = view(9 * 1024, 2 * PH, PK, dt=BF16)
        o = 10 * 1024
        s_sb = view(o, 2, PK); o += 2 * PK
        s_cut = view(o, 2, PK); o += 2 * PK
        top_v = view(o, 2, PTOP); o += 2 * PTOP
        top_i = view(o, 2, PTOP, dt=U32); o += 2 * PTOP
        cand = view(o, PTOP, PTOP); o += PTOP * PTOP
        cand_cut = view(o, PTOP, PTOP); o += PTOP * PTOP
        best_v = view(o, PTOP); o += PTOP
        best_p = view(o, PTOP, dt=U32); o += PTOP
        best_k = view(o, 2, PTOP, dt=U32); o += 2 * PTOP
        pick = view(o, 2, PTOP, PTOP); o += 2 * PTOP * PTOP
        assert o <= 16 * 1024
        g_st = view(0, 2, PK, T // 8)
        slot_T = view(16 * 1024, 4, T)
        oh_b = view(18 * 1024, 2, 8, PK, dt=BF16)
        c_slot = view(19 * 1024, 4, T // 8)
        xn_flat = xn[:, :, :].rearrange("p t d -> p (t d)")
        u_st = xn_flat[:, 0:2048].rearrange("p (r j t) -> p r j t", r=2, j=2)
        key1 = xn_flat[:, 2048:2560]
        key2 = xn_flat[:, 2560:3072]
        score = xn_flat[:, 3072:3584]
        gate_t = xn_flat[:, 3584:4096]
        oh_a = xn_flat[:, 2048:4096].bitcast(BF16).rearrange("p (r t s k) -> p r t s k", r=2, t=8, s=2)
        ga_in = view(0, 2, 2, T)
        g_in = view(2048, 2, 8, 2, T // 8)
        h_f = view(4096, 2, 2, T)
        h_hi = view(6144, 2, 2, T, dt=BF16)
        h_lo = view(7168, 2, 2, T, dt=BF16)
        g_b16 = view(18 * 1024, T, dt=BF16)
        first_st = sb("first_st", [P, 2, 3, 4])
        soft = sb("soft", [P, 2, TB * PH])
        iota_f = sb("iota_f", [P, P])
        iota_b = sb("iota_b", [P, P], BF16)
        zero_b = sb("zero_b", [P, T], BF16)
        act_dram = nc.dram_tensor("act_dram", (N_U, P, 2 * T), F32, kind="Internal").ap()
        gate_dram = nc.dram_tensor("gate_dram", (8, P, PK, T // 8), F32, kind="Internal").ap()

        c_hi = view(0, KT, T, dt=BF16)
        c_lo = view(2048, KT, T, dt=BF16)
        m1 = view(4096, KT, T)
        m_split = view(4096, KT, 2, T, dt=BF16)
        v_s = view(8192, TB, D)
        cu_s, cc_s, cb_s = (view(8192 + 1024 * n, 2, T) for n in range(3))
        z_s = view(8192 + 3072, T + 4)
        q_z = view(12288, 2, 2, T)
        k_s = view(14336, 2, T)
        f_x, f_e = view(14336, T), view(14336 + T, T)
        p_s = view(15360, 2, T)
        acc_s = view(15360, T)
        mix_s = view(15360, 2, T)
        pT_s = view(16384, 2, TB, P)
        cv_s = view(16384, 2, T)
        prod_s = view(16384, 2, T)
        n_cum = view(17408, T)
        sg_s = view(17920, 2, T)
        f_one = view(18944, T)
        pk = view(0, TB, 2, D, dt=BF16)
        x_g = view(4096, 2, 2, D, dt=BF16)
        xeT = view(6144, 2, 2, KT, CAP, dt=BF16)
        o = 6144 + 2 * KT * CAP
        sil = view(o, DE); o += DE
        hid_f = view(o, DE); o += DE
        hid_b = view(o, 2, DE, dt=BF16); o += DE
        hidT = view(o, 2, DE // P, CAP, dt=BF16); o += DE // P * CAP
        y_st = view(o, 2, D); o += 2 * D
        y_g = view(0, TB, 2, D)
        o = max(o, TB * 2 * D)
        lr = view(o, TB, SM_R); o += TB * SM_R
        lr_g = view(o, TB, 8); o += TB * 8
        g_max = view(o, TB, 8); o += TB * 8
        g_idx = view(o, TB, 8, dt=U32); o += TB * 8
        g_num = view(o, TB); o += TB
        g_one = view(o, TB, EG); o += TB * EG
        le_all = view(o, TB, EG, EPG); o += TB * NE
        le_sel = view(o, TB, EPG); o += TB * EPG
        e_max = view(o, TB, 8); o += TB * 8
        e_idx = view(o, TB, 8, dt=U32); o += TB * 8
        e_num = view(o, 2, TB); o += 2 * TB
        e_of = view(o, 2, TB); o += 2 * TB
        r_exp = view(o, TB, EG + 1); o += TB * (EG + 1)
        g_sum = view(o, TB); o += TB
        w_den = view(o, TB); o += TB
        w_tok = view(o, 2, TB); o += 2 * TB
        e_one = view(o, 2, TB, NE); o += 2 * TB * NE
        e_any = view(o, TB, NE); o += TB * NE
        e_rank = view(o, 2, TB, NE); o += 2 * TB * NE
        rank_f = view(o, 2, TB); o += 2 * TB
        rank_u = view(o, 2, TB, dt=U32); o += 2 * TB
        blk_u = view(o, 2, 2, TB, dt=U32); o += 4 * TB
        blk_f = view(o, 2, 2, TB); o += 4 * TB
        e_blk = view(o, 2, TB); o += 2 * TB
        to_tok = view(o, 2, TB, dt=I32); o += 2 * TB
        to_y = view(o, 2, TB, dt=I32); o += 2 * TB
        n_rows = view(o, 1); o += 1
        n_rows_i = view(o, 1, dt=I32); o += 1
        tok_i = view(o, TB, dt=I32); o += TB
        row_i = view(o, PASSES * NE, dt=I32); o += PASSES * NE
        idx = view(o, 2, dt=I32); o += 2
        x_dram = nc.dram_tensor("x_dram", (T, 2 * D), BF16, kind="Internal").ap()
        tok_dram = nc.dram_tensor("tok_dram", (CAP * PASSES * NE, 1), I32, kind="Internal").ap()
        y_dram = nc.dram_tensor("y_dram", (PASSES * NE, CAP, D), F32, kind="Internal").ap()
        row = sb("row", [P, D])
        n_max = sb("n_max", [P, 2])
        r_sum = sb("r_sum", [P, 4])
        r_inv = sb("r_inv", [P, 2])

        w_ld = [sem(f"w_ld{s}") for s in range(RING)]
        w_hi_done = sem("w_hi_done")
        w_lo_done = sem("w_lo_done")
        ft_done, ft_out = sem("ft_done"), sem("ft_out")
        tok_half, tok_done, tok_out = sem("tok_half"), sem("tok_done"), sem("tok_out")
        x_ld, cols_ld, small_ld = sem("x_ld"), sem("cols_ld"), sem("small_ld")
        small_hi_done, small_done = sem("small_hi_done"), sem("small_done")
        const_step, const_done = sem("const_step"), sem("const_done")
        res_done = sem("res_done")
        sd_done, xn_done = sem("sd_done"), sem("xn_done")
        tp_done, tp_hi, tp_lo = sem("tp_done"), sem("tp_hi"), sem("tp_lo")
        sm_done, sm_out = sem("sm_done"), sem("sm_out")
        conv_done, silu_done = sem("conv_done"), sem("silu_done")
        gate_mm, gate_x, gate_ln, gate_cum, gate_exp = (sem(n) for n in ("gate_mm", "gate_x", "gate_ln", "gate_cum", "gate_exp"))
        dt_x, dt_ln, dt_done = sem("dt_x"), sem("dt_ln"), sem("dt_done")
        gla_qk, gla_kt, gla_ktc, gla_att, gla_attc, gla_st, gla_S = (
            sem(n) for n in ("gla_qk", "gla_kt", "gla_ktc", "gla_att", "gla_attc", "gla_st", "gla_S"))
        gla_o, gla_oc, gla_od, gla_sd, gla_y = (sem(n) for n in ("gla_o", "gla_oc", "gla_od", "gla_sd", "gla_y"))
        xt_tp, xt_c, dta_tp, dta_c, cum_mm, cum_exp = (sem(n) for n in ("xt_tp", "xt_c", "dta_tp", "dta_c", "cum_mm", "cum_exp"))
        xd_done, ssd_mm, ssd_L, ssd_W, ssd_st, ssd_S, ssd_y, ssd_yc, ssd_yd, ssd_sd = (
            sem(n) for n in ("xd_done", "ssd_mm", "ssd_L", "ssd_W", "ssd_st", "ssd_S", "ssd_y", "ssd_yc", "ssd_yd", "ssd_sd"))
        out_st = sem("out_st")
        row_ld, row_used = sem("row_ld"), sem("row_used")
        f_mm, f_xs, f_ln, f_cum = (sem(n) for n in ("f_mm", "f_xs", "f_ln", "f_cum"))
        cv_used, cv_mul, cv_hi, cv_lo = (sem(n) for n in ("cv_used", "cv_mul", "cv_hi", "cv_lo"))
        sg_done, m1_done = sem("sg_done"), sem("m1_done")
        qz_zero, qk_out = sem("qz_zero"), sem("qk_out")
        at_s, at_max, at_p, at_t, at_tc, at_o, at_out = (sem(n) for n in ("at_s", "at_max", "at_p", "at_t", "at_tc", "at_o", "at_out"))
        mix_done, mix_hi, mix_lo = sem("mix_done"), sem("mix_hi"), sem("mix_lo")
        q_hi_done = sem("q_hi_done")
        u_done, u_out = sem("u_done"), sem("u_out")
        u_stored = [sem(f"u_stored{r}") for r in range(2)]
        s_done, s_out = sem("s_done"), sem("s_out")
        soft_x, soft_e, soft_done, slot_tp, slot_done = (sem(n) for n in ("soft_x", "soft_e", "soft_done", "slot_tp", "slot_done"))
        oh_done, g_done, g_out = sem("oh_done"), sem("g_done"), sem("g_out")
        g_stored = [sem(f"g_stored{b}") for b in range(2)]
        ga_ld = [sem(f"ga_ld{r}") for r in range(2)]
        g_ld = [sem(f"g_ld{r}") for r in range(2)]
        h_mul, h_hi_done, h_lo_done, v_done = (sem(n) for n in ("h_mul", "h_hi_done", "h_lo_done", "v_done"))
        peer_done = sem("peer_done")
        pk_hi, pk_lo, x_st = sem("pk_hi"), sem("pk_lo"), sem("x_st")
        rt_mm, rt_x, rt_e, rt_pick, rt_rank, rt_dest = (sem(n) for n in ("rt_mm", "rt_x", "rt_e", "rt_pick", "rt_rank", "rt_dest"))
        tok_zero, tok_st, row_i_ld = sem("tok_zero"), sem("tok_st"), sem("row_i_ld")
        xe_ld = [sem(f"xe_ld{p}") for p in range(2)]
        xe_tp, xe_hi, xe_lo = sem("xe_tp"), sem("xe_hi"), sem("xe_lo")
        moe_mm = sem("moe_mm")
        sil_done, hid_mul, hid_hi, hid_lo, hid_tp, hid_c = (sem(n) for n in ("sil_done", "hid_mul", "hid_hi", "hid_lo", "hid_tp", "hid_c"))
        y_out = sem("y_out")
        y_stored = [sem(f"y_stored{p}") for p in range(2)]
        yg_ld = [sem(f"yg_ld{tb}") for tb in range(TB)]
        end_sd, end_done = sem("end_sd"), sem("end_done")

        F_P1 = 0
        F_QUERY = F_P1 + 2 * N_P1F
        F_CONV = F_QUERY + 2 * N_QUERY
        F_CO = F_CONV + 2 * N_CONV
        F_QK = F_CO + 2 * N_CO
        F_AO = F_QK + 2 * N_QK
        G_P1, G_WOUT, G_V2, G_WO2 = 0, 3, 5, 7
        UNITS = [(h, qb) for h in range(AH) for qb in range(TB)]

        def used(n):
            for c, k, f in ((C_P1F, N_P1F, F_P1), (C_QUERY, N_QUERY, F_QUERY), (C_CONV, N_CONV, F_CONV), (C_CO, N_CO, F_CO),
                            (C_QK, N_QK, F_QK), (C_AO, N_AO, F_AO)):
                if c <= n < c + k:
                    return ft_done, f + 2 * (n - c) + 2
            if n == C_KEYS:
                return used(n - RING)
            if C_U <= n < C_U + N_U:
                return u_done, 2 + 2 * (n - C_U) + 2
            if C_V <= n < C_V + N_V:
                return v_done, 2 + n - C_V + 1
            for c, k, g in ((C_P1T, N_P1T, G_P1), (C_WOUT, N_WOUT, G_WOUT), (C_V2, N_V2, G_V2), (C_WO2, N_WO2, G_WO2)):
                if c <= n < c + k:
                    at = g + (n - c) // 2 + 1
                    return (tok_done, TB * at) if (n - c) % 2 else (tok_half, at)

        PASS = N_MOE
        moe = lambda r, i, c: r * NE + 2 * i + c
        pairs_of = lambda r, i, c: r * (NE // 2) + i + c // 2

        def wait(eng, semaphore, count):
            if not isinstance(count, int) or count > 0:
                eng.wait_ge(semaphore, count)

        def every_expert(first, step, last):
            def one_pass(eng, r):
                first(r)
                with eng.Fori(0, (NE - 2) // 2) as i:
                    for c in (1, 2):
                        step(r, i, c)
                last(r)
            return one_pass

        def more_passes(eng, one_pass, gather=None):
            eng.wait_ge(rt_dest, 1)
            with eng.If(eng.value_load(n_rows_i[0:1, 0:1], min_val=0, max_val=T) > CAP):
                with eng.Fori(1, PASSES) as r:
                    one_pass(eng, r)
                if gather:
                    gather(PASSES)
            if gather:
                with eng.Else():
                    gather(1)

        block = ctx.enter_context(nc.Block())

        @block.sync
        def _(sp):
            for tb in range(TB):
                sp.dma_start(res[:, tb, :], x_in[tb * P:(tb + 1) * P, :]).then_inc(x_ld, 16)
            sp.dma_start(cols[:, :], cols_in).then_inc(cols_ld, 16)
            for n in range(RING):
                sp.dma_start(w_st[:, n, :], w_all[n]).then_inc(w_ld[n], 16)
            sp.dma_start(small[:, :], small_in).then_inc(small_ld, 16)
            with sp.Fori(1, C_MOE // RING) as i:
                for s in range(RING):
                    sp.wait_ge(w_lo_done, i * RING + (s + 1 - RING))
                    sp.dma_start(w_st[:, s, :], w_all[i * RING + s]).then_inc(w_ld[s], 16)

            def one_pass(eng, r):
                with sp.Fori(0, PASS // RING) as i:
                    for s in range(RING):
                        sp.wait_ge(w_lo_done, C_MOE + r * PASS + i * RING + (s + 1 - RING))
                        sp.dma_start(w_st[:, s, :], w_all[C_MOE + i * RING + s]).then_inc(w_ld[s], 16)

            one_pass(sp, 0)
            more_passes(sp, one_pass)
            for tb in range(TB):
                sp.wait_ge(end_done, tb + 1)
                sp.dma_start(out[tb * P:(tb + 1) * P, :], xn[:, tb, :]).then_inc(out_st, 16)
            sp.wait_ge(out_st, 16 * TB)

        @block.gpsimd
        def _(pool):
            pool.memset(ident[:, :], 0.0)
            pool.memset(ones[:, :], 1.0)
            pool.memset(eps[:, :], EPS)
            pool.memset(reset[:, :], 1.0)
            pool.memset(neg_gt[:, :], 0.0).then_inc(const_step, 1)
            pool.wait_ge(const_step, 1)
            pool.affine_select(out=ident[:, :], in_=ident[:, :], compare_op=ALU.not_equal, fill=1.0, base=0,
                               pattern=[[-1, P]], channel_multiplier=1)
            pool.affine_select(out=tri_le[:, :], in_=ones[:, :], compare_op=ALU.is_ge, fill=0.0, base=0,
                               pattern=[[1, P]], channel_multiplier=-1)
            pool.affine_select(out=tri_gt[:, :], in_=ones[:, :], compare_op=ALU.is_gt, fill=0.0, base=0,
                               pattern=[[-1, P]], channel_multiplier=1)
            pool.affine_select(out=neg_gt[:, :], in_=neg_gt[:, :], compare_op=ALU.is_ge, fill=NEG, base=0,
                               pattern=[[1, P]], channel_multiplier=-1)
            pool.memset(reset[:, :].rearrange("p (c i) -> p c i", i=GC)[:, :, 0:1], 0.0)
            pool.memset(xbc[:, :, 0:4], 0.0).then_inc(const_step, 1)
            pool.wait_ge(const_step, 2)
            pool.tensor_scalar(tri_neg[:, :], tri_le[:, :], -1.0, None, ALU.mult)
            pool.iota(iota_i[:, :], [[1, P]], base=0, channel_multiplier=0)
            pool.memset(zero_b[:, :], 0.0)
            pool.tensor_copy(ident_b[:, :], ident[:, :]).then_inc(const_step, 1)
            pool.wait_ge(const_step, 3)
            pool.tensor_copy(iota_f[:, :], iota_i[:, :])
            pool.tensor_copy(iota_b[:, :], iota_i[:, :]).then_inc(const_done, 1)
            pool.wait_ge(const_done, 1)
            pool.dma_start(tok_dram.rearrange("(p n) o -> p (n o)", p=P), zero_b[:, 0:2 * CAP * PASSES * NE // P].bitcast(I32)).then_inc(tok_zero, 16)

            for r in range(2):
                pool.dma_start(first_st[:, r, 0, :], cols_in[:, 0:4]).then_inc(u_stored[r], 16)
                pool.dma_start(first_st[:, r, 1, :], cols_in[:, 0:4]).then_inc(g_stored[r], 16)
                pool.dma_start(first_st[:, r, 2, :], cols_in[:, 0:4]).then_inc(y_stored[r], 16)

            def store_activations(i, c):
                pool.wait_ge(u_out, 16 * i + 2 * c + 4)
                pool.dma_start(act_dram[i * 8 + c], u_st[:, c % 2, :, :].rearrange("p j t -> p (j t)")).then_inc(u_stored[c % 2], 16)

            with pool.Fori(0, 4) as i:
                for c in range(8):
                    store_activations(i, c)
            with pool.Fori(4, 8) as i:
                for c in range(8):
                    store_activations(i, c)
                    if c % 4 == 3:
                        b = c // 4
                        pool.wait_ge(g_out, 4 + 2 * (16 * (i - 4) + 8 * b + 8))
                        pool.dma_start(gate_dram[(i - 4) * 2 + b], g_st[:, b, :, :]).then_inc(g_stored[b], 16)
            for r in range(2):
                pool.wait_ge(u_stored[r], 16 * (N_U // 2 + 1))
                pool.wait_ge(g_stored[r], 16 * 5)
            with pool.Fori(0, N_V // 4) as i:
                for c in range(4):
                    pool.wait_ge(h_mul, i * 4 + c + 1)
                    pool.dma_start(ga_in[:, c % 2, :, :].rearrange("p j t -> p (j t)"), act_dram[i * 4 + c]).then_inc(ga_ld[c % 2], 16)
                    pairs = gate_dram.rearrange("g p (n j) t -> n p g (j t)", j=2)
                    pool.dma_start(g_in[:, c % 2, :, :, :].rearrange("p g j t -> p g (j t)"), pairs[i * 4 + c]).then_inc(g_ld[c % 2], 16)

            pool.dma_start(row[:, :], row_final.to_broadcast([P, D])).then_inc(row_ld, 16)
            pool.wait_ge(row_used, 1)
            pool.dma_start(row[:, :], row_ffn2.to_broadcast([P, D])).then_inc(row_ld, 16)
            for tb in range(TB):
                pool.wait_ge(pk_lo, tb + 1)
                pool.dma_start(x_dram[tb * P:(tb + 1) * P, :], pk[:, tb, :, :].rearrange("p a d -> p (a d)")).then_inc(x_st, 16)
            pool.iota(tok_i, [[P, TB]], base=0, channel_multiplier=1)
            pool.drain()
            pool.wait_ge(rt_dest, 1)
            pool.wait_ge(tok_zero, 16)
            for s in range(2):
                for tb in range(TB):
                    pool.indirect_dma_start(tok_dram, bass.IndirectOffsetOnAxis(ap=to_tok[:, s, tb:tb + 1], axis=0),
                                            tok_i[:, tb:tb + 1], None).then_inc(tok_st, 16)
            pool.wait_ge(row_used, 2)
            pool.dma_start(row[:, :], row_final2.to_broadcast([P, D])).then_inc(row_ld, 16)
            pool.wait_ge(tok_st, 16 * 2 * TB)
            pool.dma_start(row_i[0:CAP, :], tok_dram.rearrange("(p n) o -> p (n o)", p=CAP)).then_inc(row_i_ld, 16)
            pool.wait_ge(row_i_ld, 16)
            pool.wait_ge(x_st, 16 * TB)

            def gather(r, i, c):
                pool.wait_ge(xe_tp, 2 * moe(r, i, c) + 2)
                pool.tensor_copy(idx[0:CAP, c % 2:c % 2 + 1], row_i[0:CAP, bass.ds(moe(r, i, c), 1)])
                pool.drain()
                pool.indirect_dma_start(x_g[0:CAP, c % 2, :, :].rearrange("p a d -> p (a d)"), None, x_dram,
                                        bass.IndirectOffsetOnAxis(ap=idx[0:CAP, c % 2:c % 2 + 1], axis=0)).then_inc(xe_ld[c % 2], 16)

            def store(r, i, c):
                pool.wait_ge(y_out, moe(r, i, c) + 2)
                pool.dma_start(y_dram[moe(r, i, c)], y_st[0:CAP, c % 2, :]).then_inc(y_stored[c % 2], 16)

            def first(r):
                gather(r, 0, 0)
                gather(r, 0, 1)

            def step(r, i, c):
                gather(r, i, c + 1)
                store(r, i, c - 1)

            def last(r):
                store(r, 0, NE - 2)
                store(r, 0, NE - 1)
                for p in range(2):
                    pool.wait_ge(y_stored[p], 16 * (pairs_of(r, 0, NE) + 1))

            one_pass = every_expert(first, step, last)
            one_pass(pool, 0)

            def gather_outputs(passes):
                for tb in range(TB):
                    for s in range(2):
                        pool.indirect_dma_start(y_g[:, tb, s, :], None, y_dram[0:passes * NE].rearrange("q r d -> (q r) d"),
                                                bass.IndirectOffsetOnAxis(ap=to_y[:, s, tb:tb + 1], axis=0)).then_inc(yg_ld[tb], 16)

            more_passes(pool, one_pass, gather_outputs)

        @block.tensor
        def _(pe):
            def chunk(n):
                pe.wait_ge(w_lo_done, n + 1)

            def mm3(dst, l_hi, l_lo, r_hi, r_lo, start, stop):
                pe.matmul(dst, l_hi, r_hi, start=start, stop=False)
                pe.matmul(dst, l_hi, r_lo, start=False, stop=False)
                return pe.matmul(dst, l_lo, r_hi, start=False, stop=stop)

            def feature_tile(f, n, half, r_hi, r_lo, bank=None):
                chunk(n)
                if bank is None and f >= 4:
                    pe.wait_ge(ft_out, f - 3)
                dst = ps[:, 4 + f % 4 if bank is None else bank, :]
                for kt in range(KT):
                    w = slice(half * D + kt * P, half * D + (kt + 1) * P)
                    last = mm3(dst, w_hi[:, n % RING, w], w_lo[:, n % RING, w], r_hi[:, kt, :], r_lo[:, kt, :],
                               kt == 0, kt == KT - 1)
                last.then_inc(ft_done, 1)

            def token_tiles(n, bank, l_hi, l_lo):
                for part in range(2):
                    chunk(n + part)
                    for tb in range(TB):
                        rows = slice(tb * P, (tb + 1) * P)
                        for k in range(4):
                            kt = part * 4 + k
                            w = slice(k * 512, (k + 1) * 512)
                            last = mm3(ps[:, bank + tb, :], l_hi[:, kt, rows], l_lo[:, kt, rows],
                                       w_hi[:, (n + part) % RING, w], w_lo[:, (n + part) % RING, w],
                                       kt == 0, kt == KT - 1)
                        if part == 1:
                            last.then_inc(tok_done, 1)
                        elif tb == TB - 1:
                            last.then_inc(tok_half, 1)

            def transpose_rows(use):
                for kt in range(KT):
                    g = KT * use + kt
                    if g >= 2:
                        pe.wait_ge(tp_lo, g - 1)
                    for tb in range(TB):
                        if kt == 0:
                            pe.wait_ge(xn_done, TB * use + tb + 1)
                        last = pe.transpose(ps[:, g % 2, tb * P:(tb + 1) * P], xn[:, tb, kt * P:(kt + 1) * P], ident[:, :])
                    last.then_inc(tp_done, 1)

            pe.wait_ge(const_done, 1)
            transpose_rows(0)
            pe.wait_ge(tp_lo, KT)
            for m in range(2 * N_P1F):
                feature_tile(F_P1 + m, C_P1F + m // 2, m % 2, a_hi, a_lo)
            pe.wait_ge(small_done, 1)
            for kt in range(KT):
                w = slice(O_IN + kt * SM_IN, O_IN + (kt + 1) * SM_IN)
                last = mm3(ps[0:SM_IN, 2, :], small_hi[:, w], small_lo[:, w], a_hi[:, kt, :], a_lo[:, kt, :], kt == 0, kt == KT - 1)
            last.then_inc(sm_done, 1)
            pe.wait_ge(sm_out, 1)
            token_tiles(C_P1T, 0, a_hi, a_lo)
            pe.wait_ge(ft_out, F_P1 + 2 * N_P1F)
            token_tiles(C_P1T + 2, 4, a_hi, a_lo)
            pe.wait_ge(tok_out, TB)
            token_tiles(C_P1T + 4, 0, a_hi, a_lo)

            pe.wait_ge(tok_out, 2 * TB)
            for j in range(2):
                pe.matmul(ps[:, 4 + j, :], small[0:GRANK, O_G2 + j * P:O_G2 + (j + 1) * P], sm[0:GRANK, :],
                          start=True, stop=True).then_inc(gate_mm, 1)
            pe.wait_ge(dt_done, 1)
            for tb in range(TB):
                for s in range(2):
                    last = pe.transpose(ps[:, 6, (tb * 2 + s) * SH:(tb * 2 + s + 1) * SH],
                                        dtm[DT0:DT0 + SH, 2 + s, tb * P:(tb + 1) * P], ident[DT0:DT0 + SH, DT0:DT0 + SH])
            last.then_inc(dta_tp, 1)
            pe.wait_ge(dta_c, 1)
            for s, tri in enumerate((tri_le, tri_gt, ones)):
                last = pe.matmul(ps[:, 6, s * TB * SH:(s + 1) * TB * SH].rearrange("p (t h) -> p t h", t=TB), tri[:, :], dta[:, :, 1, :], start=True, stop=True)
            last.then_inc(cum_mm, 1)
            pe.wait_ge(cum_exp, 1)
            for j in range(2):
                pe.wait_ge(gla_qk, j + 1)
                for tb in range(TB):
                    last = pe.transpose(ps[:, 6 + j, tb * P:(tb + 1) * P], k_end[:, j, tb * P:(tb + 1) * P], ident[:, :])
                last.then_inc(gla_kt, 1)
            for hh in range(2):
                for c in range(NGC):
                    for j in range(2):
                        rows, t0 = slice(hh * GDK, (hh + 1) * GDK), c * GC
                        last = pe.matmul(ps[(c % 2) * GC:(c % 2 + 1) * GC, 4 + hh, ((c // 2) * 2 + j) * GC:((c // 2) * 2 + j + 1) * GC],
                                         qk[rows, 2 + j, t0:t0 + GC], qk[rows, j, t0:t0 + GC], start=True, stop=True)
                last.then_inc(gla_att, 1)
            pe.wait_ge(gla_ktc, 2)
            pe.wait_ge(tok_out, 3 * TB)
            for j in range(2):
                for c in range(NGC):
                    rows = slice((c % 2) * GC, (c % 2 + 1) * GC)
                    for hh in range(2):
                        h = 2 * j + hh
                        last = pe.matmul(ps[hh * GDK:(hh + 1) * GDK, j * 2 + c % 2, (c // 2) * GDV:(c // 2 + 1) * GDV],
                                         k_endT[rows, j, c // 2, hh * GDK:(hh + 1) * GDK],
                                         vT[rows, c // 2, h * GDV:(h + 1) * GDV], start=True, stop=True)
                last.then_inc(gla_st, 1)
            pe.wait_ge(gla_attc, 2)
            pe.wait_ge(gla_S, 1)
            for tb in range(TB):
                b = (tb % 2) * 3
                if tb >= 2:
                    pe.wait_ge(gla_od, tb - 1)
                for par in range(2):
                    rows, c = slice(par * GC, (par + 1) * GC), 2 * tb + par
                    for h in range(GH):
                        j, hh = h // 2, h % 2
                        pe.matmul(ps[rows, b, h * GDV:(h + 1) * GDV], att_s[rows, hh, 2 * tb + j, :],
                                  vT[rows, tb, h * GDV:(h + 1) * GDV], start=True, stop=True)
                        dk = slice(hh * GDK, (hh + 1) * GDK)
                        last = pe.matmul(ps[rows, b + 1 + hh, j * GDV:(j + 1) * GDV], qk[dk, j, c * GC:(c + 1) * GC],
                                         s_gla[dk, j, c, :], start=True, stop=True)
                last.then_inc(gla_o, 1)

            pe.wait_ge(silu_done, 6)
            for tb in range(TB + 1):
                if tb >= 2:
                    pe.wait_ge(xt_c, tb - 1)
                for m in range(4):
                    src = xc[:, m, tb * P:(tb + 1) * P] if tb < TB else xc[:, 4, m * P:(m + 1) * P]
                    last = pe.transpose(ps[:, 6 + tb % 2, m * P:(m + 1) * P], src, ident[:, :])
                last.then_inc(xt_tp, 1)
            pe.wait_ge(xt_c, TB + 1)
            pe.wait_ge(gla_od, TB)
            for tb in range(TB):
                t0 = slice(tb * P, (tb + 1) * P)
                if tb >= 1:
                    pe.wait_ge(ssd_W, 2 * tb)
                for g in range(SG):
                    for jj in range(SJ):
                        a_col = dta[:, tb, 1, g * SJ + jj:g * SJ + jj + 1].to_broadcast([P, P])
                        dst = ps[:, g, jj * P:(jj + 1) * P]
                        pe.matmul(dst, a_col, tri_le[:, :], start=True, stop=False)
                        pe.matmul(dst, tri_neg[:, :], a_col, start=False, stop=False)
                        pe.matmul(dst, ident[:, :], neg_gt[:, :], start=False, stop=True)
                    n = slice(g * SN, (g + 1) * SN)
                    pe.matmul(ps[:, 2 + g, 0:P], xc[n, 4, t0], xc[n, 5, t0], start=True, stop=True).then_inc(ssd_mm, 1)
                pe.wait_ge(xd_done, tb + 1)
                if tb >= 1:
                    pe.wait_ge(ssd_S, tb)
                for g in range(SG):
                    last = pe.matmul(ps[g * SN:(g + 1) * SN, 6, 0:SJ * SP_], bt[:, tb, g * SN:(g + 1) * SN],
                                     xdte[:, tb, g * SJ * SP_:(g + 1) * SJ * SP_], start=True, stop=True)
                last.then_inc(ssd_st, 1)
                if tb == 0:
                    pe.wait_ge(ssd_S, 1)
                else:
                    pe.wait_ge(ssd_yd, tb)
                for g in range(SG):
                    n = slice(g * SN, (g + 1) * SN)
                    pe.matmul(ps[:, 7 - 3 * g, 0:SJ * SP_], xc[n, 5, t0], s_ssd[n, tb, :], start=True, stop=True)
                pe.wait_ge(ssd_W, 2 * tb + 2)
                for h in range(SH):
                    last = pe.matmul(ps[:, 5, h * SP_:(h + 1) * SP_], w_s[:, h // SJ, (h % SJ) * P:(h % SJ + 1) * P],
                                     xdt[:, tb, h * SP_:(h + 1) * SP_], start=True, stop=True)
                last.then_inc(ssd_y, 1)

            pe.wait_ge(ssd_yd, TB)
            transpose_rows(1)
            pe.wait_ge(tp_lo, 2 * KT)
            token_tiles(C_WOUT, 4, a_hi, a_lo)
            token_tiles(C_WOUT + 2, 0, a_hi, a_lo)

            transpose_rows(2)
            pe.wait_ge(tp_lo, 3 * KT)
            for m in range(2 * N_QUERY):
                feature_tile(F_QUERY + m, C_QUERY + m // 2, m % 2, a_hi, a_lo)

            def expert_tile(i, c, t):
                n = C_U + 8 * i + c
                if t == 0:
                    chunk(n)
                pe.wait_ge(u_out, 16 * i + 2 * c + t + 1)
                for kt in range(KT):
                    w = slice(t * D + kt * P, t * D + (kt + 1) * P)
                    last = mm3(ps[:, t, :], w_hi[:, c % RING, w], w_lo[:, c % RING, w], a_hi[:, kt, :], a_lo[:, kt, :],
                               kt == 0, kt == KT - 1)
                last.then_inc(u_done, 1)

            pe.wait_ge(ft_out, F_QUERY + 2 * N_QUERY)
            pe.drain().then_inc(u_done, 2)
            with pe.Fori(0, 4) as i:
                for c in range(8):
                    for t in range(2):
                        expert_tile(i, c, t)
                    pe.wait_ge(s_out, 8 * i + c + 1)
                    for half in range(2):
                        q = 2 * c + half
                        rows = bass.ts(i, P)
                        last = mm3(ps[:, 2 + c % 2, half * PK:(half + 1) * PK], q_hi[:, q, rows], q_lo[:, q, rows],
                                   keys_hi[:, q, :], keys_lo[:, q, :], True, True)
                    last.then_inc(s_done, 1)
            pe.wait_ge(soft_done, 1)
            for a, src in enumerate((key1, key2, score)):
                for tb in range(TB):
                    last = pe.transpose(ps[:, 4 + a, tb * P:(tb + 1) * P], src[:, tb * P:(tb + 1) * P], ident[:, :])
            last.then_inc(slot_tp, 1)
            pe.wait_ge(slot_done, 1)
            pe.drain().then_inc(g_done, 4)
            with pe.Fori(4, 8) as i:
                for c in range(8):
                    for t in range(2):
                        expert_tile(i, c, t)
                        at = 2 * c + t
                        pe.wait_ge(oh_done, 16 * (i - 4) + at + 1)
                        pe.wait_ge(g_out, 2 * (16 * (i - 4) + at) + 2)
                        for r in range(8):
                            dst = ps[:, 2 + 2 * (at % 2) + r // 4, (r % 4) * PK:(r % 4 + 1) * PK]
                            pe.matmul(dst, oh_b[:, at % 2, r, :], oh_a[:, at % 2, r, 0, :], start=True, stop=False)
                            last = pe.matmul(dst, oh_b[:, at % 2, r, :], oh_a[:, at % 2, r, 1, :], start=False, stop=True)
                            if r % 4 == 3:
                                last.then_inc(g_done, 1)
            pe.wait_ge(u_out, 2 + 2 * N_U)
            pe.wait_ge(g_out, 4 + 2 * 64)
            for b in range(8):
                pe.matmul(ps[:, b, :], zero_b[:, 0:P], zero_b[:, :], start=True, stop=False)
            pe.drain().then_inc(v_done, 2)
            with pe.Fori(0, N_V // 4) as i:
                for c in range(4):
                    chunk(C_V + 4 * i + c)
                    pe.wait_ge(h_lo_done, 4 * i + c + 1)
                    for j in range(2):
                        for tb in range(TB):
                            rows = slice(tb * P, (tb + 1) * P)
                            for part in range(2):
                                w = slice(j * D + part * 512, j * D + (part + 1) * 512)
                                last = mm3(ps[:, 2 * tb + part, :], h_hi[:, c % 2, j, rows], h_lo[:, c % 2, j, rows],
                                           w_hi[:, c, w], w_lo[:, c, w], False, False)
                    last.then_inc(v_done, 1)
            for b in range(8):
                pe.matmul(ps[:, b, :], zero_b[:, 0:P], zero_b[:, :], start=False, stop=True).then_inc(peer_done, 1)

            transpose_rows(3)
            pe.wait_ge(tp_lo, 4 * KT)
            for kt in range(KT):
                w = slice(O_F + kt * SM_F, O_F + (kt + 1) * SM_F)
                last = mm3(ps[0:SM_F, 2, :], small_hi[:, w], small_lo[:, w], a_hi[:, kt, :], a_lo[:, kt, :], kt == 0, kt == KT - 1)
            last.then_inc(f_mm, 1)
            for m in range(2 * N_CONV):
                feature_tile(F_CONV + m, C_CONV + m // 2, m % 2, a_hi, a_lo)
            pe.wait_ge(cv_lo, KT)
            pe.wait_ge(ft_out, F_CONV + 2 * N_CONV)
            for j in range(KT):
                if j >= 2:
                    pe.wait_ge(m1_done, j - 1)
                feature_tile(F_CO + 2 * j, C_CO + j, 0, a_hi, a_lo, bank=4 + 2 * (j % 2))
                feature_tile(F_CO + 2 * j + 1, C_CO + j, 1, c_hi, c_lo, bank=5 + 2 * (j % 2))
            token_tiles(C_V2, 0, a_hi, a_lo)
            pe.wait_ge(m1_done, KT)
            token_tiles(C_V2 + 2, 4, a_hi, a_lo)

            def project_heads(j):
                if j:
                    pe.wait_ge(qk_out, 2 * j)
                feature_tile(F_QK + 2 * j, C_QK + j, 0, a_hi, a_lo, bank=6)
                feature_tile(F_QK + 2 * j + 1, C_QK + j, 1, a_hi, a_lo, bank=7)

            pe.wait_ge(tok_out, TB * (G_V2 - 2 + 2))
            pe.wait_ge(f_cum, 1)
            project_heads(0)
            for u in range(len(UNITS) + 2):
                if u < len(UNITS):
                    h, qb = UNITS[u]
                    j, hh, n = h // 2, h % 2, (qb + 1) * P
                    if (hh, qb) == (0, 0):
                        pe.wait_ge(qk_out, 2 * j + 2)
                    if u >= 2:
                        pe.wait_ge(at_p, u - 1)
                    dst = ps[:, u % 2, 0:n]
                    pe.matmul(dst, q_z[:, j % 2, hh, qb * P:n], k_s[:, j % 2, 0:n], start=True, stop=False)
                    pe.matmul(dst, ident[:, h:h + 1].to_broadcast([P, P]), n_cum[:, 0:n], start=False, stop=False)
                    pe.matmul(ps[:, u % 2, qb * P:n], neg_gt[:, :], ident[:, :], start=False, stop=True).then_inc(at_s, 1)
                    if (hh, qb) == (0, 2) and j + 1 < AH // 2:
                        project_heads(j + 1)
                if 1 <= u <= len(UNITS):
                    v = u - 1
                    pe.wait_ge(at_p, v + 1)
                    if v >= 2:
                        pe.wait_ge(at_tc, v - 1)
                    for kb in range(UNITS[v][1] + 1):
                        last = pe.transpose(ps[:, 2 + v % 2, kb * P:(kb + 1) * P], p_s[:, v % 2, kb * P:(kb + 1) * P], ident[:, :])
                    last.then_inc(at_t, 1)
                if u >= 2:
                    v = u - 2
                    h, qb = UNITS[v]
                    pe.wait_ge(at_tc, v + 1)
                    if v >= 2:
                        pe.wait_ge(at_out, v - 1)
                    for kb in range(qb + 1):
                        last = pe.matmul(ps[:, 4 + v % 2, 0:ADH], pT_s[:, v % 2, kb, :], v_s[:, kb, h * ADH:(h + 1) * ADH],
                                         start=kb == 0, stop=kb == qb)
                    last.then_inc(at_o, 1)
            transpose_rows(4)
            pe.wait_ge(tp_lo, 5 * KT)
            pe.wait_ge(at_out, len(UNITS))
            for j in range(KT):
                if j >= 2:
                    pe.wait_ge(mix_done, j - 1)
                feature_tile(F_AO + 2 * j, C_AO + j, 0, a_hi, a_lo, bank=4 + 2 * (j % 2))
                feature_tile(F_AO + 2 * j + 1, C_AO + j, 1, c_hi, c_lo, bank=5 + 2 * (j % 2))
            pe.wait_ge(mix_lo, KT)
            token_tiles(C_WO2, 0, m_split[:, :, 0, :], m_split[:, :, 1, :])
            token_tiles(C_WO2 + 2, 4, m_split[:, :, 0, :], m_split[:, :, 1, :])

            transpose_rows(5)
            pe.wait_ge(tp_lo, 6 * KT)
            for tb in range(TB):
                for kt in range(KT):
                    rows, w = slice(tb * P, (tb + 1) * P), slice(O_R + kt * SM_R, O_R + (kt + 1) * SM_R)
                    last = mm3(ps[:, 2, tb * SM_R:(tb + 1) * SM_R], a_hi[:, kt, rows], a_lo[:, kt, rows], small_hi[:, w], small_lo[:, w],
                               kt == 0, kt == KT - 1)
            last.then_inc(rt_mm, 1)
            pe.wait_ge(rt_pick, 1)
            for tb in range(TB + 1):
                before = min(tb, TB)
                for b in range(before):
                    last = pe.matmul(ps[:, 3, tb * NE:(tb + 1) * NE], ones[:, :], e_any[:, b, :], start=b == 0, stop=tb == TB and b == TB - 1)
                if tb < TB:
                    pe.matmul(ps[:, 3, tb * NE:(tb + 1) * NE], tri_le[:, :], e_any[:, tb, :], start=tb == 0, stop=True)
            last.then_inc(rt_rank, 1)
            pe.drain().then_inc(xe_tp, 4)
            pe.drain().then_inc(moe_mm, RING)

            def expert_rows(r, i, c):
                pe.wait_ge(xe_ld[c % 2], 16 * (pairs_of(r, i, c) + 1))
                wait(pe, xe_hi, moe(r, i, c))
                wait(pe, xe_lo, moe(r, i, c))
                for a in range(2):
                    for kt in range(KT):
                        last = pe.matmul(ps[:, 6 + a, kt * CAP:(kt + 1) * CAP], x_g[0:CAP, c % 2, a, kt * P:(kt + 1) * P],
                                         ident_b[0:CAP, 0:CAP], start=True, stop=True)
                    last.then_inc(xe_tp, 1)

            def expert_in(r, i, c, k, bank):
                for part in range(2):
                    chunk(C_MOE + r * PASS + 12 * i + (k + part))
                    for j in range(4):
                        kt, w = part * 4 + j, slice(j * DE, (j + 1) * DE)
                        last = mm3(ps[0:CAP, bank, :], xeT[:, c % 2, 0, kt, :], xeT[:, c % 2, 1, kt, :],
                                   w_hi[:, (k + part) % RING, w], w_lo[:, (k + part) % RING, w], kt == 0, kt == KT - 1)
                    last.then_inc(moe_mm, 1)

            def expert_gate(r, i, c):
                wait(pe, sil_done, moe(r, i, c))
                pe.wait_ge(xe_hi, moe(r, i, c) + 1)
                pe.wait_ge(xe_lo, moe(r, i, c) + 1)
                expert_in(r, i, c, 6 * c - 2 if c else 0, 0)

            def expert_up(r, i, c):
                wait(pe, hid_mul, moe(r, i, c))
                expert_in(r, i, c, 6 * c + 2, 1)

            def expert_hidden(r, i, c):
                pe.wait_ge(hid_lo, moe(r, i, c) + 1)
                for a in range(2):
                    for f in range(DE // P):
                        n = a * (DE // P) + f
                        last = pe.matmul(ps[:, 4, n * CAP:(n + 1) * CAP], hid_b[0:CAP, a, f * P:(f + 1) * P], ident_b[0:CAP, 0:CAP],
                                         start=True, stop=True)
                last.then_inc(hid_tp, 1)

            def expert_down(r, i, c, k):
                pe.wait_ge(hid_c, moe(r, i, c) + 1)
                pe.wait_ge(y_out, moe(r, i, c) + 1)
                for part in range(2):
                    chunk(C_MOE + r * PASS + 12 * i + (k + part))
                    for half in range(2):
                        for j in range(2):
                            f, w = part * 2 + j, slice(j * D + half * 512, j * D + (half + 1) * 512)
                            last = mm3(ps[0:CAP, 2 + half, :], hidT[:, 0, f, :], hidT[:, 1, f, :],
                                       w_hi[:, (k + part) % RING, w], w_lo[:, (k + part) % RING, w], f == 0, f == DE // P - 1)
                    last.then_inc(moe_mm, 1)

            def first(r):
                expert_rows(r, 0, 0)
                expert_rows(r, 0, 1)
                expert_gate(r, 0, 0)
                expert_up(r, 0, 0)

            def step(r, i, c, more=True):
                expert_gate(r, i, c)
                expert_hidden(r, i, c - 1)
                if more:
                    expert_rows(r, i, c + 1)
                expert_down(r, i, c - 1, 6 * c)
                expert_up(r, i, c)

            def last(r):
                step(r, 0, NE - 1, more=False)
                expert_hidden(r, 0, NE - 1)
                expert_down(r, 0, NE - 1, 6 * NE - 2)

            one_pass = every_expert(first, step, last)
            one_pass(pe, 0)
            more_passes(pe, one_pass)

        @block.scalar
        def _(act):
            split = [0]

            def hi(n, dst=None):
                act.wait_ge(w_ld[n % RING], 16 * (n // RING + 1))
                if n >= RING:
                    act.wait_ge(*used(n - RING))
                dst = w_hi[:, n % RING, :] if n != C_KEYS else keys_hi.rearrange("p q k -> p (q k)")
                act.activation(dst, w_st[:, n % RING, :], ACT.Copy).then_inc(w_hi_done, 1)

            def ahead(n):
                while split[0] <= min(n + AHEAD, C_MOE - 1):
                    hi(split[0])
                    split[0] += 1

            def norm(use):
                for tb in range(TB):
                    if use:
                        act.wait_ge(res_done, TB * (use - 1) + tb + 1)
                    else:
                        act.wait_ge(x_ld, 16 * TB)
                    act.activation(xn[:, tb, :], res[:, tb, :], ACT.Square, accum_out=ss[:, tb:tb + 1])
                act.drain()
                act.activation(sd[:, 0:TB], ss[:, 0:TB], ACT.Sqrt, scale=1.0 / D, bias=eps[:, :]).then_inc(sd_done, 1)

            def transposed(use, weight, dst=a_hi):
                for kt in range(KT):
                    act.wait_ge(tp_done, KT * use + kt + 1)
                    act.activation(dst[:, kt, :], ps[:, kt % 2, :], ACT.Copy, scale=weight(kt)).then_inc(tp_hi, 1)

            act.wait_ge(const_done, 1)
            norm(0)
            ahead(-1)
            act.wait_ge(cols_ld, 16)
            transposed(0, lambda kt: col("norm_mix", kt))
            act.wait_ge(small_ld, 16)
            act.activation(small_hi[:, :], small[:, 0:N_SPLIT], ACT.Copy).then_inc(small_hi_done, 1)
            for m in range(2 * N_P1F):
                ahead(C_P1F + m // 2)
                act.wait_ge(ft_done, F_P1 + m + 1)
                bank = ps[:, 4 + (F_P1 + m) % 4, :]
                if m < 4:
                    act.activation(qk[:, m, :], bank, ACT.Copy, scale=GDK ** -0.5 if m < 2 else 1.0).then_inc(ft_out, 1)
                else:
                    act.activation(xbc[:, m - 4, 4:], bank, ACT.Copy).then_inc(ft_out, 1)
            act.wait_ge(sm_done, 1)
            act.activation(sm[0:SM_IN, :], ps[0:SM_IN, 2, :], ACT.Copy).then_inc(sm_out, 1)
            for g in range(3):
                ahead(C_P1T + 2 * g)
                act.wait_ge(tok_half, G_P1 + g + 1)
                ahead(C_P1T + 2 * g + 1)
                for tb in range(TB):
                    act.wait_ge(tok_done, TB * (G_P1 + g) + tb + 1)
                    bank = ps[:, (g % 2) * 4 + tb, :]
                    if g == 0:
                        act.activation(vT[:, tb, :], bank, ACT.Copy).then_inc(tok_out, 1)
                    else:
                        act.activation(xn[:, tb, (g - 1) * 512:g * 512], bank, ACT.Silu).then_inc(tok_out, 1)
            for m in range(6):
                act.wait_ge(conv_done, m + 1)
                act.activation(xc[:, m, :], xc[:, m, :], ACT.Silu).then_inc(silu_done, 1)

            d = slice(DT0, DT0 + SH)
            act.activation(ea[d, 0:1], col("a_log")[d, :], ACT.Exp)
            act.wait_ge(dt_x, 1)
            act.activation(dtm[d, 1, :], dtm[d, 0, :], ACT.Abs)
            act.drain()
            act.activation(dtm[d, 1, :], dtm[d, 1, :], ACT.Exp, scale=-1.0)
            act.drain()
            act.activation(dtm[d, 1, :], dtm[d, 1, :], ACT.Ln, bias=ones[d, 0:1]).then_inc(dt_ln, 1)
            for j in range(2):
                act.wait_ge(gate_x, j + 1)
                act.activation(e_pos[:, j, :], g_cum[:, j, :], ACT.Abs)
                act.drain()
                act.activation(e_pos[:, j, :], e_pos[:, j, :], ACT.Exp, scale=-1.0)
                act.drain()
                act.activation(e_pos[:, j, :], e_pos[:, j, :], ACT.Ln, bias=ones[:, 0:1]).then_inc(gate_ln, 1)
            act.wait_ge(dta_tp, 1)
            act.activation(dta.rearrange("p t s h -> p (t s h)"), ps[:, 6, 0:TB * 2 * SH], ACT.Copy).then_inc(dta_c, 1)
            act.wait_ge(cum_mm, 1)
            act.activation(ecum.rearrange("p s t h -> p (s t h)"), ps[:, 6, 0:3 * TB * SH], ACT.Exp).then_inc(cum_exp, 1)
            for j in range(2):
                act.wait_ge(gate_cum, j + 1)
                act.activation(e_pos[:, j, :], g_cum[:, j, :], ACT.Exp)
                act.activation(e_neg[:, j, :], g_cum[:, j, :], ACT.Exp, scale=-1.0)
                act.activation(lg[:, j, :], lg[:, j, :], ACT.Exp).then_inc(gate_exp, 1)
            for j in range(2):
                act.wait_ge(gla_kt, j + 1)
                act.activation(k_endT[:, j, :, :].rearrange("p t d -> p (t d)"), ps[:, 6 + j, :], ACT.Copy).then_inc(gla_ktc, 1)
            for tb in range(TB):
                act.wait_ge(gla_o, tb + 1)
                if tb >= 2:
                    act.wait_ge(gla_y, tb - 1)
                act.activation(o_s[:, tb % 2, :], ps[:, (tb % 2) * 3, :], ACT.Copy).then_inc(gla_oc, 1)
                act.wait_ge(gla_od, tb + 1)
                for h in range(GH):
                    act.activation(y_t[:, 0, h * GDV:(h + 1) * GDV], o_s[:, tb % 2, h * GDV:(h + 1) * GDV], ACT.Square, accum_out=ss[:, h:h + 1])
                act.drain()
                act.activation(sd[:, 0:GH], ss[:, 0:GH], ACT.Sqrt, scale=1.0 / GDV, bias=eps[:, :]).then_inc(gla_sd, 1)
            for tb in range(TB + 1):
                act.wait_ge(xt_tp, tb + 1)
                dst = xt[:, tb, :] if tb < TB else bt.rearrange("p t n -> p (t n)")
                act.activation(dst, ps[:, 6 + tb % 2, :], ACT.Copy).then_inc(xt_c, 1)
            for tb in range(TB):
                for g in range(SG):
                    act.wait_ge(ssd_mm, 2 * tb + g + 1)
                    if tb >= 1:
                        act.wait_ge(ssd_W, 2 * (tb - 1) + g + 1)
                    act.activation(l_s[:, g, :], ps[:, g, :], ACT.Exp).then_inc(ssd_L, 1)
                act.wait_ge(ssd_yc, tb + 1)
                for g in range(SG):
                    act.activation(y_t[:, 0, g * SJ * SP_:(g + 1) * SJ * SP_], y_t[:, 1, g * SJ * SP_:(g + 1) * SJ * SP_], ACT.Square, accum_out=ss[:, g:g + 1])
                act.drain()
                act.activation(sd[:, 0:SG], ss[:, 0:SG], ACT.Sqrt, scale=1.0 / (SJ * SP_), bias=eps[:, :]).then_inc(ssd_sd, 1)
            transposed(1, lambda kt: col("gla_norm") if kt < 4 else col("ssd_norm", kt - 4))
            for g in range(2):
                ahead(C_WOUT + 2 * g)
                act.wait_ge(tok_half, G_WOUT + g + 1)
                ahead(C_WOUT + 2 * g + 1)

            norm(1)
            transposed(2, lambda kt: col("norm_ffn", kt))
            for m in range(2 * N_QUERY):
                ahead(C_QUERY + m // 2)
                act.wait_ge(ft_done, F_QUERY + m + 1)
                act.activation(q_hi[:, m, :], ps[:, 4 + (F_QUERY + m) % 4, :], ACT.Copy).then_inc(q_hi_done, 1)
            ahead(C_KEYS)
            act.drain().then_inc(u_out, 2)

            def hi_in_loop(c, arrived, done, count):
                s = (c + AHEAD) % RING
                act.wait_ge(w_ld[s], arrived)
                act.wait_ge(done, count)
                act.activation(w_hi[:, s, :], w_st[:, s, :], ACT.Copy).then_inc(w_hi_done, 1)

            def gelu_tile(i, c, t):
                if t == 0:
                    act.wait_ge(u_stored[c % 2], 16 * (4 * i + c // 2 + 1))
                act.wait_ge(u_done, 16 * i + 2 * c + t + 3)
                act.activation(u_st[:, c % 2, t, :], ps[:, t, :], ACT.Gelu).then_inc(u_out, 1)

            with act.Fori(0, 4) as i:
                for c in range(8):
                    hi_in_loop(c, 16 * (C_U // RING + 2 * i + (c + AHEAD) // RING + 1), u_done, 16 * i + 2 * c + 2)
                    for t in range(2):
                        gelu_tile(i, c, t)
            act.wait_ge(soft_x, 1)
            act.activation(gate_t, gate_t, ACT.Exp).then_inc(soft_e, 1)
            act.drain().then_inc(g_out, 4)
            with act.Fori(4, 8) as i:
                for c in range(8):
                    hi_in_loop(c, 16 * (C_U // RING + 2 * i + (c + AHEAD) // RING + 1), u_done, 16 * i + 2 * c + 2)
                    for t in range(2):
                        gelu_tile(i, c, t)
                        at = 2 * c + t
                        b, first = at // 8, (at % 8) * 8
                        if at % 8 == 0:
                            act.wait_ge(g_stored[b], 16 * (i - 3))
                        for bank in range(2):
                            act.wait_ge(g_done, 2 * (16 * (i - 4) + at) + bank + 5)
                            tok = slice(first + bank * 4, first + bank * 4 + 4)
                            act.activation(g_st[:, b, :, tok].rearrange("p k t -> p t k"),
                                           ps[:, 2 + 2 * (at % 2) + bank, :].rearrange("p (t k) -> p t k", t=4), ACT.Copy).then_inc(g_out, 1)
            with act.Fori(0, N_V // 4) as i:
                for c in range(4):
                    act.wait_ge(h_mul, 4 * i + c + 3)
                    act.wait_ge(v_done, 4 * i + c + 1)
                    act.activation(h_hi[:, c % 2, :, :], h_f[:, c % 2, :, :], ACT.Copy).then_inc(h_hi_done, 1)
                    hi_in_loop(c, 16 * (C_V // RING + i + (c + AHEAD) // RING + 1), v_done, 4 * i + c + 2)
            split[0] = C_CONV + AHEAD

            norm(2)
            norm(3)
            transposed(3, lambda kt: col("norm_mix2", kt))
            act.wait_ge(f_xs, 1)
            act.activation(f_e[0:AH, :], f_x[0:AH, :], ACT.Abs)
            act.drain()
            act.activation(f_e[0:AH, :], f_e[0:AH, :], ACT.Exp, scale=-1.0)
            act.drain()
            act.activation(f_e[0:AH, :], f_e[0:AH, :], ACT.Ln, bias=ones[0:AH, 0:1]).then_inc(f_ln, 1)

            def conv_hi(j):
                act.wait_ge(cv_mul, j + 1)
                act.activation(c_hi[:, j, :], cv_s[:, j % 2, :], ACT.Copy).then_inc(cv_hi, 1)

            for j in range(KT):
                for a, dst in enumerate((cu_s, cc_s, cb_s)):
                    m = 3 * j + a
                    ahead(C_CONV + m // 2)
                    act.wait_ge(ft_done, F_CONV + m + 1)
                    if j >= 2:
                        act.wait_ge(cv_mul, j - 1)
                    act.activation(dst[:, j % 2, :], ps[:, 4 + (F_CONV + m) % 4, :], ACT.Copy).then_inc(ft_out, 1)
                if j:
                    conv_hi(j - 1)
            conv_hi(KT - 1)
            for j in range(KT):
                ahead(C_CO + j)
                act.wait_ge(ft_done, F_CO + 2 * j + 1)
                if j >= 2:
                    act.wait_ge(m1_done, j - 1)
                act.activation(sg_s[:, j % 2, :], ps[:, 4 + 2 * (j % 2), :], ACT.Sigmoid).then_inc(sg_done, 1)
            for g in range(2):
                ahead(C_V2 + 2 * g)
                act.wait_ge(tok_half, G_V2 + g + 1)
                ahead(C_V2 + 2 * g + 1)
                for tb in range(TB):
                    act.wait_ge(tok_done, TB * (G_V2 + g) + tb + 1)
                    act.activation(v_s[:, tb, g * 512:(g + 1) * 512], ps[:, 4 * g + tb, :], ACT.Copy).then_inc(tok_out, 1)

            def copy_heads(j):
                ahead(C_QK + j)
                act.wait_ge(ft_done, F_QK + 2 * j + 1)
                if j >= 2:
                    act.wait_ge(at_s, 8 * (j - 1))
                for hh in range(2):
                    rows = slice(hh * ADH, (hh + 1) * ADH)
                    last = act.activation(q_z[rows, j % 2, hh, :], ps[rows, 6, :], ACT.Copy, scale=ADH ** -0.5)
                last.then_inc(qk_out, 1)
                act.wait_ge(ft_done, F_QK + 2 * j + 2)
                act.activation(k_s[:, j % 2, :], ps[:, 7, :], ACT.Copy).then_inc(qk_out, 1)

            act.wait_ge(qz_zero, 1)
            act.wait_ge(f_cum, 1)
            copy_heads(0)
            for u, (h, qb) in enumerate(UNITS):
                n = (qb + 1) * P
                act.wait_ge(at_max, u + 1)
                if u >= 2:
                    act.wait_ge(at_t, u - 1)
                if u >= 4:
                    act.wait_ge(at_out, u - 3)
                act.activation(p_s[:, u % 2, 0:n], ps[:, u % 2, 0:n], ACT.Exp, bias=n_max[:, u % 2:u % 2 + 1],
                               accum_out=r_sum[:, u % 4:u % 4 + 1]).then_inc(at_p, 1)
                if h % 2 == 0 and qb == 3 and h // 2 + 1 < AH // 2:
                    copy_heads(h // 2 + 1)
            transposed(4, lambda kt: 1.0, c_hi)

            def mix_high(j):
                act.wait_ge(mix_done, j + 1)
                act.activation(m_split[:, j, 0, :], mix_s[:, j % 2, :], ACT.Copy).then_inc(mix_hi, 1)

            for j in range(KT):
                ahead(C_AO + j)
                act.wait_ge(ft_done, F_AO + 2 * j + 1)
                if j >= 2:
                    act.wait_ge(mix_done, j - 1)
                act.activation(sg_s[:, j % 2, :], ps[:, 4 + 2 * (j % 2), :], ACT.Sigmoid).then_inc(sg_done, 1)
                if j:
                    mix_high(j - 1)
            mix_high(KT - 1)
            for g in range(2):
                ahead(C_WO2 + 2 * g)
                act.wait_ge(tok_half, G_WO2 + g + 1)
                ahead(C_WO2 + 2 * g + 1)

            norm(4)
            transposed(5, lambda kt: 1.0)
            for tb in range(TB):
                act.activation(pk[:, tb, 0, :], xn[:, tb, :], ACT.Copy).then_inc(pk_hi, 1)
            act.wait_ge(rt_x, 1)
            act.activation(r_exp, r_exp, ACT.Exp).then_inc(rt_e, 1)
            act.drain().then_inc(y_out, 1)

            def hi_of(r, i, k):
                s = k % RING
                act.wait_ge(w_ld[s], 16 * ((C_MOE + r * PASS) // RING + 3 * i + k // RING + 1) if isinstance(r, int) else
                            16 * (r * (PASS // RING) + 3 * i + (C_MOE // RING + k // RING + 1)))
                act.wait_ge(moe_mm, r * PASS + 12 * i + k + 1)
                act.activation(w_hi[:, s, :], w_st[:, s, :], ACT.Copy).then_inc(w_hi_done, 1)

            def rows_hi(r, i, c):
                act.wait_ge(xe_tp, 2 * moe(r, i, c) + 5)
                act.activation(xeT[:, c % 2, 0, :, :].rearrange("p k t -> p (k t)"), ps[:, 6, 0:KT * CAP], ACT.Copy).then_inc(xe_hi, 1)

            def silu(r, i, c, k):
                wait(act, hid_mul, moe(r, i, c))
                act.wait_ge(moe_mm, r * PASS + 12 * i + (k + 2 + RING))
                act.activation(sil[0:CAP, :], ps[0:CAP, 0, :], ACT.Silu).then_inc(sil_done, 1)

            def hidden_hi(r, i, c):
                act.wait_ge(hid_mul, moe(r, i, c) + 1)
                act.activation(hid_b[0:CAP, 0, :], hid_f[0:CAP, :], ACT.Copy).then_inc(hid_hi, 1)

            def hidden_copy(r, i, c):
                act.wait_ge(hid_tp, moe(r, i, c) + 1)
                act.activation(hidT.rearrange("p a f t -> p (a f t)"), ps[:, 4, 0:2 * DE // P * CAP], ACT.Copy).then_inc(hid_c, 1)

            def outputs(r, i, c, k):
                act.wait_ge(moe_mm, r * PASS + 12 * i + (k + 2 + RING))
                act.wait_ge(y_stored[c % 2], 16 * (pairs_of(r, i, c) + 1))
                act.activation(y_st[0:CAP, c % 2, :].rearrange("p (b n) -> p b n", b=2), ps[0:CAP, 2:4, :], ACT.Copy).then_inc(y_out, 1)

            def first(r):
                for k in range(AHEAD):
                    hi_of(r, 0, k)
                rows_hi(r, 0, 0)
                rows_hi(r, 0, 1)
                hi_of(r, 0, 3)
                hi_of(r, 0, 4)
                silu(r, 0, 0, 0)
                hi_of(r, 0, 5)
                hi_of(r, 0, 6)

            def step(r, i, c, more=True):
                k = 6 * c - 2
                hidden_hi(r, i, c - 1)
                hi_of(r, i, k + 3)
                hi_of(r, i, k + 4)
                hidden_copy(r, i, c - 1)
                silu(r, i, c, k)
                if more:
                    rows_hi(r, i, c + 1)
                hi_of(r, i, k + 5)
                hi_of(r, i, k + 6)
                outputs(r, i, c - 1, k + 2)
                hi_of(r, i, k + 7)
                if more:
                    hi_of(r, i, k + 8)

            def last(r):
                step(r, 0, NE - 1, more=False)
                hidden_hi(r, 0, NE - 1)
                hidden_copy(r, 0, NE - 1)
                outputs(r, 0, NE - 1, PASS - 2)

            one_pass = every_expert(first, step, last)
            one_pass(act, 0)
            more_passes(act, one_pass)
            for tb in range(TB):
                act.wait_ge(res_done, TB * 4 + tb + 1)
                act.activation(xn[:, tb, :], res[:, tb, :], ACT.Square, accum_out=ss[:, tb:tb + 1])
                act.drain()
                act.activation(sd[:, tb:tb + 1], ss[:, tb:tb + 1], ACT.Sqrt, scale=1.0 / D, bias=eps[:, :]).then_inc(end_sd, 1)

        @block.vector
        def _(dve):
            split = [0]

            def lo(n):
                dve.wait_ge(w_hi_done, n + 1)
                lo_n, hi_n = w_lo[:, n % RING, :], w_hi[:, n % RING, :]
                if n == C_KEYS:
                    lo_n, hi_n = (v.rearrange("p q k -> p (q k)") for v in (keys_lo, keys_hi))
                dve.tensor_tensor(lo_n, w_st[:, n % RING, :], hi_n, ALU.subtract).then_inc(w_lo_done, 1)

            def ahead(n):
                while split[0] <= min(n + AHEAD, C_MOE - 1):
                    lo(split[0])
                    split[0] += 1

            def normalise(use):
                dve.wait_ge(sd_done, use + 1)
                dve.reciprocal(rstd[:, 0:TB], sd[:, 0:TB])
                dve.drain()
                for tb in range(TB):
                    dve.tensor_scalar(xn[:, tb, :], res[:, tb, :], rstd[:, tb:tb + 1], None, ALU.mult).then_inc(xn_done, 1)

            def transposed(use, weight, dst_hi=a_hi, dst_lo=a_lo):
                for kt in range(KT):
                    dve.wait_ge(tp_hi, KT * use + kt + 1)
                    dve.scalar_tensor_tensor(dst_lo[:, kt, :], ps[:, kt % 2, :], weight(kt), dst_hi[:, kt, :],
                                             ALU.mult, ALU.subtract).then_inc(tp_lo, 1)

            dve.wait_ge(const_done, 1)
            for half in range(2):
                rows = slice(half * GC, (half + 1) * GC)
                dve.tensor_copy(mask64[rows, :], tri_le[rows, rows])
            normalise(0)
            dve.wait_ge(cols_ld, 16)
            transposed(0, lambda kt: col("norm_mix", kt))
            ahead(-1)
            dve.wait_ge(small_hi_done, 1)
            dve.tensor_tensor(small_lo[:, :], small[:, 0:N_SPLIT], small_hi[:, :], ALU.subtract).then_inc(small_done, 1)
            for m in range(2 * N_P1F):
                ahead(C_P1F + m // 2)
                if m >= 4:
                    f = m - 4
                    dve.wait_ge(ft_out, F_P1 + m + 1)
                    dve.tensor_scalar(xc[:, f, :], xbc[:, f, 1:1 + T], col("conv_w", f * SCONV), col("conv_b", f), ALU.mult, ALU.add)
                    for k in range(1, SCONV):
                        dve.drain()
                        last = dve.scalar_tensor_tensor(xc[:, f, :], xbc[:, f, 1 + k:1 + k + T], col("conv_w", f * SCONV + k),
                                                        xc[:, f, :], ALU.mult, ALU.add)
                    last.then_inc(conv_done, 1)
            for g in range(3):
                ahead(C_P1T + 2 * g)
                ahead(C_P1T + 2 * g + 1)

            d = slice(DT0, DT0 + SH)
            dve.wait_ge(sm_out, 1)
            dve.tensor_scalar(dtm[d, 0, :], sm[d, :], col("dt_b")[d, :], None, ALU.add).then_inc(dt_x, 1)
            for j in range(2):
                dve.wait_ge(gate_mm, j + 1)
                dve.tensor_scalar(g_cum[:, j, :], ps[:, 4 + j, :], col("gla_b", j), None, ALU.add).then_inc(gate_x, 1)
            dve.drain()
            for j in range(2):
                dve.tensor_scalar(lg[:, j, :], g_cum[:, j, :], 0.0, 1.0 / GATE_NORM, ALU.min, ALU.mult)
            dve.wait_ge(dt_ln, 1)
            dve.scalar_tensor_tensor(dtm[d, 2, :], dtm[d, 0, :], 0.0, dtm[d, 1, :], ALU.max, ALU.add)
            dve.drain()
            dve.tensor_scalar(dtm[d, 3, :], dtm[d, 2, :], ea[d, 0:1], -1.0, ALU.mult, ALU.mult).then_inc(dt_done, 1)
            for j in range(2):
                dve.wait_ge(gate_ln, j + 1)
                dve.scalar_tensor_tensor(lg[:, j, :], e_pos[:, j, :], -1.0 / GATE_NORM, lg[:, j, :], ALU.mult, ALU.add)
                dve.drain()
                dve.tensor_tensor_scan(g_cum[:, j, :], reset[:, :], lg[:, j, :], 0.0, ALU.mult, ALU.add)
                dve.drain()
                by_chunk = g_cum[:, j, :].rearrange("p (c i) -> p c i", i=GC)
                dve.tensor_tensor(lg[:, j, :].rearrange("p (c i) -> p c i", i=GC), by_chunk[:, :, GC - 1:GC].to_broadcast([P, NGC, GC]),
                                  by_chunk, ALU.subtract).then_inc(gate_cum, 1)
            for j in range(2):
                dve.wait_ge(gate_exp, j + 1)
                dve.tensor_tensor(qk[:, j, :], qk[:, j, :], e_pos[:, j, :], ALU.mult)
                dve.tensor_tensor(k_end[:, j, :], qk[:, 2 + j, :], lg[:, j, :], ALU.mult)
                dve.tensor_tensor(qk[:, 2 + j, :], qk[:, 2 + j, :], e_neg[:, j, :], ALU.mult).then_inc(gla_qk, 1)
            for hh in range(2):
                dve.wait_ge(gla_att, hh + 1)
                dve.tensor_tensor(att_s[:, hh, :, :], ps[:, 4 + hh, :].rearrange("p (c i) -> p c i", i=GC),
                                  mask64[:, :].unsqueeze(1).to_broadcast([P, 8, GC]), ALU.mult).then_inc(gla_attc, 1)
            dve.memset(s_gla[:, :, 0, :], 0.0)
            dve.drain()
            for c in range(NGC - 1):
                for j in range(2):
                    if c == 0:
                        dve.wait_ge(gla_st, 2)
                    last = dve.scalar_tensor_tensor(s_gla[:, j, c + 1, :], s_gla[:, j, c, :], e_pos[:, j, c * GC + GC - 1:c * GC + GC],
                                                    ps[:, j * 2 + c % 2, (c // 2) * GDV:(c // 2 + 1) * GDV], ALU.mult, ALU.add)
                if c < NGC - 2:
                    dve.drain()
            last.then_inc(gla_S, 1)
            for tb in range(TB):
                b = (tb % 2) * 3
                dve.wait_ge(gla_oc, tb + 1)
                pairs = o_s[:, tb % 2, :].rearrange("p (j h v) -> p j h v", j=2, h=2)
                for hh in range(2):
                    last = dve.tensor_tensor(pairs[:, :, hh, :], pairs[:, :, hh, :],
                                             ps[:, b + 1 + hh, 0:2 * GDV].rearrange("p (j v) -> p j v", j=2), ALU.add)
                last.then_inc(gla_od, 1)
                dve.wait_ge(gla_sd, tb + 1)
                dve.reciprocal(rstd[:, 0:GH], sd[:, 0:GH])
                dve.drain()
                for h in range(GH):
                    hs = slice(h * GDV, (h + 1) * GDV)
                    last = dve.scalar_tensor_tensor(xn[:, tb, hs], o_s[:, tb % 2, hs], rstd[:, h:h + 1], xn[:, tb, hs], ALU.mult, ALU.mult)
                last.then_inc(gla_y, 1)

            dve.wait_ge(xt_c, TB + 1)
            dve.memset(s_ssd[:, 0, :], 0.0)
            for tb in range(TB):
                heads = lambda v: v.rearrange("p (h e) -> p h e", e=SP_)
                dve.tensor_tensor(heads(xdt[:, tb, :]), heads(xt[:, tb, :]), dta[:, tb, 0, :].unsqueeze(2).to_broadcast([P, SH, SP_]), ALU.mult)
                dve.drain()
                dve.tensor_tensor(heads(xdte[:, tb, :]), heads(xdt[:, tb, :]), ecum[:, 1, tb, :].unsqueeze(2).to_broadcast([P, SH, SP_]),
                                  ALU.mult).then_inc(xd_done, 1)
                if tb == 0:
                    dve.drain().then_inc(ssd_S, 1)
                for g in range(SG):
                    dve.wait_ge(ssd_L, 2 * tb + g + 1)
                    if tb >= 1:
                        dve.wait_ge(ssd_y, tb)
                    dve.tensor_tensor(w_s[:, g, :].rearrange("p (j l) -> p j l", j=SJ), l_s[:, g, :].rearrange("p (j l) -> p j l", j=SJ),
                                      ps[:, 2 + g, 0:P].unsqueeze(1).to_broadcast([P, SJ, P]), ALU.mult).then_inc(ssd_W, 1)
                dve.wait_ge(ssd_st, tb + 1)
                if tb < TB - 1:
                    for g in range(SG):
                        n = slice(g * SN, (g + 1) * SN)
                        dve.tensor_tensor(heads(s_ssd[n, tb + 1, :]), heads(s_ssd[n, tb, :]),
                                          ecum[n, 2, tb, g * SJ:(g + 1) * SJ].unsqueeze(2).to_broadcast([SN, SJ, SP_]), ALU.mult)
                    dve.drain()
                    dve.tensor_tensor(s_ssd[:, tb + 1, :], s_ssd[:, tb + 1, :], ps[:, 6, 0:SJ * SP_], ALU.add).then_inc(ssd_S, 1)
                dve.wait_ge(ssd_y, tb + 1)
                dve.tensor_tensor(heads(y_t[:, 1, :]), heads(xt[:, tb, :]), col("d_skip", 0, SH).unsqueeze(2).to_broadcast([P, SH, SP_]), ALU.mult)
                for g in range(SG):
                    gs = slice(g * SJ * SP_, (g + 1) * SJ * SP_)
                    dve.tensor_tensor(heads(y_t[:, 0, gs]), heads(ps[:, 7 - 3 * g, 0:SJ * SP_]),
                                      ecum[:, 0, tb, g * SJ:(g + 1) * SJ].unsqueeze(2).to_broadcast([P, SJ, SP_]), ALU.mult)
                dve.drain()
                dve.tensor_tensor(y_t[:, 1, :], y_t[:, 1, :], y_t[:, 0, :], ALU.add)
                dve.drain()
                dve.tensor_tensor(y_t[:, 1, :], y_t[:, 1, :], ps[:, 5, :], ALU.add).then_inc(ssd_yd, 1)
                dve.drain()
                dve.tensor_tensor(y_t[:, 1, :], y_t[:, 1, :], xn[:, tb, GW:], ALU.mult).then_inc(ssd_yc, 1)
                dve.wait_ge(ssd_sd, tb + 1)
                dve.reciprocal(rstd[:, 0:SG], sd[:, 0:SG])
                dve.drain()
                for g in range(SG):
                    gs = slice(g * SJ * SP_, (g + 1) * SJ * SP_)
                    last = dve.tensor_scalar(xn[:, tb, GW + g * SJ * SP_:GW + (g + 1) * SJ * SP_], y_t[:, 1, gs], rstd[:, g:g + 1], None, ALU.mult)
                last.then_inc(xn_done, 1)
            transposed(1, lambda kt: col("gla_norm") if kt < 4 else col("ssd_norm", kt - 4))
            for g in range(2):
                ahead(C_WOUT + 2 * g)
                ahead(C_WOUT + 2 * g + 1)
                for tb in range(TB):
                    dve.wait_ge(tok_done, TB * (G_WOUT + g) + tb + 1)
                    s = slice(g * 512, (g + 1) * 512)
                    last = dve.tensor_tensor(res[:, tb, s], res[:, tb, s], ps[:, 4 - 4 * g + tb, :], ALU.add)
                    if g == 1:
                        last.then_inc(res_done, 1)

            normalise(1)
            transposed(2, lambda kt: col("norm_ffn", kt))
            for m in range(2 * N_QUERY):
                ahead(C_QUERY + m // 2)
                dve.wait_ge(q_hi_done, m + 1)
                dve.tensor_tensor(q_lo[:, m, :], ps[:, 4 + (F_QUERY + m) % 4, :], q_hi[:, m, :], ALU.subtract).then_inc(ft_out, 1)
            ahead(C_KEYS)
            dve.drain().then_inc(s_out, 2)

            def lo_in_loop(c, n):
                s = (c + AHEAD) % RING
                dve.wait_ge(w_hi_done, n + 1)
                dve.tensor_tensor(w_lo[:, s, :], w_st[:, s, :], w_hi[:, s, :], ALU.subtract).then_inc(w_lo_done, 1)

            def best_keys(i, h):
                dve.wait_ge(s_done, 8 * i + h + 1)
                dve.tensor_copy(s_sb, ps[:, 2 + h % 2, 0:2 * PK].rearrange("p (a k) -> p a k", a=2)).then_inc(s_out, 1)
                dve.drain()
                for a in range(2):
                    dve.max(top_v[:, a, 0:8], s_sb[:, a, :])
                dve.drain()
                for a in range(2):
                    dve.max_index(top_i[:, a, 0:8], top_v[:, a, 0:8], s_sb[:, a, :])
                    dve.match_replace(s_cut[:, a, :], top_v[:, a, 0:8], s_sb[:, a, :], LOWEST)
                dve.drain()
                for a in range(2):
                    dve.max(top_v[:, a, 8:16], s_cut[:, a, :])
                dve.drain()
                for a in range(2):
                    dve.max_index(top_i[:, a, 8:16], top_v[:, a, 8:16], s_cut[:, a, :])
                square = [P, PTOP, PTOP]
                dve.tensor_tensor(cand, top_v[:, 0, :].unsqueeze(2).to_broadcast(square), top_v[:, 1, :].unsqueeze(1).to_broadcast(square), ALU.add)
                dve.drain()
                flat, flat_cut = cand.rearrange("p a b -> p (a b)"), cand_cut.rearrange("p a b -> p (a b)")
                dve.max(best_v[:, 0:8], flat)
                dve.drain()
                dve.max_index(best_p[:, 0:8], best_v[:, 0:8], flat)
                dve.match_replace(flat_cut, best_v[:, 0:8], flat, LOWEST)
                dve.drain()
                dve.max(best_v[:, 8:16], flat_cut)
                dve.drain()
                dve.max_index(best_p[:, 8:16], best_v[:, 8:16], flat_cut)
                dve.drain()
                dve.tensor_scalar(best_k[:, 0, :], best_p, 4, None, ALU.logical_shift_right)
                dve.tensor_scalar(best_k[:, 1, :], best_p, PTOP - 1, None, ALU.bitwise_and)
                at = slice(h * PTOP, (h + 1) * PTOP)
                dve.tensor_copy(score.rearrange("p (t s) -> p t s", t=TB)[:, i, at], best_v)
                dve.drain()
                for a in range(2):
                    dve.tensor_tensor(pick[:, a, :, :], best_k[:, a, :].unsqueeze(2).to_broadcast(square),
                                      iota_f[:, 0:PTOP].unsqueeze(1).to_broadcast(square), ALU.is_equal)
                dve.drain()
                for a in range(2):
                    dve.tensor_tensor(pick[:, a, :, :], pick[:, a, :, :], top_i[:, a, :].unsqueeze(1).to_broadcast(square), ALU.mult)
                dve.drain()
                for a, key in enumerate((key1, key2)):
                    dve.tensor_reduce(key.rearrange("p (t s) -> p t s", t=TB)[:, i, at], pick[:, a, :, :], AX_X, ALU.add)

            with dve.Fori(0, 4) as i:
                for c in range(8):
                    lo_in_loop(c, C_U + 8 * i + c + AHEAD)
                    best_keys(i, c)
            dve.drain()
            by_head = lambda v: v.rearrange("p (h s) -> p h s", s=PTOP)
            whole = [P, TB * PH, PTOP]
            dve.tensor_tensor(by_head(gate_t), by_head(score), by_head(score)[:, :, 0:1].to_broadcast(whole), ALU.subtract).then_inc(soft_x, 1)
            dve.wait_ge(soft_e, 1)
            dve.tensor_reduce(soft[:, 0, :], by_head(gate_t), AX_X, ALU.add)
            dve.drain()
            dve.reciprocal(soft[:, 1, :], soft[:, 0, :])
            dve.drain()
            dve.tensor_tensor(by_head(score), by_head(gate_t), soft[:, 1, :].unsqueeze(2).to_broadcast(whole), ALU.mult).then_inc(soft_done, 1)
            dve.wait_ge(slot_tp, 1)
            dve.tensor_copy(slot_T[:, 0, :], ps[:, 4, :])
            dve.tensor_copy(slot_T[:, 1, :], ps[:, 5, :])
            dve.tensor_copy(g_b16, ps[:, 6, :])
            dve.drain()
            dve.tensor_copy(slot_T[:, 2, :], g_b16)
            dve.tensor_tensor(slot_T[:, 3, :], ps[:, 6, :], g_b16, ALU.subtract).then_inc(slot_done, 1)
            dve.drain()
            with dve.Fori(4, 8) as i:
                for c in range(8):
                    if c % 4 == 0:
                        first = (i - 4) * P + (c // 4) * 64
                        dve.drain()
                        dve.tensor_copy(c_slot, slot_T[:, :, bass.ds(first, 64)])
                        dve.drain()
                    for t in range(2):
                        if t == 1:
                            lo_in_loop(c, C_U + 8 * i + c + AHEAD)
                        at = 2 * c + t
                        dve.wait_ge(g_done, 2 * (16 * (i - 4) + at) + 2)
                        toks = slice((at % 8) * 8, (at % 8) * 8 + 8)
                        dve.tensor_tensor(oh_b[:, at % 2, :, :], iota_b[:, :].unsqueeze(1).to_broadcast([P, 8, PK]),
                                          c_slot[:, 1, toks].unsqueeze(2).to_broadcast([P, 8, PK]), ALU.is_equal)
                        for r in range(8):
                            k = (at % 8) * 8 + r
                            for part in range(2):
                                last = dve.tensor_scalar(oh_a[:, at % 2, r, part, :], iota_b[:, :], c_slot[:, 0, k:k + 1],
                                                         c_slot[:, 2 + part, k:k + 1], ALU.is_equal, ALU.mult)
                        last.then_inc(oh_done, 1)
            dve.drain().then_inc(h_mul, 2)
            with dve.Fori(0, N_V // 4) as i:
                for c in range(4):
                    dve.wait_ge(ga_ld[c % 2], 16 * (2 * i + c // 2 + 1))
                    dve.wait_ge(g_ld[c % 2], 16 * (2 * i + c // 2 + 1))
                    for j in range(2):
                        by_group = lambda v: v.rearrange("p (g t) -> p g t", g=8)
                        last = dve.tensor_tensor(by_group(h_f[:, c % 2, j, :]), by_group(ga_in[:, c % 2, j, :]), g_in[:, c % 2, :, j, :], ALU.mult)
                    last.then_inc(h_mul, 1)
                    dve.wait_ge(h_hi_done, 4 * i + c + 1)
                    dve.tensor_tensor(h_lo[:, c % 2, :, :], h_f[:, c % 2, :, :], h_hi[:, c % 2, :, :], ALU.subtract).then_inc(h_lo_done, 1)
                    lo_in_loop(c, C_V + 4 * i + c + AHEAD)
            split[0] = C_CONV + AHEAD
            for b in range(8):
                dve.wait_ge(peer_done, b + 1)
                s = slice((b % 2) * 512, (b % 2 + 1) * 512)
                last = dve.tensor_tensor(res[:, b // 2, s], res[:, b // 2, s], ps[:, b, :], ALU.add)
                if b % 2:
                    last.then_inc(res_done, 1)

            dve.wait_ge(sd_done, 3)
            dve.reciprocal(rstd[:, 0:TB], sd[:, 0:TB])
            dve.drain()
            dve.wait_ge(row_ld, 16)
            for tb in range(TB):
                last = dve.scalar_tensor_tensor(res[:, tb, :], res[:, tb, :], rstd[:, tb:tb + 1], row[:, :], ALU.mult, ALU.mult).then_inc(res_done, 1)
            dve.drain().then_inc(row_used, 1)
            normalise(3)
            dve.memset(n_cum, 0.0)
            dve.memset(f_one[0:AH, :], 1.0)
            dve.memset(z_s[:, 0:4], 0.0)
            transposed(3, lambda kt: col("norm_mix2", kt))
            dve.wait_ge(f_mm, 1)
            dve.tensor_scalar(f_x[0:AH, :], ps[0:AH, 2, :], col("b_forget")[0:AH, :], None, ALU.add).then_inc(f_xs, 1)
            dve.wait_ge(f_ln, 1)
            dve.scalar_tensor_tensor(f_x[0:AH, :], f_x[0:AH, :], 0.0, f_e[0:AH, :], ALU.min, ALU.subtract)
            dve.drain()
            dve.tensor_tensor_scan(n_cum[0:AH, :], f_one[0:AH, :], f_x[0:AH, :], 0.0, ALU.mult, ALU.subtract).then_inc(f_cum, 1)

            def conv_low(j):
                dve.wait_ge(cv_hi, j + 1)
                dve.tensor_tensor(c_lo[:, j, :], cv_s[:, j % 2, :], c_hi[:, j, :], ALU.subtract).then_inc(cv_lo, 1)

            for j in range(KT):
                for a in range(3):
                    ahead(C_CONV + (3 * j + a) // 2)
                dve.wait_ge(ft_out, F_CONV + 3 * j + 2)
                dve.tensor_tensor(z_s[:, 4:], cu_s[:, j % 2, :], cc_s[:, j % 2, :], ALU.mult)
                dve.drain()
                dve.tensor_scalar(acc_s, z_s[:, 2:2 + T], col("conv_w2", j * CONVW), col("conv_b2", j), ALU.mult, ALU.add)
                for k in range(1, CONVW):
                    dve.drain()
                    dve.scalar_tensor_tensor(acc_s, z_s[:, 2 + k:2 + k + T], col("conv_w2", j * CONVW + k), acc_s, ALU.mult, ALU.add)
                dve.drain()
                dve.wait_ge(ft_out, F_CONV + 3 * j + 3)
                dve.tensor_tensor(cv_s[:, j % 2, :], acc_s, cb_s[:, j % 2, :], ALU.mult).then_inc(cv_mul, 1)
                if j:
                    conv_low(j - 1)
            conv_low(KT - 1)
            for j in range(KT):
                ahead(C_CO + j)
                dve.wait_ge(sg_done, j + 1)
                dve.wait_ge(ft_done, F_CO + 2 * j + 2)
                dve.tensor_tensor(m1[:, j, :], ps[:, 5 + 2 * (j % 2), :], sg_s[:, j % 2, :], ALU.mult).then_inc(m1_done, 1)
            for g in range(2):
                ahead(C_V2 + 2 * g)
                ahead(C_V2 + 2 * g + 1)
            dve.memset(q_z, 0.0).then_inc(qz_zero, 1)
            for u in range(len(UNITS) + 2):
                if u < len(UNITS):
                    h, qb = UNITS[u]
                    if h % 2 == 0 and qb == 0:
                        ahead(C_QK + h // 2)
                    dve.wait_ge(at_s, u + 1)
                    if u >= 2:
                        dve.wait_ge(at_p, u - 1)
                    dve.tensor_reduce(n_max[:, u % 2:u % 2 + 1], ps[:, u % 2, 0:(qb + 1) * P], AX_X, ALU.max, negate=True).then_inc(at_max, 1)
                if 1 <= u <= len(UNITS):
                    v = u - 1
                    n = UNITS[v][1] + 1
                    dve.wait_ge(at_t, v + 1)
                    if v >= 2:
                        dve.wait_ge(at_o, v - 1)
                    dve.tensor_copy(pT_s[:, v % 2, 0:n, :], ps[:, 2 + v % 2, 0:n * P].rearrange("p (k q) -> p k q", k=n)).then_inc(at_tc, 1)
                if u >= 2:
                    v = u - 2
                    h, qb = UNITS[v]
                    dve.reciprocal(r_inv[:, v % 2:v % 2 + 1], r_sum[:, v % 4:v % 4 + 1])
                    dve.drain()
                    dve.wait_ge(at_o, v + 1)
                    last = dve.tensor_scalar(xn[:, qb, h * ADH:(h + 1) * ADH], ps[:, 4 + v % 2, 0:ADH], r_inv[:, v % 2:v % 2 + 1], None, ALU.mult)
                    last.then_inc(at_out, 1)
            dve.drain().then_inc(xn_done, TB)
            transposed(4, lambda kt: 1.0, c_hi, c_lo)

            def mix_low(j):
                dve.wait_ge(mix_hi, j + 1)
                dve.tensor_tensor(m_split[:, j, 1, :], mix_s[:, j % 2, :], m_split[:, j, 0, :], ALU.subtract).then_inc(mix_lo, 1)

            for j in range(KT):
                ahead(C_AO + j)
                dve.wait_ge(sg_done, KT + j + 1)
                dve.wait_ge(ft_done, F_AO + 2 * j + 2)
                dve.tensor_tensor(prod_s[:, j % 2, :], ps[:, 5 + 2 * (j % 2), :], sg_s[:, j % 2, :], ALU.mult)
                dve.drain()
                dve.tensor_tensor(mix_s[:, j % 2, :], prod_s[:, j % 2, :], m1[:, j, :], ALU.add).then_inc(mix_done, 1)
                if j:
                    mix_low(j - 1)
            mix_low(KT - 1)
            for g in range(2):
                ahead(C_WO2 + 2 * g)
                ahead(C_WO2 + 2 * g + 1)
                for tb in range(TB):
                    dve.wait_ge(tok_done, TB * (G_WO2 + g) + tb + 1)
                    s = slice(g * 512, (g + 1) * 512)
                    last = dve.tensor_tensor(res[:, tb, s], res[:, tb, s], ps[:, 4 * g + tb, :], ALU.add)
                    if g == 1:
                        last.then_inc(res_done, 1)

            dve.wait_ge(sd_done, 5)
            dve.reciprocal(rstd[:, 0:TB], sd[:, 0:TB])
            dve.drain()
            dve.wait_ge(row_ld, 32)
            for tb in range(TB):
                dve.scalar_tensor_tensor(xn[:, tb, :], res[:, tb, :], rstd[:, tb:tb + 1], row[:, :], ALU.mult, ALU.mult).then_inc(xn_done, 1)
            dve.drain().then_inc(row_used, 1)
            transposed(5, lambda kt: 1.0)
            for tb in range(TB):
                dve.wait_ge(pk_hi, tb + 1)
                dve.tensor_tensor(pk[:, tb, 1, :], xn[:, tb, :], pk[:, tb, 0, :], ALU.subtract).then_inc(pk_lo, 1)
            dve.memset(lr_g, LOWEST)
            dve.wait_ge(rt_mm, 1)
            dve.tensor_copy(lr, ps[:, 2, 0:TB * SM_R].rearrange("p (t n) -> p t n", t=TB))
            dve.drain()
            dve.tensor_copy(lr_g[:, :, 0:EG], lr[:, :, 0:EG])
            dve.drain()
            for tb in range(TB):
                dve.max(g_max[:, tb, :], lr_g[:, tb, :])
            dve.drain()
            for tb in range(TB):
                dve.max_index(g_idx[:, tb, :], g_max[:, tb, :], lr_g[:, tb, :])
            dve.tensor_tensor(r_exp[:, :, 0:EG], lr[:, :, 0:EG], g_max[:, :, 0:1].to_broadcast([P, TB, EG]), ALU.subtract)
            dve.drain()
            dve.tensor_copy(g_num, g_idx[:, :, 0])
            dve.drain()
            dve.tensor_tensor(g_one, g_num.unsqueeze(2).to_broadcast([P, TB, EG]), iota_f[:, 0:EG].unsqueeze(1).to_broadcast([P, TB, EG]), ALU.is_equal)
            dve.drain()
            dve.tensor_tensor(le_all, lr[:, :, EG:].rearrange("p t (g e) -> p t g e", g=EG), g_one.unsqueeze(3).to_broadcast([P, TB, EG, EPG]), ALU.mult)
            dve.drain()
            dve.tensor_reduce(le_sel, le_all.rearrange("p t g e -> p t e g"), AX_X, ALU.add)
            dve.drain()
            for tb in range(TB):
                dve.max(e_max[:, tb, :], le_sel[:, tb, :])
            dve.drain()
            for tb in range(TB):
                dve.max_index(e_idx[:, tb, :], e_max[:, tb, :], le_sel[:, tb, :])
            dve.tensor_tensor(r_exp[:, :, EG:EG + 1], e_max[:, :, 1:2], e_max[:, :, 0:1], ALU.subtract).then_inc(rt_x, 1)
            dve.drain()
            for s in range(2):
                dve.tensor_copy(e_num[:, s, :], e_idx[:, :, s])
            dve.drain()
            for s in range(2):
                dve.scalar_tensor_tensor(e_of[:, s, :], g_num, float(EPG), e_num[:, s, :], ALU.mult, ALU.add)
            dve.drain()
            for s in range(2):
                dve.tensor_tensor(e_one[:, s, :, :], e_of[:, s, :].unsqueeze(2).to_broadcast([P, TB, NE]),
                                  iota_f[:, 0:NE].unsqueeze(1).to_broadcast([P, TB, NE]), ALU.is_equal)
            dve.drain()
            dve.tensor_tensor(e_any, e_one[:, 0, :, :], e_one[:, 1, :, :], ALU.add).then_inc(rt_pick, 1)
            dve.wait_ge(rt_e, 1)
            dve.tensor_reduce(g_sum, r_exp[:, :, 0:EG], AX_X, ALU.add)
            dve.drain()
            dve.scalar_tensor_tensor(w_den, r_exp[:, :, EG], 1.0, g_sum, ALU.add, ALU.mult)
            dve.drain()
            dve.reciprocal(w_tok[:, 0, :], w_den)
            dve.drain()
            dve.tensor_tensor(w_tok[:, 1, :], w_tok[:, 0, :], r_exp[:, :, EG], ALU.mult)
            dve.wait_ge(rt_rank, 1)
            up_to = ps[:, 3, 0:TB * NE].rearrange("p (t e) -> p t e", t=TB)
            for s in range(2):
                dve.tensor_tensor(e_rank[:, s, :, :], e_one[:, s, :, :], up_to, ALU.mult)
            dve.tensor_reduce(n_rows, ps[:, 3, TB * NE:(TB + 1) * NE], AX_X, ALU.max)
            dve.drain()
            dve.tensor_reduce(rank_f, e_rank, AX_X, ALU.add)
            dve.tensor_copy(n_rows_i, n_rows)
            dve.drain()
            dve.tensor_scalar(rank_u, rank_f, -1.0, None, ALU.add)
            dve.drain()
            dve.tensor_scalar(blk_u[:, 0, :, :], rank_u, CAP.bit_length() - 1, None, ALU.logical_shift_right)
            dve.tensor_scalar(blk_u[:, 1, :, :], rank_u, CAP - 1, None, ALU.bitwise_and)
            dve.drain()
            dve.tensor_copy(blk_f, blk_u)
            dve.drain()
            dve.scalar_tensor_tensor(e_blk, blk_f[:, 0, :, :], float(NE), e_of, ALU.mult, ALU.add)
            dve.drain()
            dve.scalar_tensor_tensor(to_tok, blk_f[:, 1, :, :], float(PASSES * NE), e_blk, ALU.mult, ALU.add)
            dve.scalar_tensor_tensor(to_y, e_blk, float(CAP), blk_f[:, 1, :, :], ALU.mult, ALU.add)
            dve.drain().then_inc(rt_dest, 1)

            def lo_of(r, i, k):
                s = k % RING
                dve.wait_ge(w_hi_done, r * PASS + 12 * i + (C_MOE + k + 1))
                dve.tensor_tensor(w_lo[:, s, :], w_st[:, s, :], w_hi[:, s, :], ALU.subtract).then_inc(w_lo_done, 1)

            def rows_lo(r, i, c):
                dve.wait_ge(xe_tp, 2 * moe(r, i, c) + 6)
                dve.tensor_copy(xeT[:, c % 2, 1, :, :].rearrange("p k t -> p (k t)"), ps[:, 7, 0:KT * CAP]).then_inc(xe_lo, 1)

            def hidden(r, i, c, k):
                dve.wait_ge(sil_done, moe(r, i, c) + 1)
                dve.wait_ge(moe_mm, r * PASS + 12 * i + (k + 2 + RING))
                dve.tensor_tensor(hid_f[0:CAP, :], sil[0:CAP, :], ps[0:CAP, 1, :], ALU.mult).then_inc(hid_mul, 1)

            def hidden_lo(r, i, c):
                dve.wait_ge(hid_hi, moe(r, i, c) + 1)
                dve.tensor_tensor(hid_b[0:CAP, 1, :], hid_f[0:CAP, :], hid_b[0:CAP, 0, :], ALU.subtract).then_inc(hid_lo, 1)

            def first(r):
                for k in range(AHEAD):
                    lo_of(r, 0, k)
                rows_lo(r, 0, 0)
                rows_lo(r, 0, 1)
                for k in range(AHEAD, 7):
                    lo_of(r, 0, k)

            def step(r, i, c, more=True):
                k = 6 * c - 2
                hidden(r, i, c - 1, k - 2)
                lo_of(r, i, k + 3)
                hidden_lo(r, i, c - 1)
                lo_of(r, i, k + 4)
                if more:
                    rows_lo(r, i, c + 1)
                for n in range(5, 9 if more else 8):
                    lo_of(r, i, k + n)

            def last(r):
                step(r, 0, NE - 1, more=False)
                hidden(r, 0, NE - 1, PASS - 4)
                hidden_lo(r, 0, NE - 1)

            one_pass = every_expert(first, step, last)
            one_pass(dve, 0)
            more_passes(dve, one_pass)

            def finish(tb):
                dve.wait_ge(end_sd, tb + 1)
                dve.reciprocal(rstd[:, tb:tb + 1], sd[:, tb:tb + 1])
                dve.drain()
                dve.scalar_tensor_tensor(xn[:, tb, :], res[:, tb, :], rstd[:, tb:tb + 1], row[:, :], ALU.mult, ALU.mult).then_inc(end_done, 1)

            dve.wait_ge(row_ld, 48)
            for tb in range(TB):
                dve.wait_ge(yg_ld[tb], 32)
                for s in range(2):
                    last = dve.scalar_tensor_tensor(res[:, tb, :], y_g[:, tb, s, :], w_tok[:, s, tb:tb + 1], res[:, tb, :], ALU.mult, ALU.add)
                    if s == 0:
                        dve.drain()
                last.then_inc(res_done, 1)
                if tb:
                    finish(tb - 1)
            finish(TB - 1)


def _features(w):
    n = w.shape[1] // P
    return w.reshape(KT, P, n, P).transpose(2, 1, 0, 3).reshape(n, P, D)


def _pairs(tiles):
    n = tiles.shape[0] // 2
    return tiles.reshape(n, 2, P, -1).transpose(0, 2, 1, 3).reshape(n, P, CW)


def _tokens(w):
    n, k = w.shape[1] // 512, w.shape[0] // 512
    return w.reshape(k, 4, P, n, 512).transpose(3, 0, 2, 1, 4).reshape(n * k, P, CW)


def _column(v):
    return v.reshape(-1, P).T


def _rows(v, at=0):
    out = np.zeros((P, 1), np.float32)
    out[at:at + v.shape[0], 0] = v
    return out


def lay_out(a):
    w_in = a["w_in"][0]
    ends = np.cumsum([GQK, GQK, GW, GRANK, GW, SW, XBC, SH])
    q, k, v, rank, gate, z, xbc, dt = np.split(w_in, ends[:-1], axis=1)
    f = np.float32
    w = np.empty((N_CHUNKS, P, CW), f)

    def put(at, n, chunks):
        assert chunks.shape == (n, P, CW), (at, n, chunks.shape)
        w[at:at + n] = chunks

    put(C_P1F, N_P1F, _pairs(_features(np.concatenate([q, k, xbc], 1))))
    put(C_P1T, N_P1T, _tokens(np.concatenate([v, gate, z], 1)))
    put(C_WOUT, N_WOUT, _tokens(a["w_out"][0]))
    put(C_QUERY, N_QUERY, _pairs(_features(a["peer_w_query"][0])))
    put(C_KEYS, N_KEYS, a["peer_sub_keys"][0].reshape(2 * PH, PK, P).transpose(2, 0, 1).reshape(1, P, CW))
    put(C_U, N_U, _pairs(a["peer_u"][0].reshape(PK, PK, KT, P).transpose(0, 3, 2, 1).reshape(PK, P, D)))
    put(C_V, N_V, _pairs(a["peer_v"][0].reshape(PK, PK, D)))
    sizes = [D] * 6 + [AH, D, D]
    cb, cc, cu, q2, k2, v2, fl, gc, ga = np.split(a["w_in_2"], np.cumsum(sizes)[:-1], axis=1)
    mix = lambda *ws: _pairs(np.stack([_features(x) for x in ws], 1).reshape(-1, P, D))
    put(C_CONV, N_CONV, mix(cu, cc, cb))
    put(C_CO, N_CO, mix(gc, a["w_conv_out_2"]))
    put(C_V2, N_V2, _tokens(v2))
    put(C_QK, N_QK, mix(q2, k2))
    put(C_AO, N_AO, mix(ga, a["w_att_out_2"]))
    put(C_WO2, N_WO2, _tokens(a["w_out_2"]))
    gates = a["w_e_gate_2"].reshape(NE, 2, 4, P, DE).transpose(0, 1, 3, 2, 4).reshape(NE, 2, P, CW)
    ups = a["w_e_up_2"].reshape(NE, 2, 4, P, DE).transpose(0, 1, 3, 2, 4).reshape(NE, 2, P, CW)
    downs = a["w_e_down_2"].reshape(NE, 2, 2, P, D).transpose(0, 1, 3, 2, 4).reshape(NE, 2, P, CW)
    for e in range(NE):
        w[MOE_GATE(e):MOE_GATE(e) + 2] = gates[e]
        w[MOE_UP(e):MOE_UP(e) + 2] = ups[e]
        w[MOE_DOWN(e):MOE_DOWN(e) + 2] = downs[e]
    small_in = np.zeros((KT, P, SM_IN), f)
    small_in[:, :, 0:GRANK] = rank.reshape(KT, P, GRANK)
    small_in[:, :, DT0:DT0 + SH] = dt.reshape(KT, P, SH)
    router = np.concatenate([a["w_router_group_2"], a["w_router_expert_2"].transpose(1, 0, 2).reshape(D, NE)], 1)
    gate2 = np.zeros((P, GQK), f)
    gate2[0:GRANK] = a["gla_w_gate2"][0]
    by_part = lambda x: x.reshape(KT, P, -1).transpose(1, 0, 2).reshape(P, -1)
    small = np.concatenate([by_part(small_in), by_part(fl), by_part(router), gate2], 1)
    taps = lambda x: x.reshape(x.shape[0], -1, P).transpose(2, 1, 0).reshape(P, -1)
    table = np.concatenate([
        _column(a["norm_mix_w"][0]), _column(a["gla_b_gate"][0]), _column(a["gla_norm_w"][0]), taps(a["ssd_conv_w"][0]),
        _column(a["ssd_conv_b"][0]), _rows(a["ssd_dt_bias"][0], DT0), _rows(a["ssd_a_log"][0], DT0),
        np.broadcast_to(a["ssd_d"][0], (P, SH)), _column(a["ssd_norm_w"][0]), _column(a["norm_ffn_w"][0]),
        _column(a["norm_mix_g_2"]), taps(a["conv_w_2"]), _column(a["conv_b_2"]), _rows(a["b_forget_2"]),
    ], 1)
    return {
        "w_all": w, "x": np.ascontiguousarray(a["x"][0]), "cols": np.ascontiguousarray(table), "small": np.ascontiguousarray(small),
        "row_final": a["norm_final_w"].reshape(1, D), "row_ffn2": a["norm_ffn_g_2"].reshape(1, D),
        "row_final2": a["norm_final_g_2"].reshape(1, D),
    }


def kernel(**inputs):
    import concourse.bacc as bacc
    from concourse.bass_utils import run_bass_kernel_spmd

    arrays = lay_out({k: np.asarray(v) for k, v in inputs.items()})
    nc = bacc.Bacc("TRN2", target_bir_lowering=False, num_devices=1)
    args = [nc.dram_tensor("in_" + k, v.shape, mybir.dt.from_np(v.dtype), kind="ExternalInput").ap() for k, v in arrays.items()]
    out = nc.dram_tensor("out", (T, D), F32, kind="ExternalOutput").ap()
    build_program(nc, *args, out)
    r = run_bass_kernel_spmd(nc, [{"in_" + k: v for k, v in arrays.items()}], core_ids=[0])
    return r.results[0]["out"].reshape(1, T, D)
```

```python
from contextlib import ExitStack

import numpy as np

import concourse.bass as bass
from concourse import mybir

F32 = mybir.dt.float32
BF16 = mybir.dt.bfloat16
I32 = mybir.dt.int32
U32 = mybir.dt.uint32
ALU = mybir.AluOpType
ACT = mybir.ActivationFunctionType
AX_X = mybir.AxisListType.X

P = 128
T = 512
TB = T // P
D = 1024
KT = D // P
EPS = 1e-6
NEG = -1.0e30
LOWEST = -3.4e38

GH, GDK, GDV, GC = 4, 64, 128, 64
GQK, GW, GRANK = GH * GDK, GH * GDV, 16
NGC = T // GC
GATE_NORM = 16.0
SH, SP_, SG, SN, SCONV = 8, 64, 2, 64, 4
SJ = SH // SG
SW = SH * SP_
XBC = SW + 2 * SG * SN
PH, PK, PTOP = 8, 128, 16
PE_N = PK * PK
SLOTS = PH * PTOP
CONVW = 3
AH, ADH = 16, 64
EG, EPG, DE = 4, 8, 512
NE = EG * EPG
CAP = 64
PASSES = T // CAP

CW = 2048
RING = 4
AHEAD = 3
N_P1F = (2 * GQK + XBC) // P // 2
N_P1T = 3 * 2
N_WOUT = 4
N_QUERY = 2 * PH // 2
N_KEYS = 1
N_U = PK // 2
N_V = PK // 2
N_CONV = 3 * KT // 2
N_CO = KT
N_V2 = 4
N_QK = KT
N_AO = KT
N_WO2 = 4
N_MOE = NE * 6
MOE_RING = 6
C_P1F = 0
C_P1T = C_P1F + N_P1F
C_WOUT = C_P1T + N_P1T
C_QUERY = C_WOUT + N_WOUT
C_KEYS = C_QUERY + N_QUERY
C_U = C_KEYS + N_KEYS
C_V = C_U + N_U
C_CONV = C_V + N_V
C_CO = C_CONV + N_CONV
C_V2 = C_CO + N_CO
C_QK = C_V2 + N_V2
C_AO = C_QK + N_QK
C_WO2 = C_AO + N_AO
C_MOE = C_WO2 + N_WO2
N_CHUNKS = C_MOE + N_MOE

_cols = {}
_at = 0
for _name, _n in (("gla_b", 2), ("gla_norm", 1), ("conv_w", 6 * SCONV), ("conv_b", 6),
                  ("dt_b", 1), ("a_log", 1), ("d_skip", SH), ("ssd_norm", 4),
                  ("conv_w2", KT * CONVW), ("conv_b2", KT), ("b_forget", 1)):
    _cols[_name] = _at
    _at += _n
N_COLS = _at
SM_IN, SM_F, SM_R = 40, 16, EG + NE
O_IN, O_F, O_R = 0, KT * SM_IN, KT * (SM_IN + SM_F)
N_SPLIT = KT * (SM_IN + SM_F + SM_R)
O_G2 = N_SPLIT
N_SMALL = N_SPLIT + GQK
DT0 = 32


def MOE_GATE(e):
    return C_MOE + (0 if e == 0 else 4 + (e - 1) * 6)


def MOE_UP(e):
    return C_MOE + (2 if e == 0 else 4 + (e - 1) * 6 + 4)


def MOE_DOWN(e):
    return C_MOE + 4 + e * 6 + (2 if e < NE - 1 else 0)



def build_program(nc, w_all, x_in, cols_in, small_in, rows_in, out):
    ctx = ExitStack()
    with ctx:
        def sb(name, shape, dt=F32):
            return ctx.enter_context(nc.sbuf_tensor(name, shape, dt))

        def sem(name):
            return ctx.enter_context(nc.semaphore(name))

        w_st = sb("w_st", [P, RING, CW])
        w_hi = sb("w_hi", [P, RING, CW], BF16)
        w_lo = sb("w_lo", [P, RING, CW], BF16)
        res = sb("res", [P, TB, D])
        a_hi = sb("a_hi", [P, KT, T], BF16)
        a_lo = sb("a_lo", [P, KT, T], BF16)
        xn = sb("xn", [P, TB, D])
        cols = sb("cols", [P, N_COLS])
        small_hi = sb("small_hi", [P, N_SPLIT], BF16)
        small_lo = sb("small_lo", [P, N_SPLIT], BF16)
        ident = sb("ident", [P, P])
        ident_b = sb("ident_b", [P, P], BF16)
        tri_le = sb("tri_le", [P, P])
        tri_gt = sb("tri_gt", [P, P])
        tri_neg = sb("tri_neg", [P, P])
        neg_gt = sb("neg_gt", [P, P])
        neg_gt_b = sb("neg_gt_b", [P, P], BF16)
        ones = sb("ones", [P, P])
        mask64 = sb("mask64", [P, GC])
        eps = sb("eps", [P, 1])
        iota_i = sb("iota_i", [P, P], I32)
        ss = sb("ss", [P, 16])
        sd = sb("sd", [P, 16])
        rstd = sb("rstd", [P, 16])
        ARENA = 19712
        arena = sb("arena", [P, ARENA])
        ps = ctx.enter_context(nc.psum_tensor("ps", [P, 8, 512], F32))

        def col(name, i=0, n=1):
            return cols[:, _cols[name] + i:_cols[name] + i + n]

        def view(at, *shape, dt=F32):
            n = int(np.prod(shape)) * (2 if dt == BF16 else 4) // 4
            assert at + n <= ARENA, (at, n)
            v = arena[:, at:at + n]
            if dt != F32:
                v = v.bitcast(dt)
            names = "abcd"[:len(shape)]
            return v.rearrange(f"p ({' '.join(names)}) -> p {' '.join(names)}",
                               **{c: s for c, s in zip(names, shape)}) if len(shape) > 1 else v

        o = 0
        qk = view(o, 4, T); xdte = view(o, TB, T); o += 4 * T
        xbc = view(o, 6, T + 4); o += 6 * (T + 4)
        xt = view(o - 6 * (T + 4), TB, T); bt = view(o - 6 * (T + 4) + 4 * T, TB, P)
        sm = view(o, T); o += T
        vT = view(o, TB, GW); o += TB * GW
        lg = view(o, 2, T); att_s = view(o, 2, 8, GC); l_s = view(o, 2, 4 * P); o += 2 * T
        g_cum = view(o, 2, T); e_neg = view(o + 2 * T, 2, T); s_gla = view(o, 2, NGC, GDV); xdt = view(o, TB, T); o += 4 * T
        e_pos = view(o, 2, T); y_t = view(o, 2, T); o += 2 * T
        k_end = view(o, 2, T); o_s = view(o, 2, T); w_s = view(o, 2, 4 * P); o += 2 * T
        small = view(o, N_SMALL); k_endT = view(o, 2, TB, P); s_ssd = view(o, TB, SJ * SP_); o += 2 * T
        xc = view(o, 6, T); o += 6 * T
        reset = view(o, T); o += T
        dtm = view(o, 4, T); o += 4 * T
        dta = view(o, TB, 2, SH); o += TB * 2 * SH
        ecum = view(o, 3, TB, SH); o += 3 * TB * SH
        ea = view(o, 2); o += 2

        q_hi = view(0, 2 * PH, T, dt=BF16)
        q_lo = view(4 * 1024, 2 * PH, T, dt=BF16)
        keys_hi = view(8 * 1024, 2 * PH, PK, dt=BF16)
        keys_lo = view(9 * 1024, 2 * PH, PK, dt=BF16)
        o = 10 * 1024
        s_cut = view(o, 2, PK); o += 2 * PK
        top_v = view(o, 2, PTOP); o += 2 * PTOP
        top_i = view(o, 2, PTOP, dt=U32); o += 2 * PTOP
        cand = view(o, PTOP, PTOP); o += PTOP * PTOP
        cand_cut = view(o, PTOP, PTOP); o += PTOP * PTOP
        best_v = view(o, PTOP); o += PTOP
        best_p = view(o, PTOP, dt=U32); o += PTOP
        best_k = view(o, 2, PTOP, dt=U32); o += 2 * PTOP
        pick = view(o, 2, PTOP, PTOP); o += 2 * PTOP * PTOP
        assert o <= 16 * 1024
        g_st = view(0, 2, PK, T // 8)
        slot_T = view(16 * 1024, 4, T)
        oh_b = view(18 * 1024, 2, 8, PK, dt=BF16)
        c_slot = view(19 * 1024, 4, T // 8)
        xn_flat = xn[:, :, :].rearrange("p t d -> p (t d)")
        u_st = xn_flat[:, 0:2048].rearrange("p (r j t) -> p r j t", r=2, j=2)
        key1 = xn_flat[:, 2048:2560]
        key2 = xn_flat[:, 2560:3072]
        score = xn_flat[:, 3072:3584]
        gate_t = xn_flat[:, 3584:4096]
        oh_a = xn_flat[:, 2048:4096].bitcast(BF16).rearrange("p (r t s k) -> p r t s k", r=2, t=8, s=2)
        ga_in = view(0, 2, 2, T)
        g_in = view(2048, 2, 8, 2, T // 8)
        h_f = view(4096, 2, 2, T)
        h_hi = view(6144, 2, 2, T, dt=BF16)
        h_lo = view(7168, 2, 2, T, dt=BF16)
        g_b16 = view(18 * 1024, T, dt=BF16)
        first_st = sb("first_st", [P, 2, 3, 4])
        soft = sb("soft", [P, 2, TB * PH])
        iota_f = sb("iota_f", [P, P])
        iota_b = sb("iota_b", [P, P], BF16)
        tok_i = sb("tok_i", [P, TB], I32)
        tok_f = sb("tok_f", [P, TB])
        zero_b = sb("zero_b", [P, T], BF16)
        act_dram = nc.dram_tensor("act_dram", (N_U, P, 2 * T), F32, kind="Internal").ap()
        gate_dram = nc.dram_tensor("gate_dram", (8, P, PK, T // 8), F32, kind="Internal").ap()

        c_hi = view(0, KT, T, dt=BF16)
        c_lo = view(2048, KT, T, dt=BF16)
        m1 = view(4096, KT, T)
        m_split = view(4096, KT, 2, T, dt=BF16)
        v_s = view(8192, TB, D)
        cu_s, cc_s, cb_s = (view(8192 + 1024 * n, 2, T) for n in range(3))
        z_s = view(8192 + 3072, T + 4)
        q_z = view(12288, 2, 2, T)
        k_s = view(14336, 2, T)
        f_x, f_e = view(14336, T), view(14336 + T, T)
        p_s = view(15360, 2, T)
        acc_s = view(15360, T)
        mix_s = view(15360, 2, T)
        pT_s = view(16384, 2, TB, P)
        cv_s = view(16384, 2, T)
        prod_s = view(16384, 2, T)
        cum_b = view(17408, T, dt=BF16)
        n_cum = view(15360, T)
        c_rest = view(16384, 2, T)
        sg_s = view(17920, 2, T)
        f_one = view(18944, T)
        head_b = sb("head_b", [P, AH], BF16)
        moe_st = [w_st[:, s, :] for s in range(RING)] + [v[:, :, :].rearrange("p k t -> p (k t)").bitcast(F32) for v in (a_hi, a_lo)]
        pk = view(0, TB, 2, D, dt=BF16)
        x_g = view(4096, 2, 2, D, dt=BF16)
        xeT = view(6144, 2, 2, KT, CAP, dt=BF16)
        o = 6144 + 2 * KT * CAP
        sil = view(o, DE); o += DE
        hid_f = view(o, DE); o += DE
        hid_b = view(o, 2, DE, dt=BF16); o += DE
        hidT = view(o, 2, DE // P, CAP, dt=BF16); o += DE // P * CAP
        y_st = view(o, 2, D); o += 2 * D
        y_g = view(0, TB, 2, D)
        o = max(o, TB * 2 * D)
        lr = view(o, TB, SM_R); o += TB * SM_R
        lr_g = view(o, TB, 8); o += TB * 8
        g_max = view(o, TB, 8); o += TB * 8
        g_idx = view(o, TB, 8, dt=U32); o += TB * 8
        g_num = view(o, TB); o += TB
        g_one = view(o, TB, EG); o += TB * EG
        le_all = view(o, TB, EG, EPG); o += TB * NE
        le_sel = view(o, TB, EPG); o += TB * EPG
        e_max = view(o, TB, 8); o += TB * 8
        e_idx = view(o, TB, 8, dt=U32); o += TB * 8
        e_num = view(o, 2, TB); o += 2 * TB
        e_of = view(o, 2, TB); o += 2 * TB
        r_exp = view(o, TB, EG + 1); o += TB * (EG + 1)
        g_sum = view(o, TB); o += TB
        w_den = view(o, TB); o += TB
        w_tok = view(o, 2, TB); o += 2 * TB
        e_one = view(o, 2, TB, NE); o += 2 * TB * NE
        e_any = view(o, TB, NE); o += TB * NE
        e_rank = view(o, 2, TB, NE); o += 2 * TB * NE
        rank_f = view(o, 2, TB); o += 2 * TB
        rank_u = view(o, 2, TB, dt=U32); o += 2 * TB
        blk_u = view(o, 2, 2, TB, dt=U32); o += 4 * TB
        blk_f = view(o, 2, 2, TB); o += 4 * TB
        e_blk = view(o, 2, TB); o += 2 * TB
        to_y = view(o, 2, TB, dt=I32); o += 2 * TB
        row_one = view(o, 2, TB, CAP); o += 2 * TB * CAP
        now = view(o, 1); o += 1
        tok_now = view(o, 2, TB); o += 2 * TB
        tok_e = view(o, 2, TB, NE); o += 2 * TB * NE
        n_rows = view(o, 1); o += 1
        n_rows_i = view(o, 1, dt=I32); o += 1
        row_i = view(o, NE, dt=I32); o += NE
        idx = view(o, 2, dt=I32); o += 2
        x_dram = nc.dram_tensor("x_dram", (T, 2 * D), BF16, kind="Internal").ap()
        y_dram = nc.dram_tensor("y_dram", (PASSES * NE, CAP, D), F32, kind="Internal").ap()
        row = sb("row", [P, 2, D])
        n_max = sb("n_max", [P, 2])
        r_sum = sb("r_sum", [P, 4])
        r_inv = sb("r_inv", [P, 2])

        w_ld = [sem(f"w_ld{s}") for s in range(RING)]
        w_hi_done = sem("w_hi_done")
        w_lo_done = sem("w_lo_done")
        ft_done, ft_out = sem("ft_done"), sem("ft_out")
        tok_half, tok_done, tok_out = sem("tok_half"), sem("tok_done"), sem("tok_out")
        cols_ld, small_ld = sem("cols_ld"), sem("small_ld")
        x_ld = [sem(f"x_ld{tb}") for tb in range(TB)]
        small_hi_done, small_done = sem("small_hi_done"), sem("small_done")
        const_step, const_done = sem("const_step"), sem("const_done")
        res_done = sem("res_done")
        res2_done = sem("res2_done")
        sd_done, xn_done = sem("sd_done"), sem("xn_done")
        tp_done, tp_hi, tp_lo = sem("tp_done"), sem("tp_hi"), sem("tp_lo")
        sm_done, sm_out = sem("sm_done"), sem("sm_out")
        conv_done, silu_done = sem("conv_done"), sem("silu_done")
        gate_mm, gate_x, gate_ln, gate_cum, gate_exp = (sem(n) for n in ("gate_mm", "gate_x", "gate_ln", "gate_cum", "gate_exp"))
        dt_x, dt_ln, dt_done = sem("dt_x"), sem("dt_ln"), sem("dt_done")
        gla_qk, gla_kt, gla_ktc, gla_att, gla_attc, gla_st, gla_S = (
            sem(n) for n in ("gla_qk", "gla_kt", "gla_ktc", "gla_att", "gla_attc", "gla_st", "gla_S"))
        gla_o, gla_oc, gla_od, gla_sd, gla_y = (sem(n) for n in ("gla_o", "gla_oc", "gla_od", "gla_sd", "gla_y"))
        xt_tp, xt_c, dta_tp, dta_c, cum_mm, cum_exp = (sem(n) for n in ("xt_tp", "xt_c", "dta_tp", "dta_c", "cum_mm", "cum_exp"))
        xd_done, ssd_mm, ssd_L, ssd_W, ssd_st, ssd_S, ssd_y, ssd_yc, ssd_yd, ssd_sd = (
            sem(n) for n in ("xd_done", "ssd_mm", "ssd_L", "ssd_W", "ssd_st", "ssd_S", "ssd_y", "ssd_yc", "ssd_yd", "ssd_sd"))
        out_st = sem("out_st")
        row_ld, row_used = [sem(f"row_ld{b}") for b in range(2)], sem("row_used")
        f_mm, f_xs, f_ln, f_cum = (sem(n) for n in ("f_mm", "f_xs", "f_ln", "f_cum"))
        cv_mul, cv_hi, cv_lo = sem("cv_mul"), sem("cv_hi"), sem("cv_lo")
        sg_done, m1_done = sem("sg_done"), sem("m1_done")
        qz_zero, qk_out = sem("qz_zero"), sem("qk_out")
        at_s, at_max, at_p, at_t, at_tc, at_o, at_out = (sem(n) for n in ("at_s", "at_max", "at_p", "at_t", "at_tc", "at_o", "at_out"))
        mix_done, mix_hi, mix_lo = sem("mix_done"), sem("mix_hi"), sem("mix_lo")
        q_hi_done = sem("q_hi_done")
        u_done, u_out = sem("u_done"), sem("u_out")
        u_stored = [sem(f"u_stored{r}") for r in range(2)]
        s_done, s_out = sem("s_done"), sem("s_out")
        soft_x, soft_e, soft_done, slot_tp, slot_done = (sem(n) for n in ("soft_x", "soft_e", "soft_done", "slot_tp", "slot_done"))
        oh_done, g_done, g_out = sem("oh_done"), sem("g_done"), sem("g_out")
        g_stored = [sem(f"g_stored{b}") for b in range(2)]
        ga_ld = [sem(f"ga_ld{r}") for r in range(2)]
        g_ld = [sem(f"g_ld{r}") for r in range(2)]
        h_mul, h_hi_done, h_lo_done, v_done = (sem(n) for n in ("h_mul", "h_hi_done", "h_lo_done", "v_done"))
        peer_done = sem("peer_done")
        pk_hi, pk_lo, x_st = sem("pk_hi"), sem("pk_lo"), sem("x_st")
        rt_mm, rt_x, rt_e, rt_pick, rt_rank, rt_dest = (sem(n) for n in ("rt_mm", "rt_x", "rt_e", "rt_pick", "rt_rank", "rt_dest"))
        rt_all = sem("rt_all")
        rt_tok, rt_sum, rt_row = sem("rt_tok"), sem("rt_sum"), sem("rt_row")
        xe_ld = [sem(f"xe_ld{p}") for p in range(2)]
        xe_tp, xe_hi, xe_lo = sem("xe_tp"), sem("xe_hi"), sem("xe_lo")
        moe_ld = w_ld + [sem(f"moe_ld{s}") for s in range(RING, MOE_RING)]
        moe_mm = sem("moe_mm")
        sil_done, hid_mul, hid_hi, hid_lo, hid_tp, hid_c = (sem(n) for n in ("sil_done", "hid_mul", "hid_hi", "hid_lo", "hid_tp", "hid_c"))
        y_out = sem("y_out")
        y_stored = [sem(f"y_stored{p}") for p in range(2)]
        yg_ld = [sem(f"yg_ld{tb}") for tb in range(TB)]
        end_done = sem("end_done")

        F_P1 = 0
        F_QUERY = F_P1 + 2 * N_P1F
        F_CONV = F_QUERY + 2 * N_QUERY
        F_CO = F_CONV + 2 * N_CONV
        F_QK = F_CO + 2 * N_CO
        F_AO = F_QK + 2 * N_QK
        G_P1, G_WOUT, G_V2, G_WO2 = 0, 3, 5, 7
        UNITS = [(h, qb) for h in range(AH) for qb in range(TB)]

        def used(n):
            for c, k, f in ((C_P1F, N_P1F, F_P1), (C_QUERY, N_QUERY, F_QUERY), (C_CONV, N_CONV, F_CONV), (C_CO, N_CO, F_CO),
                            (C_QK, N_QK, F_QK), (C_AO, N_AO, F_AO)):
                if c <= n < c + k:
                    return ft_done, f + 2 * (n - c) + 2
            if n == C_KEYS:
                return used(n - RING)
            if C_U <= n < C_U + N_U:
                return u_done, 2 + 2 * (n - C_U) + 2
            if C_V <= n < C_V + N_V:
                return v_done, 2 + n - C_V + 1
            for c, k, g in ((C_P1T, N_P1T, G_P1), (C_WOUT, N_WOUT, G_WOUT), (C_V2, N_V2, G_V2), (C_WO2, N_WO2, G_WO2)):
                if c <= n < c + k:
                    at = g + (n - c) // 2 + 1
                    return (tok_done, TB * at) if (n - c) % 2 else (tok_half, at)

        PASS = N_MOE
        moe = lambda r, i, c: r * NE + 2 * i + c
        pairs_of = lambda r, i, c: r * (NE // 2) + i + c // 2

        def wait(eng, semaphore, count):
            if not isinstance(count, int) or count > 0:
                eng.wait_ge(semaphore, count)

        def every_expert(first, step, last):
            def one_pass(eng, r):
                first(r)
                with eng.Fori(0, (NE - 2) // 2) as i:
                    for c in (1, 2):
                        step(r, i, c)
                last(r)
            return one_pass

        def more_passes(eng, one_pass, gather=None):
            eng.wait_ge(rt_dest, 1)
            with eng.If(eng.value_load(n_rows_i[0:1, 0:1], min_val=0, max_val=T) > CAP):
                with eng.Fori(1, PASSES) as r:
                    one_pass(eng, r)
                if gather:
                    gather(PASSES)
            if gather:
                with eng.Else():
                    gather(1)

        block = ctx.enter_context(nc.Block())

        @block.sync
        def _(sp):
            for tb in range(TB):
                sp.dma_start(res[:, tb, :], x_in[tb * P:(tb + 1) * P, :]).then_inc(x_ld[tb], 16)
            sp.dma_start(cols[:, :], cols_in).then_inc(cols_ld, 16)
            for n in range(RING):
                sp.dma_start(w_st[:, n, :], w_all[n]).then_inc(w_ld[n], 16)
            sp.dma_start(small, small_in).then_inc(small_ld, 16)
            with sp.Fori(1, C_MOE // RING) as i:
                for s in range(RING):
                    sp.wait_ge(w_lo_done, i * RING + (s + 1 - RING))
                    sp.dma_start(w_st[:, s, :], w_all[i * RING + s]).then_inc(w_ld[s], 16)

            def one_pass(eng, r):
                for s in range(MOE_RING):
                    if s < RING:
                        sp.wait_ge(w_lo_done, C_MOE + r * PASS + (s + 1 - RING))
                    else:
                        sp.wait_ge(w_lo_done, C_MOE + r * PASS + (s + 1 - MOE_RING))
                        sp.wait_ge(rt_mm, 1)
                    sp.dma_start(moe_st[s], w_all[C_MOE + s]).then_inc(moe_ld[s], 16)
                with sp.Fori(1, PASS // MOE_RING) as i:
                    for s in range(MOE_RING):
                        sp.wait_ge(w_lo_done, C_MOE + r * PASS + i * MOE_RING + (s + 1 - MOE_RING))
                        sp.dma_start(moe_st[s], w_all[C_MOE + i * MOE_RING + s]).then_inc(moe_ld[s], 16)

            one_pass(sp, 0)
            more_passes(sp, one_pass)
            for tb in range(TB):
                sp.wait_ge(end_done, tb + 1)
                sp.dma_start(out[tb * P:(tb + 1) * P, :], xn[:, tb, :]).then_inc(out_st, 16)
            sp.wait_ge(out_st, 16 * TB)

        @block.gpsimd
        def _(pool):
            def load_row(n):
                if n >= 2:
                    pool.wait_ge(row_used, n - 1)
                pool.dma_start(row[:, n % 2, :], rows_in[n].to_broadcast([P, D])).then_inc(row_ld[n % 2], 16)

            load_row(0)
            pool.memset(ident[:, :], 0.0)
            pool.memset(ones[:, :], 1.0)
            pool.memset(eps[:, :], EPS)
            pool.memset(reset[:, :], 1.0)
            pool.memset(neg_gt[:, :], 0.0).then_inc(const_step, 1)
            pool.wait_ge(const_step, 1)
            pool.affine_select(out=ident[:, :], in_=ident[:, :], compare_op=ALU.not_equal, fill=1.0, base=0,
                               pattern=[[-1, P]], channel_multiplier=1)
            pool.affine_select(out=tri_le[:, :], in_=ones[:, :], compare_op=ALU.is_ge, fill=0.0, base=0,
                               pattern=[[1, P]], channel_multiplier=-1)
            pool.affine_select(out=tri_gt[:, :], in_=ones[:, :], compare_op=ALU.is_gt, fill=0.0, base=0,
                               pattern=[[-1, P]], channel_multiplier=1)
            pool.affine_select(out=neg_gt[:, :], in_=neg_gt[:, :], compare_op=ALU.is_ge, fill=NEG, base=0,
                               pattern=[[1, P]], channel_multiplier=-1)
            pool.memset(reset[:, :].rearrange("p (c i) -> p c i", i=GC)[:, :, 0:1], 0.0)
            pool.memset(xbc[:, :, 0:4], 0.0).then_inc(const_step, 1)
            pool.wait_ge(const_step, 2)
            pool.tensor_scalar(tri_neg[:, :], tri_le[:, :], -1.0, None, ALU.mult)
            pool.iota(iota_i[:, :], [[1, P]], base=0, channel_multiplier=0)
            pool.iota(tok_i[:, :], [[P, TB]], base=0, channel_multiplier=1)
            pool.memset(zero_b[:, :], 0.0)
            pool.tensor_copy(neg_gt_b[:, :], neg_gt[:, :])
            pool.tensor_copy(ident_b[:, :], ident[:, :]).then_inc(const_step, 1)
            pool.wait_ge(const_step, 3)
            pool.tensor_copy(iota_f[:, :], iota_i[:, :])
            pool.tensor_copy(tok_f[:, :], tok_i[:, :])
            pool.tensor_copy(iota_b[:, :], iota_i[:, :]).then_inc(const_done, 1)

            for n in range(1, 4):
                load_row(n)
            for r in range(2):
                pool.dma_start(first_st[:, r, 0, :], cols_in[:, 0:4]).then_inc(u_stored[r], 16)
                pool.dma_start(first_st[:, r, 1, :], cols_in[:, 0:4]).then_inc(g_stored[r], 16)
                pool.dma_start(first_st[:, r, 2, :], cols_in[:, 0:4]).then_inc(y_stored[r], 16)

            def store_activations(i, c):
                pool.wait_ge(u_out, 16 * i + 2 * c + 4)
                pool.dma_start(act_dram[i * 8 + c], u_st[:, c % 2, :, :].rearrange("p j t -> p (j t)")).then_inc(u_stored[c % 2], 16)

            with pool.Fori(0, 4) as i:
                for c in range(8):
                    store_activations(i, c)
            with pool.Fori(4, 8) as i:
                for c in range(8):
                    store_activations(i, c)
                    if c % 4 == 3:
                        b = c // 4
                        pool.wait_ge(g_out, 4 + 2 * (16 * (i - 4) + 8 * b + 8))
                        pool.dma_start(gate_dram[(i - 4) * 2 + b], g_st[:, b, :, :]).then_inc(g_stored[b], 16)
            for r in range(2):
                pool.wait_ge(u_stored[r], 16 * (N_U // 2 + 1))
                pool.wait_ge(g_stored[r], 16 * 5)
            with pool.Fori(0, N_V // 4) as i:
                for c in range(4):
                    pool.wait_ge(h_mul, i * 4 + c + 1)
                    pool.dma_start(ga_in[:, c % 2, :, :].rearrange("p j t -> p (j t)"), act_dram[i * 4 + c]).then_inc(ga_ld[c % 2], 16)
                    pairs = gate_dram.rearrange("g p (n j) t -> n p g (j t)", j=2)
                    pool.dma_start(g_in[:, c % 2, :, :, :].rearrange("p g j t -> p g (j t)"), pairs[i * 4 + c]).then_inc(g_ld[c % 2], 16)

            load_row(4)
            for tb in range(TB):
                pool.wait_ge(pk_lo, tb + 1)
                pool.dma_start(x_dram[tb * P:(tb + 1) * P, :], pk[:, tb, :, :].rearrange("p a d -> p (a d)")).then_inc(x_st, 16)
            load_row(5)
            pool.wait_ge(x_st, 16 * TB)

            def gather(p):
                pool.drain()
                pool.indirect_dma_start(x_g[0:CAP, p, :, :].rearrange("p a d -> p (a d)"), None, x_dram,
                                        bass.IndirectOffsetOnAxis(ap=idx[0:CAP, p:p + 1], axis=0)).then_inc(xe_ld[p], 16)

            def gather_next(r, i, c):
                pool.wait_ge(xe_tp, 2 * moe(r, i, c) + 2)
                pool.tensor_copy(idx[0:CAP, c % 2:c % 2 + 1], row_i[0:CAP, bass.ds(2 * i + c, 1)])
                gather(c % 2)

            def store(r, i, c):
                pool.wait_ge(y_out, moe(r, i, c) + 2)
                pool.dma_start(y_dram[moe(r, i, c)], y_st[0:CAP, c % 2, :]).then_inc(y_stored[c % 2], 16)

            pool.wait_ge(x_st, 16 * TB)

            def first(r):
                pool.wait_ge(rt_row, r + 1)
                pool.tensor_tensor(idx[0:CAP, 0:2], row_i[0:CAP, 0:2], zero_b[0:CAP, 0:4].bitcast(I32), ALU.add)
                gather(0)
                gather(1)

            def step(r, i, c):
                gather_next(r, i, c + 1)
                store(r, i, c - 1)

            def last(r):
                store(r, 0, NE - 2)
                store(r, 0, NE - 1)
                for p in range(2):
                    pool.wait_ge(y_stored[p], 16 * (pairs_of(r, 0, NE) + 1))

            one_pass = every_expert(first, step, last)
            one_pass(pool, 0)

            def gather_outputs(passes):
                for tb in range(TB):
                    for s in range(2):
                        pool.indirect_dma_start(y_g[:, tb, s, :], None, y_dram[0:passes * NE].rearrange("q r d -> (q r) d"),
                                                bass.IndirectOffsetOnAxis(ap=to_y[:, s, tb:tb + 1], axis=0)).then_inc(yg_ld[tb], 16)

            more_passes(pool, one_pass, gather_outputs)

        @block.tensor
        def _(pe):
            def chunk(n):
                pe.wait_ge(w_lo_done, n + 1)

            def mm3(dst, l_hi, l_lo, r_hi, r_lo, start, stop):
                pe.matmul(dst, l_hi, r_hi, start=start, stop=False)
                pe.matmul(dst, l_hi, r_lo, start=False, stop=False)
                return pe.matmul(dst, l_lo, r_hi, start=False, stop=stop)

            def feature_tile(f, n, half, r_hi, r_lo, bank=None):
                chunk(n)
                if bank is None and f >= 4:
                    pe.wait_ge(ft_out, f - 3)
                dst = ps[:, 4 + f % 4 if bank is None else bank, :]
                for kt in range(KT):
                    w = slice(half * D + kt * P, half * D + (kt + 1) * P)
                    last = mm3(dst, w_hi[:, n % RING, w], w_lo[:, n % RING, w], r_hi[:, kt, :], r_lo[:, kt, :],
                               kt == 0, kt == KT - 1)
                last.then_inc(ft_done, 1)

            def token_tiles(n, bank, l_hi, l_lo):
                for part in range(2):
                    chunk(n + part)
                    for tb in range(TB):
                        rows = slice(tb * P, (tb + 1) * P)
                        for k in range(4):
                            kt = part * 4 + k
                            w = slice(k * 512, (k + 1) * 512)
                            last = mm3(ps[:, bank + tb, :], l_hi[:, kt, rows], l_lo[:, kt, rows],
                                       w_hi[:, (n + part) % RING, w], w_lo[:, (n + part) % RING, w],
                                       kt == 0, kt == KT - 1)
                        if part == 1:
                            last.then_inc(tok_done, 1)
                        elif tb == TB - 1:
                            last.then_inc(tok_half, 1)

            def transpose_rows(use, by_block=True):
                for n in range(KT):
                    g = KT * use + n
                    if g >= 2:
                        pe.wait_ge(tp_lo, g - 1)
                    for m in range(4):
                        tb, kt = (n // 2, (n % 2) * 4 + m) if by_block else (m, n)
                        if kt == 0:
                            pe.wait_ge(xn_done, TB * use + tb + 1)
                        last = pe.transpose(ps[:, g % 2, m * P:(m + 1) * P], xn[:, tb, kt * P:(kt + 1) * P], ident[:, :])
                    last.then_inc(tp_done, 1)

            pe.wait_ge(const_done, 1)
            transpose_rows(0)
            pe.wait_ge(tp_lo, KT)
            pe.wait_ge(small_done, 1)
            for kt in range(KT):
                w = slice(O_IN + kt * SM_IN, O_IN + (kt + 1) * SM_IN)
                last = mm3(ps[0:SM_IN, 2, :], small_hi[:, w], small_lo[:, w], a_hi[:, kt, :], a_lo[:, kt, :], kt == 0, kt == KT - 1)
            last.then_inc(sm_done, 1)
            for m in range(2 * N_P1F):
                feature_tile(F_P1 + m, C_P1F + m // 2, m % 2, a_hi, a_lo)
                if m == 1:
                    pe.wait_ge(sm_out, 1)
                    for j in range(2):
                        pe.matmul(ps[:, j, :], small[0:GRANK, O_G2 + j * P:O_G2 + (j + 1) * P], sm[0:GRANK, :],
                                  start=True, stop=True).then_inc(gate_mm, 1)
                if m == 4:
                    pe.wait_ge(dt_done, 1)
                    for tb in range(TB):
                        for s in range(2):
                            last = pe.transpose(ps[:, 3, (tb * 2 + s) * SH:(tb * 2 + s + 1) * SH],
                                                dtm[DT0:DT0 + SH, 2 + s, tb * P:(tb + 1) * P], ident[DT0:DT0 + SH, DT0:DT0 + SH])
                    last.then_inc(dta_tp, 1)
                if m == 6:
                    pe.wait_ge(dta_c, 1)
                    for s, tri in enumerate((tri_le, tri_gt, ones)):
                        last = pe.matmul(ps[:, 3, s * TB * SH:(s + 1) * TB * SH].rearrange("p (t h) -> p t h", t=TB), tri[:, :], dta[:, :, 1, :], start=True, stop=True)
                    last.then_inc(cum_mm, 1)
            pe.wait_ge(gate_x, 2)
            pe.wait_ge(cum_exp, 1)
            token_tiles(C_P1T, 0, a_hi, a_lo)
            pe.wait_ge(ft_out, F_P1 + 2 * N_P1F)
            for j in range(2):
                pe.wait_ge(gla_qk, j + 1)
                for tb in range(TB):
                    last = pe.transpose(ps[:, 6 + j, tb * P:(tb + 1) * P], k_end[:, j, tb * P:(tb + 1) * P], ident[:, :])
                last.then_inc(gla_kt, 1)
            for hh in range(2):
                for c in range(NGC):
                    for j in range(2):
                        rows, t0 = slice(hh * GDK, (hh + 1) * GDK), c * GC
                        last = pe.matmul(ps[(c % 2) * GC:(c % 2 + 1) * GC, 4 + hh, ((c // 2) * 2 + j) * GC:((c // 2) * 2 + j + 1) * GC],
                                         qk[rows, 2 + j, t0:t0 + GC], qk[rows, j, t0:t0 + GC], start=True, stop=True)
                last.then_inc(gla_att, 1)
            pe.wait_ge(tok_out, TB)
            token_tiles(C_P1T + 2, 0, a_hi, a_lo)
            pe.wait_ge(gla_ktc, 2)
            pe.wait_ge(gla_attc, 2)
            for j in range(2):
                for c in range(NGC):
                    rows = slice((c % 2) * GC, (c % 2 + 1) * GC)
                    for hh in range(2):
                        h = 2 * j + hh
                        last = pe.matmul(ps[hh * GDK:(hh + 1) * GDK, 4 + j * 2 + c % 2, (c // 2) * GDV:(c // 2 + 1) * GDV],
                                         k_endT[rows, j, c // 2, hh * GDK:(hh + 1) * GDK],
                                         vT[rows, c // 2, h * GDV:(h + 1) * GDV], start=True, stop=True)
                last.then_inc(gla_st, 1)
            pe.wait_ge(tok_out, 2 * TB)
            token_tiles(C_P1T + 4, 0, a_hi, a_lo)
            pe.wait_ge(gla_S, 1)
            pe.wait_ge(tok_out, 3 * TB)
            for tb in range(TB):
                b = (tb % 2) * 3
                if tb >= 2:
                    pe.wait_ge(gla_od, tb - 1)
                for par in range(2):
                    rows, c = slice(par * GC, (par + 1) * GC), 2 * tb + par
                    for h in range(GH):
                        j, hh = h // 2, h % 2
                        pe.matmul(ps[rows, b, h * GDV:(h + 1) * GDV], att_s[rows, hh, 2 * tb + j, :],
                                  vT[rows, tb, h * GDV:(h + 1) * GDV], start=True, stop=True)
                        dk = slice(hh * GDK, (hh + 1) * GDK)
                        last = pe.matmul(ps[rows, b + 1 + hh, j * GDV:(j + 1) * GDV], qk[dk, j, c * GC:(c + 1) * GC],
                                         s_gla[dk, j, c, :], start=True, stop=True)
                last.then_inc(gla_o, 1)

            pe.wait_ge(silu_done, 6)
            for tb in range(TB + 1):
                if tb >= 2:
                    pe.wait_ge(xt_c, tb - 1)
                for m in range(4):
                    src = xc[:, m, tb * P:(tb + 1) * P] if tb < TB else xc[:, 4, m * P:(m + 1) * P]
                    last = pe.transpose(ps[:, 6 + tb % 2, m * P:(m + 1) * P], src, ident[:, :])
                last.then_inc(xt_tp, 1)
            pe.wait_ge(xt_c, TB + 1)
            pe.wait_ge(gla_od, TB)
            for tb in range(TB):
                t0 = slice(tb * P, (tb + 1) * P)
                if tb >= 1:
                    pe.wait_ge(ssd_W, 2 * tb)
                for g in range(SG):
                    for jj in range(SJ):
                        a_col = dta[:, tb, 1, g * SJ + jj:g * SJ + jj + 1].to_broadcast([P, P])
                        dst = ps[:, g, jj * P:(jj + 1) * P]
                        pe.matmul(dst, a_col, tri_le[:, :], start=True, stop=False)
                        pe.matmul(dst, tri_neg[:, :], a_col, start=False, stop=False)
                        pe.matmul(dst, ident_b[:, :], neg_gt_b[:, :], start=False, stop=True)
                    n = slice(g * SN, (g + 1) * SN)
                    pe.matmul(ps[:, 2 + g, 0:P], xc[n, 4, t0], xc[n, 5, t0], start=True, stop=True).then_inc(ssd_mm, 1)
                pe.wait_ge(xd_done, tb + 1)
                if tb >= 1:
                    pe.wait_ge(ssd_S, tb)
                for g in range(SG):
                    last = pe.matmul(ps[g * SN:(g + 1) * SN, 6, 0:SJ * SP_], bt[:, tb, g * SN:(g + 1) * SN],
                                     xdte[:, tb, g * SJ * SP_:(g + 1) * SJ * SP_], start=True, stop=True)
                last.then_inc(ssd_st, 1)
                if tb == 0:
                    pe.wait_ge(ssd_S, 1)
                else:
                    pe.wait_ge(ssd_yd, tb)
                for g in range(SG):
                    n = slice(g * SN, (g + 1) * SN)
                    pe.matmul(ps[:, 7 - 3 * g, 0:SJ * SP_], xc[n, 5, t0], s_ssd[n, tb, :], start=True, stop=True)
                pe.wait_ge(ssd_W, 2 * tb + 2)
                for h in range(SH):
                    last = pe.matmul(ps[:, 5, h * SP_:(h + 1) * SP_], w_s[:, h // SJ, (h % SJ) * P:(h % SJ + 1) * P],
                                     xdt[:, tb, h * SP_:(h + 1) * SP_], start=True, stop=True)
                last.then_inc(ssd_y, 1)

            pe.wait_ge(ssd_yd, TB)
            transpose_rows(1, by_block=False)
            pe.wait_ge(tp_lo, 2 * KT)
            token_tiles(C_WOUT, 4, a_hi, a_lo)
            token_tiles(C_WOUT + 2, 0, a_hi, a_lo)

            transpose_rows(2)
            pe.wait_ge(tp_lo, 3 * KT)
            for m in range(2 * N_QUERY):
                feature_tile(F_QUERY + m, C_QUERY + m // 2, m % 2, a_hi, a_lo)

            def expert_tile(i, c, t):
                n = C_U + 8 * i + c
                if t == 0:
                    chunk(n)
                pe.wait_ge(u_out, 16 * i + 2 * c + t + 1)
                for kt in range(KT):
                    w = slice(t * D + kt * P, t * D + (kt + 1) * P)
                    last = mm3(ps[:, t, :], w_hi[:, c % RING, w], w_lo[:, c % RING, w], a_hi[:, kt, :], a_lo[:, kt, :],
                               kt == 0, kt == KT - 1)
                last.then_inc(u_done, 1)

            pe.wait_ge(ft_out, F_QUERY + 2 * N_QUERY)
            pe.drain().then_inc(u_done, 2)
            with pe.Fori(0, 4) as i:
                for c in range(8):
                    pe.wait_ge(s_out, 8 * i + c + 1)
                    for half in range(2):
                        q = 2 * c + half
                        rows = bass.ts(i, P)
                        last = mm3(ps[:, 2 + c % 2, half * PK:(half + 1) * PK], q_hi[:, q, rows], q_lo[:, q, rows],
                                   keys_hi[:, q, :], keys_lo[:, q, :], True, True)
                    last.then_inc(s_done, 1)
                    for t in range(2):
                        expert_tile(i, c, t)
            pe.wait_ge(soft_done, 1)
            for a, src in enumerate((key1, key2, score)):
                for tb in range(TB):
                    last = pe.transpose(ps[:, 4 + a, tb * P:(tb + 1) * P], src[:, tb * P:(tb + 1) * P], ident[:, :])
            last.then_inc(slot_tp, 1)
            pe.wait_ge(slot_done, 1)
            pe.drain().then_inc(g_done, 4)
            with pe.Fori(4, 8) as i:
                for c in range(8):
                    for t in range(2):
                        expert_tile(i, c, t)
                        at = 2 * c + t
                        pe.wait_ge(oh_done, 16 * (i - 4) + at + 1)
                        pe.wait_ge(g_out, 2 * (16 * (i - 4) + at) + 2)
                        for r in range(8):
                            dst = ps[:, 2 + 2 * (at % 2) + r // 4, (r % 4) * PK:(r % 4 + 1) * PK]
                            pe.matmul(dst, oh_b[:, at % 2, r, :], oh_a[:, at % 2, r, 0, :], start=True, stop=False)
                            last = pe.matmul(dst, oh_b[:, at % 2, r, :], oh_a[:, at % 2, r, 1, :], start=False, stop=True)
                            if r % 4 == 3:
                                last.then_inc(g_done, 1)
            pe.wait_ge(u_out, 2 + 2 * N_U)
            pe.wait_ge(g_out, 4 + 2 * 64)
            for b in range(8):
                pe.matmul(ps[:, b, :], zero_b[:, 0:P], zero_b[:, :], start=True, stop=False)
            pe.drain().then_inc(v_done, 2)
            with pe.Fori(0, N_V // 4) as i:
                for c in range(4):
                    chunk(C_V + 4 * i + c)
                    pe.wait_ge(h_lo_done, 4 * i + c + 1)
                    for j in range(2):
                        for tb in range(TB):
                            rows = slice(tb * P, (tb + 1) * P)
                            for part in range(2):
                                w = slice(j * D + part * 512, j * D + (part + 1) * 512)
                                last = mm3(ps[:, 2 * tb + part, :], h_hi[:, c % 2, j, rows], h_lo[:, c % 2, j, rows],
                                           w_hi[:, c, w], w_lo[:, c, w], False, False)
                    last.then_inc(v_done, 1)
            for b in range(8):
                pe.matmul(ps[:, b, :], zero_b[:, 0:P], zero_b[:, :], start=False, stop=True).then_inc(peer_done, 1)

            transpose_rows(3)
            pe.wait_ge(tp_lo, 4 * KT)
            for kt in range(KT):
                w = slice(O_F + kt * SM_F, O_F + (kt + 1) * SM_F)
                last = mm3(ps[0:SM_F, 2, :], small_hi[:, w], small_lo[:, w], a_hi[:, kt, :], a_lo[:, kt, :], kt == 0, kt == KT - 1)
            last.then_inc(f_mm, 1)
            for m in range(2 * N_CONV):
                feature_tile(F_CONV + m, C_CONV + m // 2, m % 2, a_hi, a_lo)
            pe.wait_ge(cv_lo, KT)
            pe.wait_ge(ft_out, F_CONV + 2 * N_CONV)
            for j in range(KT):
                if j >= 2:
                    pe.wait_ge(m1_done, j - 1)
                feature_tile(F_CO + 2 * j, C_CO + j, 0, a_hi, a_lo, bank=4 + 2 * (j % 2))
                feature_tile(F_CO + 2 * j + 1, C_CO + j, 1, c_hi, c_lo, bank=5 + 2 * (j % 2))
            token_tiles(C_V2, 0, a_hi, a_lo)
            pe.wait_ge(m1_done, KT)
            token_tiles(C_V2 + 2, 4, a_hi, a_lo)

            def project_heads(j):
                if j:
                    pe.wait_ge(qk_out, 2 * j)
                feature_tile(F_QK + 2 * j, C_QK + j, 0, a_hi, a_lo, bank=6)
                feature_tile(F_QK + 2 * j + 1, C_QK + j, 1, a_hi, a_lo, bank=7)

            pe.wait_ge(tok_out, TB * (G_V2 - 2 + 2))
            pe.wait_ge(f_cum, 1)
            project_heads(0)
            for u in range(len(UNITS) + 2):
                if u < len(UNITS):
                    h, qb = UNITS[u]
                    j, hh, n = h // 2, h % 2, (qb + 1) * P
                    if (hh, qb) == (0, 0):
                        pe.wait_ge(qk_out, 2 * j + 2)
                    if u >= 2:
                        pe.wait_ge(at_p, u - 1)
                    dst = ps[:, u % 2, 0:n]
                    pe.matmul(dst, q_z[:, j % 2, hh, qb * P:n], k_s[:, j % 2, 0:n], start=True, stop=False)
                    pe.matmul(dst, head_b[:, h:h + 1].to_broadcast([P, P]), cum_b[:, 0:n], start=False, stop=False)
                    pe.matmul(ps[:, u % 2, qb * P:n], neg_gt_b[:, :], ident_b[:, :], start=False, stop=True).then_inc(at_s, 1)
                    if (hh, qb) == (0, 2) and j + 1 < AH // 2:
                        project_heads(j + 1)
                if 1 <= u <= len(UNITS):
                    v = u - 1
                    pe.wait_ge(at_p, v + 1)
                    if v >= 2:
                        pe.wait_ge(at_tc, v - 1)
                    for kb in range(UNITS[v][1] + 1):
                        last = pe.transpose(ps[:, 2 + v % 2, kb * P:(kb + 1) * P], p_s[:, v % 2, kb * P:(kb + 1) * P], ident[:, :])
                    last.then_inc(at_t, 1)
                if u >= 2:
                    v = u - 2
                    h, qb = UNITS[v]
                    pe.wait_ge(at_tc, v + 1)
                    if v >= 2:
                        pe.wait_ge(at_out, v - 1)
                    for kb in range(qb + 1):
                        last = pe.matmul(ps[:, 4 + v % 2, 0:ADH], pT_s[:, v % 2, kb, :], v_s[:, kb, h * ADH:(h + 1) * ADH],
                                         start=kb == 0, stop=kb == qb)
                    last.then_inc(at_o, 1)
            transpose_rows(4)
            pe.wait_ge(tp_lo, 5 * KT)
            pe.wait_ge(at_out, len(UNITS))
            for j in range(KT):
                if j >= 2:
                    pe.wait_ge(mix_done, j - 1)
                feature_tile(F_AO + 2 * j, C_AO + j, 0, a_hi, a_lo, bank=4 + 2 * (j % 2))
                feature_tile(F_AO + 2 * j + 1, C_AO + j, 1, c_hi, c_lo, bank=5 + 2 * (j % 2))
            pe.wait_ge(mix_lo, KT)
            token_tiles(C_WO2, 0, m_split[:, :, 0, :], m_split[:, :, 1, :])
            token_tiles(C_WO2 + 2, 4, m_split[:, :, 0, :], m_split[:, :, 1, :])

            transpose_rows(5)
            pe.wait_ge(tp_lo, 6 * KT)
            for tb in range(TB):
                for kt in range(KT):
                    rows, w = slice(tb * P, (tb + 1) * P), slice(O_R + kt * SM_R, O_R + (kt + 1) * SM_R)
                    last = mm3(ps[:, 2, tb * SM_R:(tb + 1) * SM_R], a_hi[:, kt, rows], a_lo[:, kt, rows], small_hi[:, w], small_lo[:, w],
                               kt == 0, kt == KT - 1)
            last.then_inc(rt_mm, 1)
            pe.wait_ge(rt_pick, 1)
            pe.matmul(ps[:, 3, 0:TB * NE].rearrange("p (t e) -> p t e", e=NE), tri_le[:, :], e_any, start=True, stop=False)
            for b in range(TB - 1):
                last = pe.matmul(ps[:, 3, (b + 1) * NE:TB * NE].rearrange("p (t e) -> p t e", e=NE), ones[:, :],
                                 e_any[:, b, :].unsqueeze(1).to_broadcast([P, TB - 1 - b, NE]), start=False, stop=b == TB - 2)
            last.then_inc(rt_rank, 1)
            for b in range(TB):
                last = pe.matmul(ps[:, 4, 0:NE], ones[:, :], e_any[:, b, :], start=b == 0, stop=b == TB - 1)
            last.then_inc(rt_all, 1)
            pe.drain().then_inc(xe_tp, 4)
            pe.drain().then_inc(moe_mm, RING)

            def expert_rows(r, i, c):
                pe.wait_ge(xe_ld[c % 2], 16 * (pairs_of(r, i, c) + 1))
                wait(pe, xe_hi, moe(r, i, c))
                wait(pe, xe_lo, moe(r, i, c))
                for a in range(2):
                    for kt in range(KT):
                        last = pe.matmul(ps[:, 6 + a, kt * CAP:(kt + 1) * CAP], x_g[0:CAP, c % 2, a, kt * P:(kt + 1) * P],
                                         ident_b[0:CAP, 0:CAP], start=True, stop=True)
                    last.then_inc(xe_tp, 1)

            def expert_in(r, i, c, k, bank):
                for part in range(2):
                    chunk(C_MOE + r * PASS + 12 * i + (k + part))
                    for j in range(4):
                        kt, w = part * 4 + j, slice(j * DE, (j + 1) * DE)
                        last = mm3(ps[0:CAP, bank, :], xeT[:, c % 2, 0, kt, :], xeT[:, c % 2, 1, kt, :],
                                   w_hi[:, (k + part) % RING, w], w_lo[:, (k + part) % RING, w], kt == 0, kt == KT - 1)
                    last.then_inc(moe_mm, 1)

            def expert_gate(r, i, c):
                wait(pe, sil_done, moe(r, i, c))
                pe.wait_ge(xe_hi, moe(r, i, c) + 1)
                pe.wait_ge(xe_lo, moe(r, i, c) + 1)
                expert_in(r, i, c, 6 * c - 2 if c else 0, 0)

            def expert_up(r, i, c):
                wait(pe, hid_mul, moe(r, i, c))
                expert_in(r, i, c, 6 * c + 2, 1)

            def expert_hidden(r, i, c):
                pe.wait_ge(hid_lo, moe(r, i, c) + 1)
                for a in range(2):
                    for f in range(DE // P):
                        n = a * (DE // P) + f
                        last = pe.matmul(ps[:, 4, n * CAP:(n + 1) * CAP], hid_b[0:CAP, a, f * P:(f + 1) * P], ident_b[0:CAP, 0:CAP],
                                         start=True, stop=True)
                last.then_inc(hid_tp, 1)

            def expert_down(r, i, c, k):
                pe.wait_ge(hid_c, moe(r, i, c) + 1)
                pe.wait_ge(y_out, moe(r, i, c) + 1)
                for part in range(2):
                    chunk(C_MOE + r * PASS + 12 * i + (k + part))
                    for half in range(2):
                        for j in range(2):
                            f, w = part * 2 + j, slice(j * D + half * 512, j * D + (half + 1) * 512)
                            last = mm3(ps[0:CAP, 2 + half, :], hidT[:, 0, f, :], hidT[:, 1, f, :],
                                       w_hi[:, (k + part) % RING, w], w_lo[:, (k + part) % RING, w], f == 0, f == DE // P - 1)
                    last.then_inc(moe_mm, 1)

            def first(r):
                pe.wait_ge(rt_tok, r + 1)
                for n in range(2 * TB):
                    last = pe.matmul(ps[0:CAP, 5, 0:NE], row_one[:, n // TB, n % TB, :], tok_e[:, n // TB, n % TB, :], start=n == 0, stop=n == 2 * TB - 1)
                last.then_inc(rt_sum, 1)
                expert_rows(r, 0, 0)
                expert_rows(r, 0, 1)
                expert_gate(r, 0, 0)
                expert_up(r, 0, 0)

            def step(r, i, c, more=True):
                expert_gate(r, i, c)
                expert_hidden(r, i, c - 1)
                if more:
                    expert_rows(r, i, c + 1)
                expert_down(r, i, c - 1, 6 * c)
                expert_up(r, i, c)

            def last(r):
                step(r, 0, NE - 1, more=False)
                expert_hidden(r, 0, NE - 1)
                expert_down(r, 0, NE - 1, 6 * NE - 2)

            one_pass = every_expert(first, step, last)
            one_pass(pe, 0)
            more_passes(pe, one_pass)

        @block.scalar
        def _(act):
            split = [0]

            def hi(n, dst=None):
                act.wait_ge(w_ld[n % RING], 16 * (n // RING + 1))
                if n >= RING:
                    act.wait_ge(*used(n - RING))
                dst = w_hi[:, n % RING, :] if n != C_KEYS else keys_hi.rearrange("p q k -> p (q k)")
                act.activation(dst, w_st[:, n % RING, :], ACT.Copy).then_inc(w_hi_done, 1)

            def ahead(n):
                while split[0] <= min(n + AHEAD, C_MOE - 1):
                    hi(split[0])
                    split[0] += 1

            def norm(use, tb, ready, count):
                act.wait_ge(ready, count)
                act.activation(xn[:, tb, :], res[:, tb, :], ACT.Square, accum_out=ss[:, tb:tb + 1])
                act.drain()
                act.activation(sd[:, tb:tb + 1], ss[:, tb:tb + 1], ACT.Sqrt, scale=1.0 / D, bias=eps[:, :]).then_inc(sd_done, 1)

            def transposed(use, weight=None, dst=a_hi):
                for n in range(KT):
                    act.wait_ge(tp_done, KT * use + n + 1)
                    if weight is None:
                        act.activation(dst[:, (n % 2) * 4:(n % 2) * 4 + 4, (n // 2) * P:(n // 2 + 1) * P],
                                       ps[:, n % 2, :].rearrange("p (k t) -> p k t", k=4), ACT.Copy).then_inc(tp_hi, 1)
                    else:
                        act.activation(dst[:, n, :], ps[:, n % 2, :], ACT.Copy, scale=weight(n)).then_inc(tp_hi, 1)

            act.wait_ge(const_done, 1)
            for tb in range(TB):
                norm(0, tb, x_ld[tb], 16)
            ahead(-AHEAD)
            transposed(0)
            ahead(-1)
            act.wait_ge(small_ld, 16)
            act.activation(small_hi[:, :], small[:, 0:N_SPLIT], ACT.Copy).then_inc(small_hi_done, 1)
            act.wait_ge(cols_ld, 16)
            act.wait_ge(sm_done, 1)
            act.activation(sm[0:SM_IN, :], ps[0:SM_IN, 2, :], ACT.Copy).then_inc(sm_out, 1)
            d = slice(DT0, DT0 + SH)
            for m in range(2 * N_P1F):
                ahead(C_P1F + m // 2)
                act.wait_ge(ft_done, F_P1 + m + 1)
                bank = ps[:, 4 + (F_P1 + m) % 4, :]
                if m < 4:
                    act.activation(qk[:, m, :], bank, ACT.Copy, scale=GDK ** -0.5 if m < 2 else 1.0).then_inc(ft_out, 1)
                else:
                    act.activation(xbc[:, m - 4, 4:], bank, ACT.Copy).then_inc(ft_out, 1)
                if m == 2:
                    act.wait_ge(dt_x, 1)
                    act.activation(dtm[d, 1, :], dtm[d, 0, :], ACT.Abs)
                    act.wait_ge(gate_x, 2)
                    for j in range(2):
                        act.activation(e_pos[:, j, :], g_cum[:, j, :], ACT.Abs)
                    act.activation(ea[d, 0:1], col("a_log")[d, :], ACT.Exp)
                    act.drain()
                    act.activation(dtm[d, 1, :], dtm[d, 1, :], ACT.Exp, scale=-1.0)
                    for j in range(2):
                        act.activation(e_pos[:, j, :], e_pos[:, j, :], ACT.Exp, scale=-1.0)
                    act.drain()
                    act.activation(dtm[d, 1, :], dtm[d, 1, :], ACT.Ln, bias=ones[d, 0:1]).then_inc(dt_ln, 1)
                    for j in range(2):
                        act.activation(e_pos[:, j, :], e_pos[:, j, :], ACT.Ln, bias=ones[:, 0:1]).then_inc(gate_ln, 1)
                if m == 5:
                    act.wait_ge(dta_tp, 1)
                    act.activation(dta.rearrange("p t s h -> p (t s h)"), ps[:, 3, 0:TB * 2 * SH], ACT.Copy).then_inc(dta_c, 1)
                if m == 7:
                    act.wait_ge(cum_mm, 1)
                    act.activation(ecum.rearrange("p s t h -> p (s t h)"), ps[:, 3, 0:3 * TB * SH], ACT.Exp).then_inc(cum_exp, 1)
                    for j in range(2):
                        act.wait_ge(gate_cum, j + 1)
                        act.activation(e_pos[:, j, :], g_cum[:, j, :], ACT.Exp)
                        act.activation(e_neg[:, j, :], g_cum[:, j, :], ACT.Exp, scale=-1.0)
                        act.activation(lg[:, j, :], lg[:, j, :], ACT.Exp).then_inc(gate_exp, 1)
            for g in range(3):
                ahead(C_P1T + 2 * g)
                if g == 1:
                    for j in range(2):
                        act.wait_ge(gla_kt, j + 1)
                        act.activation(k_endT[:, j, :, :].rearrange("p t d -> p (t d)"), ps[:, 6 + j, :], ACT.Copy).then_inc(gla_ktc, 1)
                    for m in range(6):
                        act.wait_ge(conv_done, m + 1)
                        act.activation(xc[:, m, :], xc[:, m, :], ACT.Silu).then_inc(silu_done, 1)
                act.wait_ge(tok_half, G_P1 + g + 1)
                ahead(C_P1T + 2 * g + 1)
                for tb in range(TB):
                    act.wait_ge(tok_done, TB * (G_P1 + g) + tb + 1)
                    if g == 0:
                        act.activation(vT[:, tb, :], ps[:, tb, :], ACT.Copy).then_inc(tok_out, 1)
                    else:
                        act.activation(xn[:, tb, (g - 1) * 512:g * 512], ps[:, tb, :], ACT.Silu).then_inc(tok_out, 1)
            for tb in range(TB):
                act.wait_ge(gla_o, tb + 1)
                if tb >= 2:
                    act.wait_ge(gla_y, tb - 1)
                act.activation(o_s[:, tb % 2, :], ps[:, (tb % 2) * 3, :], ACT.Copy).then_inc(gla_oc, 1)
                act.wait_ge(gla_od, tb + 1)
                for h in range(GH):
                    act.activation(y_t[:, 0, h * GDV:(h + 1) * GDV], o_s[:, tb % 2, h * GDV:(h + 1) * GDV], ACT.Square, accum_out=ss[:, h:h + 1])
                act.drain()
                act.activation(sd[:, 0:GH], ss[:, 0:GH], ACT.Sqrt, scale=1.0 / GDV, bias=eps[:, :]).then_inc(gla_sd, 1)
            for tb in range(TB + 1):
                act.wait_ge(xt_tp, tb + 1)
                dst = xt[:, tb, :] if tb < TB else bt.rearrange("p t n -> p (t n)")
                act.activation(dst, ps[:, 6 + tb % 2, :], ACT.Copy).then_inc(xt_c, 1)
            for tb in range(TB):
                for g in range(SG):
                    act.wait_ge(ssd_mm, 2 * tb + g + 1)
                    if tb >= 1:
                        act.wait_ge(ssd_W, 2 * (tb - 1) + g + 1)
                    act.activation(l_s[:, g, :], ps[:, g, :], ACT.Exp).then_inc(ssd_L, 1)
                act.wait_ge(ssd_yc, tb + 1)
                for g in range(SG):
                    gs = slice(GW + g * SJ * SP_, GW + (g + 1) * SJ * SP_)
                    act.activation(o_s[:, g, 0:SJ * SP_], xn[:, tb, gs], ACT.Square, accum_out=ss[:, tb * SG + g:tb * SG + g + 1])
                act.drain()
            act.activation(sd[:, 0:TB * SG], ss[:, 0:TB * SG], ACT.Sqrt, scale=1.0 / (SJ * SP_), bias=eps[:, :]).then_inc(ssd_sd, 1)
            transposed(1, lambda kt: col("gla_norm") if kt < 4 else col("ssd_norm", kt - 4))
            for g in range(2):
                ahead(C_WOUT + 2 * g)
                act.wait_ge(tok_half, G_WOUT + g + 1)
                ahead(C_WOUT + 2 * g + 1)

            for tb in range(TB):
                norm(1, tb, res_done, tb + 1)
            transposed(2)
            for m in range(2 * N_QUERY):
                ahead(C_QUERY + m // 2)
                act.wait_ge(ft_done, F_QUERY + m + 1)
                act.activation(q_hi[:, m, :], ps[:, 4 + (F_QUERY + m) % 4, :], ACT.Copy).then_inc(q_hi_done, 1)
            ahead(C_KEYS)
            act.drain().then_inc(u_out, 2)

            def hi_in_loop(c, arrived, done, count):
                s = (c + AHEAD) % RING
                act.wait_ge(w_ld[s], arrived)
                act.wait_ge(done, count)
                act.activation(w_hi[:, s, :], w_st[:, s, :], ACT.Copy).then_inc(w_hi_done, 1)

            def gelu_tile(i, c, t):
                if t == 0:
                    act.wait_ge(u_stored[c % 2], 16 * (4 * i + c // 2 + 1))
                act.wait_ge(u_done, 16 * i + 2 * c + t + 3)
                act.activation(u_st[:, c % 2, t, :], ps[:, t, :], ACT.Gelu).then_inc(u_out, 1)

            with act.Fori(0, 4) as i:
                for c in range(8):
                    hi_in_loop(c, 16 * (C_U // RING + 2 * i + (c + AHEAD) // RING + 1), u_done, 16 * i + 2 * c + 2)
                    for t in range(2):
                        gelu_tile(i, c, t)
            act.wait_ge(soft_x, 1)
            act.activation(gate_t, gate_t, ACT.Exp).then_inc(soft_e, 1)
            act.drain().then_inc(g_out, 4)
            with act.Fori(4, 8) as i:
                for c in range(8):
                    hi_in_loop(c, 16 * (C_U // RING + 2 * i + (c + AHEAD) // RING + 1), u_done, 16 * i + 2 * c + 2)
                    for t in range(2):
                        gelu_tile(i, c, t)
                        at = 2 * c + t
                        b, first = at // 8, (at % 8) * 8
                        if at % 8 == 0:
                            act.wait_ge(g_stored[b], 16 * (i - 3))
                        for bank in range(2):
                            act.wait_ge(g_done, 2 * (16 * (i - 4) + at) + bank + 5)
                            tok = slice(first + bank * 4, first + bank * 4 + 4)
                            act.activation(g_st[:, b, :, tok].rearrange("p k t -> p t k"),
                                           ps[:, 2 + 2 * (at % 2) + bank, :].rearrange("p (t k) -> p t k", t=4), ACT.Copy).then_inc(g_out, 1)
            with act.Fori(0, N_V // 4) as i:
                for c in range(4):
                    act.wait_ge(h_mul, 4 * i + c + 3)
                    act.wait_ge(v_done, 4 * i + c + 1)
                    act.activation(h_hi[:, c % 2, :, :], h_f[:, c % 2, :, :], ACT.Copy).then_inc(h_hi_done, 1)
                    hi_in_loop(c, 16 * (C_V // RING + i + (c + AHEAD) // RING + 1), v_done, 4 * i + c + 2)
            split[0] = C_CONV + AHEAD

            for t in range(TB + 1):
                if t < TB:
                    norm(2, t, res_done, TB + t + 1)
                if t >= 1:
                    norm(3, t - 1, res2_done, t)
            transposed(3)
            act.wait_ge(f_xs, 1)
            act.activation(f_e[0:AH, :], f_x[0:AH, :], ACT.Abs)
            act.drain()
            act.activation(f_e[0:AH, :], f_e[0:AH, :], ACT.Exp, scale=-1.0)
            act.drain()
            act.activation(f_e[0:AH, :], f_e[0:AH, :], ACT.Ln, bias=ones[0:AH, 0:1]).then_inc(f_ln, 1)

            def conv_hi(j):
                act.wait_ge(cv_mul, j + 1)
                act.activation(c_hi[:, j, :], cv_s[:, j % 2, :], ACT.Copy).then_inc(cv_hi, 1)

            for j in range(KT):
                for a, dst in enumerate((cu_s, cc_s, cb_s)):
                    m = 3 * j + a
                    ahead(C_CONV + m // 2)
                    act.wait_ge(ft_done, F_CONV + m + 1)
                    if j >= 2:
                        act.wait_ge(cv_mul, j - 1)
                    act.activation(dst[:, j % 2, :], ps[:, 4 + (F_CONV + m) % 4, :], ACT.Copy).then_inc(ft_out, 1)
                if j:
                    conv_hi(j - 1)
            conv_hi(KT - 1)
            for j in range(KT):
                ahead(C_CO + j)
                act.wait_ge(ft_done, F_CO + 2 * j + 1)
                if j >= 2:
                    act.wait_ge(m1_done, j - 1)
                act.activation(sg_s[:, j % 2, :], ps[:, 4 + 2 * (j % 2), :], ACT.Sigmoid).then_inc(sg_done, 1)
            for g in range(2):
                ahead(C_V2 + 2 * g)
                act.wait_ge(tok_half, G_V2 + g + 1)
                ahead(C_V2 + 2 * g + 1)
                for tb in range(TB):
                    act.wait_ge(tok_done, TB * (G_V2 + g) + tb + 1)
                    act.activation(v_s[:, tb, g * 512:(g + 1) * 512], ps[:, 4 * g + tb, :], ACT.Copy).then_inc(tok_out, 1)

            def copy_heads(j):
                ahead(C_QK + j)
                act.wait_ge(ft_done, F_QK + 2 * j + 1)
                if j >= 2:
                    act.wait_ge(at_s, 8 * (j - 1))
                for hh in range(2):
                    rows = slice(hh * ADH, (hh + 1) * ADH)
                    last = act.activation(q_z[rows, j % 2, hh, :], ps[rows, 6, :], ACT.Copy, scale=ADH ** -0.5)
                last.then_inc(qk_out, 1)
                act.wait_ge(ft_done, F_QK + 2 * j + 2)
                act.activation(k_s[:, j % 2, :], ps[:, 7, :], ACT.Copy).then_inc(qk_out, 1)

            act.wait_ge(qz_zero, 1)
            act.wait_ge(f_cum, 1)
            copy_heads(0)
            for u, (h, qb) in enumerate(UNITS):
                n = (qb + 1) * P
                act.wait_ge(at_max, u + 1)
                if u >= 2:
                    act.wait_ge(at_t, u - 1)
                if u >= 4:
                    act.wait_ge(at_out, u - 3)
                act.activation(p_s[:, u % 2, 0:n], ps[:, u % 2, 0:n], ACT.Exp, bias=n_max[:, u % 2:u % 2 + 1],
                               accum_out=r_sum[:, u % 4:u % 4 + 1]).then_inc(at_p, 1)
                if h % 2 == 0 and qb == 3 and h // 2 + 1 < AH // 2:
                    copy_heads(h // 2 + 1)
            transposed(4, dst=c_hi)

            def mix_high(j):
                act.wait_ge(mix_done, j + 1)
                act.activation(m_split[:, j, 0, :], mix_s[:, j % 2, :], ACT.Copy).then_inc(mix_hi, 1)

            for j in range(KT):
                ahead(C_AO + j)
                act.wait_ge(ft_done, F_AO + 2 * j + 1)
                if j >= 2:
                    act.wait_ge(mix_done, j - 1)
                act.activation(sg_s[:, j % 2, :], ps[:, 4 + 2 * (j % 2), :], ACT.Sigmoid).then_inc(sg_done, 1)
                if j:
                    mix_high(j - 1)
            mix_high(KT - 1)
            for g in range(2):
                ahead(C_WO2 + 2 * g)
                act.wait_ge(tok_half, G_WO2 + g + 1)
                ahead(C_WO2 + 2 * g + 1)

            for tb in range(TB):
                norm(4, tb, res_done, 2 * TB + tb + 1)
            transposed(5)
            for tb in range(TB):
                act.activation(pk[:, tb, 0, :], xn[:, tb, :], ACT.Copy).then_inc(pk_hi, 1)
            act.wait_ge(rt_x, 1)
            act.activation(r_exp, r_exp, ACT.Exp).then_inc(rt_e, 1)
            act.drain().then_inc(y_out, 1)

            def hi_of(r, i, k):
                s = k % RING
                before = C_MOE // RING if k % MOE_RING < RING else 0
                act.wait_ge(moe_ld[k % MOE_RING], 16 * (r * (PASS // MOE_RING) + 2 * i + (before + k // MOE_RING + 1)))
                act.wait_ge(moe_mm, r * PASS + 12 * i + (k + 1))
                act.activation(w_hi[:, s, :], moe_st[k % MOE_RING], ACT.Copy).then_inc(w_hi_done, 1)

            def rows_hi(r, i, c):
                act.wait_ge(xe_tp, 2 * moe(r, i, c) + 5)
                act.activation(xeT[:, c % 2, 0, :, :].rearrange("p k t -> p (k t)"), ps[:, 6, 0:KT * CAP], ACT.Copy).then_inc(xe_hi, 1)

            def silu(r, i, c, k):
                wait(act, hid_mul, moe(r, i, c))
                act.wait_ge(moe_mm, r * PASS + 12 * i + (k + 2 + RING))
                act.activation(sil[0:CAP, :], ps[0:CAP, 0, :], ACT.Silu).then_inc(sil_done, 1)

            def hidden_hi(r, i, c):
                act.wait_ge(hid_mul, moe(r, i, c) + 1)
                act.activation(hid_b[0:CAP, 0, :], hid_f[0:CAP, :], ACT.Copy).then_inc(hid_hi, 1)

            def hidden_copy(r, i, c):
                act.wait_ge(hid_tp, moe(r, i, c) + 1)
                act.activation(hidT.rearrange("p a f t -> p (a f t)"), ps[:, 4, 0:2 * DE // P * CAP], ACT.Copy).then_inc(hid_c, 1)

            def outputs(r, i, c, k):
                act.wait_ge(moe_mm, r * PASS + 12 * i + (k + 2 + RING))
                act.wait_ge(y_stored[c % 2], 16 * (pairs_of(r, i, c) + 1))
                act.activation(y_st[0:CAP, c % 2, :].rearrange("p (b n) -> p b n", b=2), ps[0:CAP, 2:4, :], ACT.Copy).then_inc(y_out, 1)

            def first(r):
                for k in range(AHEAD):
                    hi_of(r, 0, k)
                rows_hi(r, 0, 0)
                rows_hi(r, 0, 1)
                hi_of(r, 0, 3)
                hi_of(r, 0, 4)
                silu(r, 0, 0, 0)
                hi_of(r, 0, 5)
                hi_of(r, 0, 6)

            def step(r, i, c, more=True):
                k = 6 * c - 2
                hidden_hi(r, i, c - 1)
                hi_of(r, i, k + 3)
                hi_of(r, i, k + 4)
                silu(r, i, c, k)
                hidden_copy(r, i, c - 1)
                if more:
                    rows_hi(r, i, c + 1)
                hi_of(r, i, k + 5)
                hi_of(r, i, k + 6)
                outputs(r, i, c - 1, k + 2)
                hi_of(r, i, k + 7)
                if more:
                    hi_of(r, i, k + 8)

            def last(r):
                step(r, 0, NE - 1, more=False)
                hidden_hi(r, 0, NE - 1)
                hidden_copy(r, 0, NE - 1)
                outputs(r, 0, NE - 1, PASS - 2)

            one_pass = every_expert(first, step, last)
            one_pass(act, 0)
            more_passes(act, one_pass)
            for tb in range(TB):
                norm(5, tb, res_done, 3 * TB + tb + 1)

        @block.vector
        def _(dve):
            split = [0]

            def lo(n):
                dve.wait_ge(w_hi_done, n + 1)
                lo_n, hi_n = w_lo[:, n % RING, :], w_hi[:, n % RING, :]
                if n == C_KEYS:
                    lo_n, hi_n = (v.rearrange("p q k -> p (q k)") for v in (keys_lo, keys_hi))
                dve.tensor_tensor(lo_n, w_st[:, n % RING, :], hi_n, ALU.subtract).then_inc(w_lo_done, 1)

            def ahead(n):
                while split[0] <= min(n + AHEAD, C_MOE - 1):
                    lo(split[0])
                    split[0] += 1

            def normalise(use, tb, dst=xn, done=xn_done):
                dve.wait_ge(sd_done, TB * use + tb + 1)
                dve.reciprocal(rstd[:, tb:tb + 1], sd[:, tb:tb + 1])
                dve.drain()
                if tb == 0:
                    dve.wait_ge(row_ld[use % 2], 16 * (use // 2 + 1))
                dve.scalar_tensor_tensor(dst[:, tb, :], res[:, tb, :], rstd[:, tb:tb + 1], row[:, use % 2, :], ALU.mult, ALU.mult).then_inc(done, 1)
                if tb == TB - 1:
                    dve.drain().then_inc(row_used, 1)

            def transposed(use, weight=None, dst_hi=a_hi, dst_lo=a_lo):
                for n in range(KT):
                    dve.wait_ge(tp_hi, KT * use + n + 1)
                    if weight is None:
                        part = (slice(None), slice((n % 2) * 4, (n % 2) * 4 + 4), slice((n // 2) * P, (n // 2 + 1) * P))
                        dve.tensor_tensor(dst_lo[part], ps[:, n % 2, :].rearrange("p (k t) -> p k t", k=4), dst_hi[part], ALU.subtract).then_inc(tp_lo, 1)
                    else:
                        dve.scalar_tensor_tensor(dst_lo[:, n, :], ps[:, n % 2, :], weight(n), dst_hi[:, n, :],
                                                 ALU.mult, ALU.subtract).then_inc(tp_lo, 1)

            dve.wait_ge(const_done, 1)
            for half in range(2):
                rows = slice(half * GC, (half + 1) * GC)
                dve.tensor_copy(mask64[rows, :], tri_le[rows, rows])
            for tb in range(TB):
                normalise(0, tb)
            ahead(-AHEAD)
            transposed(0)
            dve.wait_ge(cols_ld, 16)
            ahead(-1)
            dve.wait_ge(small_hi_done, 1)
            dve.tensor_tensor(small_lo[:, :], small[:, 0:N_SPLIT], small_hi[:, :], ALU.subtract).then_inc(small_done, 1)
            d = slice(DT0, DT0 + SH)
            for m in range(2 * N_P1F):
                ahead(C_P1F + m // 2)
                if m == 1:
                    dve.wait_ge(sm_out, 1)
                    dve.tensor_scalar(dtm[d, 0, :], sm[d, :], col("dt_b")[d, :], None, ALU.add).then_inc(dt_x, 1)
                    for j in range(2):
                        dve.wait_ge(gate_mm, j + 1)
                        dve.tensor_scalar(g_cum[:, j, :], ps[:, j, :], col("gla_b", j), None, ALU.add).then_inc(gate_x, 1)
                    dve.drain()
                    for j in range(2):
                        dve.tensor_scalar(lg[:, j, :], g_cum[:, j, :], 0.0, 1.0 / GATE_NORM, ALU.min, ALU.mult)
                if m == 3:
                    dve.wait_ge(dt_ln, 1)
                    dve.scalar_tensor_tensor(dtm[d, 2, :], dtm[d, 0, :], 0.0, dtm[d, 1, :], ALU.max, ALU.add)
                    dve.drain()
                    dve.tensor_scalar(dtm[d, 3, :], dtm[d, 2, :], ea[d, 0:1], -1.0, ALU.mult, ALU.mult).then_inc(dt_done, 1)
                    for j in range(2):
                        dve.wait_ge(gate_ln, j + 1)
                        dve.scalar_tensor_tensor(lg[:, j, :], e_pos[:, j, :], -1.0 / GATE_NORM, lg[:, j, :], ALU.mult, ALU.add)
                        dve.drain()
                        dve.tensor_tensor_scan(g_cum[:, j, :], reset[:, :], lg[:, j, :], 0.0, ALU.mult, ALU.add)
                        dve.drain()
                        by_chunk = g_cum[:, j, :].rearrange("p (c i) -> p c i", i=GC)
                        dve.tensor_tensor(lg[:, j, :].rearrange("p (c i) -> p c i", i=GC), by_chunk[:, :, GC - 1:GC].to_broadcast([P, NGC, GC]),
                                          by_chunk, ALU.subtract).then_inc(gate_cum, 1)
                if m >= 4:
                    f = m - 4
                    dve.wait_ge(ft_out, F_P1 + m + 1)
                    dve.tensor_scalar(xc[:, f, :], xbc[:, f, 1:1 + T], col("conv_w", f * SCONV), col("conv_b", f), ALU.mult, ALU.add)
                    for k in range(1, SCONV):
                        dve.drain()
                        last = dve.scalar_tensor_tensor(xc[:, f, :], xbc[:, f, 1 + k:1 + k + T], col("conv_w", f * SCONV + k),
                                                        xc[:, f, :], ALU.mult, ALU.add)
                    last.then_inc(conv_done, 1)
            for j in range(2):
                dve.wait_ge(gate_exp, j + 1)
                dve.tensor_tensor(qk[:, j, :], qk[:, j, :], e_pos[:, j, :], ALU.mult)
                dve.tensor_tensor(k_end[:, j, :], qk[:, 2 + j, :], lg[:, j, :], ALU.mult)
                dve.tensor_tensor(qk[:, 2 + j, :], qk[:, 2 + j, :], e_neg[:, j, :], ALU.mult).then_inc(gla_qk, 1)
            ahead(C_P1T)
            ahead(C_P1T + 1)
            for hh in range(2):
                dve.wait_ge(gla_att, hh + 1)
                dve.tensor_tensor(att_s[:, hh, :, :], ps[:, 4 + hh, :].rearrange("p (c i) -> p c i", i=GC),
                                  mask64[:, :].unsqueeze(1).to_broadcast([P, 8, GC]), ALU.mult).then_inc(gla_attc, 1)
            dve.memset(s_gla[:, :, 0, :], 0.0)
            ahead(C_P1T + 2)
            ahead(C_P1T + 3)
            ahead(C_P1T + 4)
            dve.drain()
            for c in range(NGC - 1):
                for j in range(2):
                    if c == 0:
                        dve.wait_ge(gla_st, 2)
                    last = dve.scalar_tensor_tensor(s_gla[:, j, c + 1, :], s_gla[:, j, c, :], e_pos[:, j, c * GC + GC - 1:c * GC + GC],
                                                    ps[:, 4 + j * 2 + c % 2, (c // 2) * GDV:(c // 2 + 1) * GDV], ALU.mult, ALU.add)
                if c < NGC - 2:
                    dve.drain()
            last.then_inc(gla_S, 1)
            ahead(C_P1T + 5)
            for tb in range(TB):
                b = (tb % 2) * 3
                dve.wait_ge(gla_oc, tb + 1)
                pairs = o_s[:, tb % 2, :].rearrange("p (j h v) -> p j h v", j=2, h=2)
                for hh in range(2):
                    last = dve.tensor_tensor(pairs[:, :, hh, :], pairs[:, :, hh, :],
                                             ps[:, b + 1 + hh, 0:2 * GDV].rearrange("p (j v) -> p j v", j=2), ALU.add)
                last.then_inc(gla_od, 1)
                dve.wait_ge(gla_sd, tb + 1)
                dve.reciprocal(rstd[:, 0:GH], sd[:, 0:GH])
                dve.drain()
                for h in range(GH):
                    hs = slice(h * GDV, (h + 1) * GDV)
                    last = dve.scalar_tensor_tensor(xn[:, tb, hs], o_s[:, tb % 2, hs], rstd[:, h:h + 1], xn[:, tb, hs], ALU.mult, ALU.mult)
                last.then_inc(gla_y, 1)

            dve.wait_ge(xt_c, TB + 1)
            dve.memset(s_ssd[:, 0, :], 0.0)
            for tb in range(TB):
                heads = lambda v: v.rearrange("p (h e) -> p h e", e=SP_)
                dve.tensor_tensor(heads(xdt[:, tb, :]), heads(xt[:, tb, :]), dta[:, tb, 0, :].unsqueeze(2).to_broadcast([P, SH, SP_]), ALU.mult)
                dve.drain()
                dve.tensor_tensor(heads(xdte[:, tb, :]), heads(xdt[:, tb, :]), ecum[:, 1, tb, :].unsqueeze(2).to_broadcast([P, SH, SP_]),
                                  ALU.mult).then_inc(xd_done, 1)
                if tb == 0:
                    dve.drain().then_inc(ssd_S, 1)
                for g in range(SG):
                    dve.wait_ge(ssd_L, 2 * tb + g + 1)
                    if tb >= 1:
                        dve.wait_ge(ssd_y, tb)
                    dve.tensor_tensor(w_s[:, g, :].rearrange("p (j l) -> p j l", j=SJ), l_s[:, g, :].rearrange("p (j l) -> p j l", j=SJ),
                                      ps[:, 2 + g, 0:P].unsqueeze(1).to_broadcast([P, SJ, P]), ALU.mult).then_inc(ssd_W, 1)
                dve.wait_ge(ssd_st, tb + 1)
                if tb < TB - 1:
                    for g in range(SG):
                        n = slice(g * SN, (g + 1) * SN)
                        dve.tensor_tensor(heads(s_ssd[n, tb + 1, :]), heads(s_ssd[n, tb, :]),
                                          ecum[n, 2, tb, g * SJ:(g + 1) * SJ].unsqueeze(2).to_broadcast([SN, SJ, SP_]), ALU.mult)
                    dve.drain()
                    dve.tensor_tensor(s_ssd[:, tb + 1, :], s_ssd[:, tb + 1, :], ps[:, 6, 0:SJ * SP_], ALU.add).then_inc(ssd_S, 1)
                dve.wait_ge(ssd_y, tb + 1)
                dve.tensor_tensor(heads(y_t[:, 1, :]), heads(xt[:, tb, :]), col("d_skip", 0, SH).unsqueeze(2).to_broadcast([P, SH, SP_]), ALU.mult)
                for g in range(SG):
                    gs = slice(g * SJ * SP_, (g + 1) * SJ * SP_)
                    dve.tensor_tensor(heads(y_t[:, 0, gs]), heads(ps[:, 7 - 3 * g, 0:SJ * SP_]),
                                      ecum[:, 0, tb, g * SJ:(g + 1) * SJ].unsqueeze(2).to_broadcast([P, SJ, SP_]), ALU.mult)
                dve.drain()
                dve.tensor_tensor(y_t[:, 1, :], y_t[:, 1, :], y_t[:, 0, :], ALU.add)
                dve.drain()
                dve.tensor_tensor(y_t[:, 1, :], y_t[:, 1, :], ps[:, 5, :], ALU.add).then_inc(ssd_yd, 1)
                dve.drain()
                dve.tensor_tensor(xn[:, tb, GW:], y_t[:, 1, :], xn[:, tb, GW:], ALU.mult).then_inc(ssd_yc, 1)
                dve.drain()
            dve.wait_ge(ssd_sd, 1)
            dve.reciprocal(rstd[:, 0:TB * SG], sd[:, 0:TB * SG])
            dve.drain()
            for tb in range(TB):
                gs = xn[:, tb, GW:].rearrange("p (g n) -> p g n", g=SG)
                dve.tensor_tensor(gs, gs, rstd[:, tb * SG:(tb + 1) * SG].unsqueeze(2).to_broadcast([P, SG, SJ * SP_]), ALU.mult).then_inc(xn_done, 1)
            transposed(1, lambda kt: col("gla_norm") if kt < 4 else col("ssd_norm", kt - 4))
            for g in range(2):
                ahead(C_WOUT + 2 * g)
                ahead(C_WOUT + 2 * g + 1)
                for tb in range(TB):
                    dve.wait_ge(tok_done, TB * (G_WOUT + g) + tb + 1)
                    s = slice(g * 512, (g + 1) * 512)
                    last = dve.tensor_tensor(res[:, tb, s], res[:, tb, s], ps[:, 4 - 4 * g + tb, :], ALU.add)
                    if g == 1:
                        last.then_inc(res_done, 1)
                        if tb:
                            normalise(1, tb - 1)
            normalise(1, TB - 1)

            transposed(2)
            for m in range(2 * N_QUERY):
                ahead(C_QUERY + m // 2)
                dve.wait_ge(q_hi_done, m + 1)
                dve.tensor_tensor(q_lo[:, m, :], ps[:, 4 + (F_QUERY + m) % 4, :], q_hi[:, m, :], ALU.subtract).then_inc(ft_out, 1)
            ahead(C_KEYS)
            dve.drain().then_inc(s_out, 2)

            def lo_in_loop(c, n):
                s = (c + AHEAD) % RING
                dve.wait_ge(w_hi_done, n + 1)
                dve.tensor_tensor(w_lo[:, s, :], w_st[:, s, :], w_hi[:, s, :], ALU.subtract).then_inc(w_lo_done, 1)

            def best_keys(i, h):
                s_ps = ps[:, 2 + h % 2, 0:2 * PK].rearrange("p (a k) -> p a k", a=2)
                for a in range(2):
                    dve.max(top_v[:, a, 0:8], s_ps[:, a, :])
                dve.drain()
                for a in range(2):
                    dve.max_index(top_i[:, a, 0:8], top_v[:, a, 0:8], s_ps[:, a, :])
                    last = dve.match_replace(s_cut[:, a, :], top_v[:, a, 0:8], s_ps[:, a, :], LOWEST)
                last.then_inc(s_out, 1)
                dve.drain()
                for a in range(2):
                    dve.max(top_v[:, a, 8:16], s_cut[:, a, :])
                dve.drain()
                for a in range(2):
                    dve.max_index(top_i[:, a, 8:16], top_v[:, a, 8:16], s_cut[:, a, :])
                square = [P, PTOP, PTOP]
                dve.tensor_tensor(cand, top_v[:, 0, :].unsqueeze(2).to_broadcast(square), top_v[:, 1, :].unsqueeze(1).to_broadcast(square), ALU.add)
                dve.drain()
                flat, flat_cut = cand.rearrange("p a b -> p (a b)"), cand_cut.rearrange("p a b -> p (a b)")
                dve.max(best_v[:, 0:8], flat)
                dve.drain()
                dve.max_index(best_p[:, 0:8], best_v[:, 0:8], flat)
                dve.match_replace(flat_cut, best_v[:, 0:8], flat, LOWEST)
                dve.drain()
                dve.max(best_v[:, 8:16], flat_cut)
                dve.drain()
                dve.max_index(best_p[:, 8:16], best_v[:, 8:16], flat_cut)
                dve.drain()
                dve.tensor_scalar(best_k[:, 0, :], best_p, 4, None, ALU.logical_shift_right)
                dve.tensor_scalar(best_k[:, 1, :], best_p, PTOP - 1, None, ALU.bitwise_and)
                at = slice(h * PTOP, (h + 1) * PTOP)
                dve.tensor_copy(score.rearrange("p (t s) -> p t s", t=TB)[:, i, at], best_v)
                dve.drain()
                for a in range(2):
                    dve.tensor_tensor(pick[:, a, :, :], best_k[:, a, :].unsqueeze(2).to_broadcast(square),
                                      iota_f[:, 0:PTOP].unsqueeze(1).to_broadcast(square), ALU.is_equal)
                dve.drain()
                for a in range(2):
                    dve.tensor_tensor(pick[:, a, :, :], pick[:, a, :, :], top_i[:, a, :].unsqueeze(1).to_broadcast(square), ALU.mult)
                dve.drain()
                for a, key in enumerate((key1, key2)):
                    dve.tensor_reduce(key.rearrange("p (t s) -> p t s", t=TB)[:, i, at], pick[:, a, :, :], AX_X, ALU.add)

            with dve.Fori(0, 4) as i:
                for c in range(8):
                    dve.wait_ge(s_done, 8 * i + c + 1)
                    lo_in_loop(c, C_U + 8 * i + c + AHEAD)
                    best_keys(i, c)
            dve.drain()
            by_head = lambda v: v.rearrange("p (h s) -> p h s", s=PTOP)
            whole = [P, TB * PH, PTOP]
            dve.tensor_tensor(by_head(gate_t), by_head(score), by_head(score)[:, :, 0:1].to_broadcast(whole), ALU.subtract).then_inc(soft_x, 1)
            dve.wait_ge(soft_e, 1)
            dve.tensor_reduce(soft[:, 0, :], by_head(gate_t), AX_X, ALU.add)
            dve.drain()
            dve.reciprocal(soft[:, 1, :], soft[:, 0, :])
            dve.drain()
            dve.tensor_tensor(by_head(score), by_head(gate_t), soft[:, 1, :].unsqueeze(2).to_broadcast(whole), ALU.mult).then_inc(soft_done, 1)
            dve.wait_ge(slot_tp, 1)
            dve.tensor_copy(slot_T[:, 0, :], ps[:, 4, :])
            dve.tensor_copy(slot_T[:, 1, :], ps[:, 5, :])
            dve.tensor_copy(g_b16, ps[:, 6, :])
            dve.drain()
            dve.tensor_copy(slot_T[:, 2, :], g_b16)
            dve.tensor_tensor(slot_T[:, 3, :], ps[:, 6, :], g_b16, ALU.subtract).then_inc(slot_done, 1)
            dve.drain()
            with dve.Fori(4, 8) as i:
                for c in range(8):
                    if c % 4 == 0:
                        first = (i - 4) * P + (c // 4) * 64
                        dve.drain()
                        dve.tensor_copy(c_slot, slot_T[:, :, bass.ds(first, 64)])
                        dve.drain()
                    for t in range(2):
                        if t == 1:
                            lo_in_loop(c, C_U + 8 * i + c + AHEAD)
                        at = 2 * c + t
                        dve.wait_ge(g_done, 2 * (16 * (i - 4) + at) + 2)
                        toks = slice((at % 8) * 8, (at % 8) * 8 + 8)
                        dve.tensor_tensor(oh_b[:, at % 2, :, :], iota_b[:, :].unsqueeze(1).to_broadcast([P, 8, PK]),
                                          c_slot[:, 1, toks].unsqueeze(2).to_broadcast([P, 8, PK]), ALU.is_equal)
                        for r in range(8):
                            k = (at % 8) * 8 + r
                            for part in range(2):
                                last = dve.tensor_scalar(oh_a[:, at % 2, r, part, :], iota_b[:, :], c_slot[:, 0, k:k + 1],
                                                         c_slot[:, 2 + part, k:k + 1], ALU.is_equal, ALU.mult)
                        last.then_inc(oh_done, 1)
            dve.drain().then_inc(h_mul, 2)
            with dve.Fori(0, N_V // 4) as i:
                for c in range(4):
                    dve.wait_ge(ga_ld[c % 2], 16 * (2 * i + c // 2 + 1))
                    dve.wait_ge(g_ld[c % 2], 16 * (2 * i + c // 2 + 1))
                    for j in range(2):
                        by_group = lambda v: v.rearrange("p (g t) -> p g t", g=8)
                        last = dve.tensor_tensor(by_group(h_f[:, c % 2, j, :]), by_group(ga_in[:, c % 2, j, :]), g_in[:, c % 2, :, j, :], ALU.mult)
                    last.then_inc(h_mul, 1)
                    dve.wait_ge(h_hi_done, 4 * i + c + 1)
                    dve.tensor_tensor(h_lo[:, c % 2, :, :], h_f[:, c % 2, :, :], h_hi[:, c % 2, :, :], ALU.subtract).then_inc(h_lo_done, 1)
                    lo_in_loop(c, C_V + 4 * i + c + AHEAD)
            split[0] = C_CONV + AHEAD
            for t in range(TB + 2):
                if t < TB:
                    for part in range(2):
                        s = slice(part * 512, (part + 1) * 512)
                        dve.wait_ge(peer_done, 2 * t + part + 1)
                        last = dve.tensor_tensor(res[:, t, s], res[:, t, s], ps[:, 2 * t + part, :], ALU.add)
                    last.then_inc(res_done, 1)
                if 1 <= t <= TB:
                    normalise(2, t - 1, res, res2_done)
                if t >= 2:
                    normalise(3, t - 2)
            dve.memset(cum_b, 0.0)
            dve.tensor_tensor(head_b[:, :], ident_b[:, 0:AH], ident_b[:, 32:32 + AH], ALU.add)
            dve.drain()
            dve.tensor_tensor(head_b[:, :], head_b[:, :], ident_b[:, 64:64 + AH], ALU.add)
            dve.memset(f_one[0:AH, :], 1.0)
            dve.memset(z_s[:, 0:4], 0.0)
            transposed(3)
            dve.wait_ge(f_mm, 1)
            dve.tensor_scalar(f_x[0:AH, :], ps[0:AH, 2, :], col("b_forget")[0:AH, :], None, ALU.add).then_inc(f_xs, 1)
            dve.wait_ge(f_ln, 1)
            dve.scalar_tensor_tensor(f_x[0:AH, :], f_x[0:AH, :], 0.0, f_e[0:AH, :], ALU.min, ALU.subtract)
            dve.drain()
            dve.tensor_tensor_scan(n_cum[0:AH, :], f_one[0:AH, :], f_x[0:AH, :], 0.0, ALU.mult, ALU.subtract)
            dve.drain()
            parts = [cum_b[32 * a:32 * a + AH, :] for a in range(3)]
            dve.tensor_copy(parts[0], n_cum[0:AH, :])
            dve.drain()
            dve.tensor_tensor(c_rest[0:AH, 0, :], n_cum[0:AH, :], parts[0], ALU.subtract)
            dve.drain()
            dve.tensor_copy(c_rest[0:AH, 1, 0:T // 2].bitcast(BF16), c_rest[0:AH, 0, :])
            dve.tensor_copy(parts[1], c_rest[0:AH, 0, :])
            dve.drain()
            dve.tensor_tensor(parts[2], c_rest[0:AH, 0, :], c_rest[0:AH, 1, 0:T // 2].bitcast(BF16), ALU.subtract).then_inc(f_cum, 1)
            dve.drain()

            def conv_low(j):
                dve.wait_ge(cv_hi, j + 1)
                dve.tensor_tensor(c_lo[:, j, :], cv_s[:, j % 2, :], c_hi[:, j, :], ALU.subtract).then_inc(cv_lo, 1)

            for j in range(KT):
                for a in range(3):
                    ahead(C_CONV + (3 * j + a) // 2)
                dve.wait_ge(ft_out, F_CONV + 3 * j + 2)
                dve.tensor_tensor(z_s[:, 4:], cu_s[:, j % 2, :], cc_s[:, j % 2, :], ALU.mult)
                dve.drain()
                dve.tensor_scalar(acc_s, z_s[:, 2:2 + T], col("conv_w2", j * CONVW), col("conv_b2", j), ALU.mult, ALU.add)
                for k in range(1, CONVW):
                    dve.drain()
                    dve.scalar_tensor_tensor(acc_s, z_s[:, 2 + k:2 + k + T], col("conv_w2", j * CONVW + k), acc_s, ALU.mult, ALU.add)
                dve.drain()
                dve.wait_ge(ft_out, F_CONV + 3 * j + 3)
                dve.tensor_tensor(cv_s[:, j % 2, :], acc_s, cb_s[:, j % 2, :], ALU.mult).then_inc(cv_mul, 1)
                if j:
                    conv_low(j - 1)
            conv_low(KT - 1)
            for j in range(KT):
                ahead(C_CO + j)
                dve.wait_ge(sg_done, j + 1)
                dve.wait_ge(ft_done, F_CO + 2 * j + 2)
                dve.tensor_tensor(m1[:, j, :], ps[:, 5 + 2 * (j % 2), :], sg_s[:, j % 2, :], ALU.mult).then_inc(m1_done, 1)
            for g in range(2):
                ahead(C_V2 + 2 * g)
                ahead(C_V2 + 2 * g + 1)
            dve.memset(q_z, 0.0).then_inc(qz_zero, 1)
            for u in range(len(UNITS) + 2):
                if u < len(UNITS):
                    h, qb = UNITS[u]
                    if h % 2 == 0 and qb == 0:
                        ahead(C_QK + h // 2)
                    dve.wait_ge(at_s, u + 1)
                    if u >= 2:
                        dve.wait_ge(at_p, u - 1)
                    dve.tensor_reduce(n_max[:, u % 2:u % 2 + 1], ps[:, u % 2, 0:(qb + 1) * P], AX_X, ALU.max, negate=True).then_inc(at_max, 1)
                if 1 <= u <= len(UNITS):
                    v = u - 1
                    n = UNITS[v][1] + 1
                    dve.wait_ge(at_t, v + 1)
                    if v >= 2:
                        dve.wait_ge(at_o, v - 1)
                    dve.tensor_copy(pT_s[:, v % 2, 0:n, :], ps[:, 2 + v % 2, 0:n * P].rearrange("p (k q) -> p k q", k=n)).then_inc(at_tc, 1)
                if u >= 2:
                    v = u - 2
                    h, qb = UNITS[v]
                    dve.reciprocal(r_inv[:, v % 2:v % 2 + 1], r_sum[:, v % 4:v % 4 + 1])
                    dve.drain()
                    dve.wait_ge(at_o, v + 1)
                    last = dve.tensor_scalar(xn[:, qb, h * ADH:(h + 1) * ADH], ps[:, 4 + v % 2, 0:ADH], r_inv[:, v % 2:v % 2 + 1], None, ALU.mult)
                    last.then_inc(at_out, 1)
            dve.drain().then_inc(xn_done, TB)
            transposed(4, None, c_hi, c_lo)

            def mix_low(j):
                dve.wait_ge(mix_hi, j + 1)
                dve.tensor_tensor(m_split[:, j, 1, :], mix_s[:, j % 2, :], m_split[:, j, 0, :], ALU.subtract).then_inc(mix_lo, 1)

            for j in range(KT):
                ahead(C_AO + j)
                dve.wait_ge(sg_done, KT + j + 1)
                dve.wait_ge(ft_done, F_AO + 2 * j + 2)
                dve.tensor_tensor(prod_s[:, j % 2, :], ps[:, 5 + 2 * (j % 2), :], sg_s[:, j % 2, :], ALU.mult)
                dve.drain()
                dve.tensor_tensor(mix_s[:, j % 2, :], prod_s[:, j % 2, :], m1[:, j, :], ALU.add).then_inc(mix_done, 1)
                if j:
                    mix_low(j - 1)
            mix_low(KT - 1)
            for g in range(2):
                ahead(C_WO2 + 2 * g)
                ahead(C_WO2 + 2 * g + 1)
                for tb in range(TB):
                    dve.wait_ge(tok_done, TB * (G_WO2 + g) + tb + 1)
                    s = slice(g * 512, (g + 1) * 512)
                    last = dve.tensor_tensor(res[:, tb, s], res[:, tb, s], ps[:, 4 * g + tb, :], ALU.add)
                    if g == 1:
                        last.then_inc(res_done, 1)
                        if tb:
                            normalise(4, tb - 1)
            normalise(4, TB - 1)

            transposed(5)
            for tb in range(TB):
                dve.wait_ge(pk_hi, tb + 1)
                dve.tensor_tensor(pk[:, tb, 1, :], xn[:, tb, :], pk[:, tb, 0, :], ALU.subtract).then_inc(pk_lo, 1)

            def rows_of_pass(r):
                if not isinstance(r, int):
                    dve.tensor_scalar(now, now, 1.0, None, ALU.add)
                    dve.drain()
                for s in range(2):
                    dve.scalar_tensor_tensor(tok_now[:, s, :], blk_f[:, 0, s, :], now, tok_f[:, :], ALU.is_equal, ALU.mult)
                dve.drain()
                dve.tensor_tensor(tok_e.rearrange("p s t e -> p (s t) e"), e_one.rearrange("p s t e -> p (s t) e"),
                                  tok_now.rearrange("p s t -> p (s t)").unsqueeze(2).to_broadcast([P, 2 * TB, NE]), ALU.mult).then_inc(rt_tok, 1)

            dve.memset(lr_g, LOWEST)
            dve.wait_ge(rt_mm, 1)
            dve.tensor_copy(lr, ps[:, 2, 0:TB * SM_R].rearrange("p (t n) -> p t n", t=TB))
            dve.drain()
            dve.tensor_copy(lr_g[:, :, 0:EG], lr[:, :, 0:EG])
            dve.drain()
            for tb in range(TB):
                dve.max(g_max[:, tb, :], lr_g[:, tb, :])
            dve.drain()
            for tb in range(TB):
                dve.max_index(g_idx[:, tb, :], g_max[:, tb, :], lr_g[:, tb, :])
            dve.tensor_tensor(r_exp[:, :, 0:EG], lr[:, :, 0:EG], g_max[:, :, 0:1].to_broadcast([P, TB, EG]), ALU.subtract)
            dve.drain()
            dve.tensor_copy(g_num, g_idx[:, :, 0])
            dve.drain()
            dve.tensor_tensor(g_one, g_num.unsqueeze(2).to_broadcast([P, TB, EG]), iota_f[:, 0:EG].unsqueeze(1).to_broadcast([P, TB, EG]), ALU.is_equal)
            dve.drain()
            dve.tensor_tensor(le_all, lr[:, :, EG:].rearrange("p t (g e) -> p t g e", g=EG), g_one.unsqueeze(3).to_broadcast([P, TB, EG, EPG]), ALU.mult)
            dve.drain()
            dve.tensor_reduce(le_sel, le_all.rearrange("p t g e -> p t e g"), AX_X, ALU.add)
            dve.drain()
            for tb in range(TB):
                dve.max(e_max[:, tb, :], le_sel[:, tb, :])
            dve.drain()
            for tb in range(TB):
                dve.max_index(e_idx[:, tb, :], e_max[:, tb, :], le_sel[:, tb, :])
            dve.tensor_tensor(r_exp[:, :, EG:EG + 1], e_max[:, :, 1:2], e_max[:, :, 0:1], ALU.subtract).then_inc(rt_x, 1)
            dve.drain()
            for s in range(2):
                dve.tensor_copy(e_num[:, s, :], e_idx[:, :, s])
            dve.drain()
            for s in range(2):
                dve.scalar_tensor_tensor(e_of[:, s, :], g_num, float(EPG), e_num[:, s, :], ALU.mult, ALU.add)
            dve.drain()
            for s in range(2):
                dve.tensor_tensor(e_one[:, s, :, :], e_of[:, s, :].unsqueeze(2).to_broadcast([P, TB, NE]),
                                  iota_f[:, 0:NE].unsqueeze(1).to_broadcast([P, TB, NE]), ALU.is_equal)
            dve.drain()
            dve.tensor_tensor(e_any, e_one[:, 0, :, :], e_one[:, 1, :, :], ALU.add).then_inc(rt_pick, 1)
            dve.wait_ge(rt_e, 1)
            dve.tensor_reduce(g_sum, r_exp[:, :, 0:EG], AX_X, ALU.add)
            dve.drain()
            dve.scalar_tensor_tensor(w_den, r_exp[:, :, EG], 1.0, g_sum, ALU.add, ALU.mult)
            dve.drain()
            dve.reciprocal(w_tok[:, 0, :], w_den)
            dve.drain()
            dve.tensor_tensor(w_tok[:, 1, :], w_tok[:, 0, :], r_exp[:, :, EG], ALU.mult)
            dve.wait_ge(rt_rank, 1)
            up_to = ps[:, 3, 0:TB * NE].rearrange("p (t e) -> p t e", t=TB)
            for s in range(2):
                dve.tensor_tensor(e_rank[:, s, :, :], e_one[:, s, :, :], up_to, ALU.mult)
            dve.drain()
            dve.tensor_reduce(rank_f, e_rank, AX_X, ALU.add)
            dve.drain()
            dve.tensor_scalar(rank_u, rank_f, -1.0, None, ALU.add)
            dve.drain()
            dve.tensor_scalar(blk_u[:, 0, :, :], rank_u, CAP.bit_length() - 1, None, ALU.logical_shift_right)
            dve.tensor_scalar(blk_u[:, 1, :, :], rank_u, CAP - 1, None, ALU.bitwise_and)
            dve.drain()
            dve.tensor_copy(blk_f, blk_u)
            dve.memset(now, 0.0)
            dve.drain()
            dve.tensor_tensor(row_one.rearrange("p s t c -> p (s t) c"), blk_f[:, 1, :, :].rearrange("p s t -> p (s t)").unsqueeze(2).to_broadcast([P, 2 * TB, CAP]),
                              iota_f[:, 0:CAP].unsqueeze(1).to_broadcast([P, 2 * TB, CAP]), ALU.is_equal)
            rows_of_pass(0)
            dve.scalar_tensor_tensor(e_blk, blk_f[:, 0, :, :], float(NE), e_of, ALU.mult, ALU.add)
            dve.drain()
            dve.scalar_tensor_tensor(to_y, e_blk, float(CAP), blk_f[:, 1, :, :], ALU.mult, ALU.add)
            dve.wait_ge(rt_all, 1)
            dve.tensor_reduce(n_rows, ps[:, 4, 0:NE], AX_X, ALU.max)
            dve.drain()
            dve.tensor_copy(n_rows_i, n_rows).then_inc(rt_dest, 1)

            def lo_of(r, i, k):
                s = k % RING
                dve.wait_ge(w_hi_done, r * PASS + 12 * i + (C_MOE + k + 1))
                dve.tensor_tensor(w_lo[:, s, :], moe_st[k % MOE_RING], w_hi[:, s, :], ALU.subtract).then_inc(w_lo_done, 1)

            def rows_lo(r, i, c):
                dve.wait_ge(xe_tp, 2 * moe(r, i, c) + 6)
                dve.tensor_copy(xeT[:, c % 2, 1, :, :].rearrange("p k t -> p (k t)"), ps[:, 7, 0:KT * CAP]).then_inc(xe_lo, 1)

            def hidden(r, i, c, k):
                dve.wait_ge(sil_done, moe(r, i, c) + 1)
                dve.wait_ge(moe_mm, r * PASS + 12 * i + (k + 2 + RING))
                dve.tensor_tensor(hid_f[0:CAP, :], sil[0:CAP, :], ps[0:CAP, 1, :], ALU.mult).then_inc(hid_mul, 1)

            def hidden_lo(r, i, c):
                dve.wait_ge(hid_hi, moe(r, i, c) + 1)
                dve.tensor_tensor(hid_b[0:CAP, 1, :], hid_f[0:CAP, :], hid_b[0:CAP, 0, :], ALU.subtract).then_inc(hid_lo, 1)

            def first(r):
                if not isinstance(r, int):
                    rows_of_pass(r)
                dve.wait_ge(rt_sum, r + 1)
                dve.tensor_copy(row_i[0:CAP, :], ps[0:CAP, 5, 0:NE]).then_inc(rt_row, 1)
                for k in range(AHEAD):
                    lo_of(r, 0, k)
                rows_lo(r, 0, 0)
                rows_lo(r, 0, 1)
                for k in range(AHEAD, 6):
                    lo_of(r, 0, k)
                hidden(r, 0, 0, 2)
                lo_of(r, 0, 6)

            def step(r, i, c, more=True):
                k = 6 * c - 2
                hidden_lo(r, i, c - 1)
                lo_of(r, i, k + 3)
                lo_of(r, i, k + 4)
                if more:
                    rows_lo(r, i, c + 1)
                for n in range(5, 8):
                    lo_of(r, i, k + n)
                hidden(r, i, c, k + 4)
                if more:
                    lo_of(r, i, k + 8)

            def last(r):
                step(r, 0, NE - 1, more=False)
                hidden_lo(r, 0, NE - 1)

            one_pass = every_expert(first, step, last)
            one_pass(dve, 0)
            more_passes(dve, one_pass)

            for tb in range(TB):
                dve.wait_ge(yg_ld[tb], 32)
                for s in range(2):
                    last = dve.scalar_tensor_tensor(res[:, tb, :], y_g[:, tb, s, :], w_tok[:, s, tb:tb + 1], res[:, tb, :], ALU.mult, ALU.add)
                    if s == 0:
                        dve.drain()
                last.then_inc(res_done, 1)
                if tb:
                    normalise(5, tb - 1, done=end_done)
            normalise(5, TB - 1, done=end_done)


def _features(w):
    n = w.shape[1] // P
    return w.reshape(KT, P, n, P).transpose(2, 1, 0, 3).reshape(n, P, D)


def _pairs(tiles):
    n = tiles.shape[0] // 2
    return tiles.reshape(n, 2, P, -1).transpose(0, 2, 1, 3).reshape(n, P, CW)


def _tokens(w):
    n, k = w.shape[1] // 512, w.shape[0] // 512
    return w.reshape(k, 4, P, n, 512).transpose(3, 0, 2, 1, 4).reshape(n * k, P, CW)


def _column(v):
    return v.reshape(-1, P).T


def _rows(v, at=0):
    out = np.zeros((P, 1), np.float32)
    out[at:at + v.shape[0], 0] = v
    return out


def lay_out(a):
    w_in = a["w_in"][0]
    ends = np.cumsum([GQK, GQK, GW, GRANK, GW, SW, XBC, SH])
    q, k, v, rank, gate, z, xbc, dt = np.split(w_in, ends[:-1], axis=1)
    f = np.float32
    w = np.empty((N_CHUNKS, P, CW), f)

    def put(at, n, chunks):
        assert chunks.shape == (n, P, CW), (at, n, chunks.shape)
        w[at:at + n] = chunks

    put(C_P1F, N_P1F, _pairs(_features(np.concatenate([q, k, xbc], 1))))
    put(C_P1T, N_P1T, _tokens(np.concatenate([v, gate, z], 1)))
    put(C_WOUT, N_WOUT, _tokens(a["w_out"][0]))
    put(C_QUERY, N_QUERY, _pairs(_features(a["peer_w_query"][0])))
    put(C_KEYS, N_KEYS, a["peer_sub_keys"][0].reshape(2 * PH, PK, P).transpose(2, 0, 1).reshape(1, P, CW))
    put(C_U, N_U, _pairs(a["peer_u"][0].reshape(PK, PK, KT, P).transpose(0, 3, 2, 1).reshape(PK, P, D)))
    put(C_V, N_V, _pairs(a["peer_v"][0].reshape(PK, PK, D)))
    sizes = [D] * 6 + [AH, D, D]
    cb, cc, cu, q2, k2, v2, fl, gc, ga = np.split(a["w_in_2"], np.cumsum(sizes)[:-1], axis=1)
    mix = lambda *ws: _pairs(np.stack([_features(x) for x in ws], 1).reshape(-1, P, D))
    put(C_CONV, N_CONV, mix(cu, cc, cb))
    put(C_CO, N_CO, mix(gc, a["w_conv_out_2"]))
    put(C_V2, N_V2, _tokens(v2))
    put(C_QK, N_QK, mix(q2, k2))
    put(C_AO, N_AO, mix(ga, a["w_att_out_2"]))
    put(C_WO2, N_WO2, _tokens(a["w_out_2"]))
    gates = a["w_e_gate_2"].reshape(NE, 2, 4, P, DE).transpose(0, 1, 3, 2, 4).reshape(NE, 2, P, CW)
    ups = a["w_e_up_2"].reshape(NE, 2, 4, P, DE).transpose(0, 1, 3, 2, 4).reshape(NE, 2, P, CW)
    downs = a["w_e_down_2"].reshape(NE, 2, 2, P, D).transpose(0, 1, 3, 2, 4).reshape(NE, 2, P, CW)
    for e in range(NE):
        w[MOE_GATE(e):MOE_GATE(e) + 2] = gates[e]
        w[MOE_UP(e):MOE_UP(e) + 2] = ups[e]
        w[MOE_DOWN(e):MOE_DOWN(e) + 2] = downs[e]
    small_in = np.zeros((KT, P, SM_IN), f)
    small_in[:, :, 0:GRANK] = rank.reshape(KT, P, GRANK)
    small_in[:, :, DT0:DT0 + SH] = dt.reshape(KT, P, SH)
    router = np.concatenate([a["w_router_group_2"], a["w_router_expert_2"].transpose(1, 0, 2).reshape(D, NE)], 1)
    gate2 = np.zeros((P, GQK), f)
    gate2[0:GRANK] = a["gla_w_gate2"][0]
    by_part = lambda x: x.reshape(KT, P, -1).transpose(1, 0, 2).reshape(P, -1)
    small = np.concatenate([by_part(small_in), by_part(fl), by_part(router), gate2], 1)
    taps = lambda x: x.reshape(x.shape[0], -1, P).transpose(2, 1, 0).reshape(P, -1)
    table = np.concatenate([
        _column(a["gla_b_gate"][0]), _column(a["gla_norm_w"][0]), taps(a["ssd_conv_w"][0]),
        _column(a["ssd_conv_b"][0]), _rows(a["ssd_dt_bias"][0], DT0), _rows(a["ssd_a_log"][0], DT0),
        np.broadcast_to(a["ssd_d"][0], (P, SH)), _column(a["ssd_norm_w"][0]),
        taps(a["conv_w_2"]), _column(a["conv_b_2"]), _rows(a["b_forget_2"]),
    ], 1)
    return {
        "w_all": w, "x": np.ascontiguousarray(a["x"][0]), "cols": np.ascontiguousarray(table), "small": np.ascontiguousarray(small),
        "rows": np.stack([a["norm_mix_w"][0], a["norm_ffn_w"][0], a["norm_final_w"], a["norm_mix_g_2"], a["norm_ffn_g_2"], a["norm_final_g_2"]])[:, None],
    }


def kernel(**inputs):
    import concourse.bacc as bacc
    from concourse.bass_utils import run_bass_kernel_spmd

    arrays = lay_out({k: np.asarray(v) for k, v in inputs.items()})
    nc = bacc.Bacc("TRN2", target_bir_lowering=False, num_devices=1)
    args = [nc.dram_tensor("in_" + k, v.shape, mybir.dt.from_np(v.dtype), kind="ExternalInput").ap() for k, v in arrays.items()]
    out = nc.dram_tensor("out", (T, D), F32, kind="ExternalOutput").ap()
    build_program(nc, *args, out)
    r = run_bass_kernel_spmd(nc, [{"in_" + k: v for k, v in arrays.items()}], core_ids=[0])
    return r.results[0]["out"].reshape(1, T, D)
```

```python
from contextlib import ExitStack

import numpy as np

import concourse.bass as bass
from concourse import mybir

F32 = mybir.dt.float32
BF16 = mybir.dt.bfloat16
I32 = mybir.dt.int32
U32 = mybir.dt.uint32
ALU = mybir.AluOpType
ACT = mybir.ActivationFunctionType
AX_X = mybir.AxisListType.X

P = 128
T = 512
TB = T // P
D = 1024
KT = D // P
EPS = 1e-6
NEG = -1.0e30
LOWEST = -3.4e38

GH, GDK, GDV, GC = 4, 64, 128, 64
GQK, GW, GRANK = GH * GDK, GH * GDV, 16
NGC = T // GC
GATE_NORM = 16.0
SH, SP_, SG, SN, SCONV = 8, 64, 2, 64, 4
SJ = SH // SG
SW = SH * SP_
XBC = SW + 2 * SG * SN
PH, PK, PTOP = 8, 128, 16
CONVW = 3
AH, ADH = 16, 64
EG, EPG, DE = 4, 8, 512
NE = EG * EPG
CAP = 64
PASSES = T // CAP

CW = 2048
RING = 4
AHEAD = 3
N_P1F = (2 * GQK + XBC) // P // 2
N_P1T = 3 * 2
N_WOUT = 4
N_QUERY = 2 * PH // 2
N_KEYS = 1
N_U = PK // 2
N_V = PK // 2
N_CONV = 3 * KT // 2
N_V2 = 4
N_QC = 2 * KT
N_AO = KT
N_WO2 = 4
N_MOE = NE * 6
MOE_RING = 12
C_P1F = 0
C_P1T = C_P1F + N_P1F
C_WOUT = C_P1T + N_P1T
C_QUERY = C_WOUT + N_WOUT
C_KEYS = C_QUERY + N_QUERY
C_U = C_KEYS + N_KEYS
C_V = C_U + N_U
C_CONV = C_V + N_V
C_V2 = C_CONV + N_CONV
C_QC = C_V2 + N_V2
C_AO = C_QC + N_QC
C_WO2 = C_AO + N_AO
C_MOE = C_WO2 + N_WO2
N_CHUNKS = C_MOE + N_MOE

_cols = {}
_at = 0
for _name, _n in (("gla_b", 2), ("gla_norm", 1), ("conv_w", 6 * SCONV), ("conv_b", 6),
                  ("dt_b", 1), ("a_log", 1), ("d_skip", SH), ("ssd_norm", 4),
                  ("conv_w2", KT * CONVW), ("conv_b2", KT), ("b_forget", 1)):
    _cols[_name] = _at
    _at += _n
N_COLS = _at
SM_IN, SM_F, SM_R = 40, 16, EG + NE
O_IN, O_F, O_R = 0, KT * SM_IN, KT * (SM_IN + SM_F)
N_SPLIT = KT * (SM_IN + SM_F + SM_R)
O_G2 = N_SPLIT
N_SMALL = N_SPLIT + GQK
DT0 = 32


def CHUNK_QK(j):
    return C_QC + max(2 * j - 1, 0)


def CHUNK_CO(j):
    return C_QC + min(2 * j + 2, N_QC - 1)


def MOE_GATE(e):
    return C_MOE + (0 if e == 0 else 4 + (e - 1) * 6)


def MOE_UP(e):
    return C_MOE + (2 if e == 0 else 4 + (e - 1) * 6 + 4)


def MOE_DOWN(e):
    return C_MOE + 4 + e * 6 + (2 if e < NE - 1 else 0)



def build_program(nc, w_all, x_in, cols_in, small_in, rows_in, out):
    ctx = ExitStack()
    with ctx:
        def sb(name, shape, dt=F32):
            return ctx.enter_context(nc.sbuf_tensor(name, shape, dt))

        def sem(name):
            return ctx.enter_context(nc.semaphore(name))

        w_st = sb("w_st", [P, RING, CW])
        w_hi = sb("w_hi", [P, RING, CW], BF16)
        w_lo = sb("w_lo", [P, RING, CW], BF16)
        res = sb("res", [P, TB, D])
        a_hi = sb("a_hi", [P, KT, T], BF16)
        a_lo = sb("a_lo", [P, KT, T], BF16)
        xn = sb("xn", [P, TB, D])
        cols = sb("cols", [P, N_COLS])
        small_hi = sb("small_hi", [P, N_SPLIT], BF16)
        small_lo = sb("small_lo", [P, N_SPLIT], BF16)
        ident = sb("ident", [P, P])
        ident_b = sb("ident_b", [P, P], BF16)
        tri_le = sb("tri_le", [P, P])
        tri_gt = sb("tri_gt", [P, P])
        tri_neg = sb("tri_neg", [P, P])
        neg_gt = sb("neg_gt", [P, P])
        neg_gt_b = sb("neg_gt_b", [P, P], BF16)
        ones = sb("ones", [P, P])
        mask64 = sb("mask64", [P, GC])
        eps = sb("eps", [P, 1])
        iota_i = sb("iota_i", [P, P], I32)
        ss = sb("ss", [P, 16])
        sd = sb("sd", [P, 16])
        rstd = sb("rstd", [P, 16])
        ARENA = 19712
        arena = sb("arena", [P, ARENA])
        ps = ctx.enter_context(nc.psum_tensor("ps", [P, 8, 512], F32))

        def col(name, i=0, n=1):
            return cols[:, _cols[name] + i:_cols[name] + i + n]

        def view(at, *shape, dt=F32):
            n = int(np.prod(shape)) * (2 if dt == BF16 else 4) // 4
            assert at + n <= ARENA, (at, n)
            v = arena[:, at:at + n]
            if dt != F32:
                v = v.bitcast(dt)
            names = "abcd"[:len(shape)]
            return v.rearrange(f"p ({' '.join(names)}) -> p {' '.join(names)}",
                               **{c: s for c, s in zip(names, shape)}) if len(shape) > 1 else v

        o = 0
        qk = view(o, 4, T); xdte = view(o, TB, T); o += 4 * T
        xbc = view(o, 6, T + 4); o += 6 * (T + 4)
        xt = view(o - 6 * (T + 4), TB, T); bt = view(o - 6 * (T + 4) + 4 * T, TB, P)
        sm = view(o, T); o += T
        vT = view(o, TB, GW); o += TB * GW
        lg = view(o, 2, T); att_s = view(o, 2, 8, GC); l_s = view(o, 2, 4 * P); o += 2 * T
        g_cum = view(o, 2, T); e_neg = view(o + 2 * T, 2, T); s_gla = view(o, 2, NGC, GDV); xdt = view(o, TB, T); o += 4 * T
        e_pos = view(o, 2, T); y_t = view(o, 2, T); o += 2 * T
        k_end = view(o, 2, T); o_s = view(o, 2, T); w_s = view(o, 2, 4 * P); o += 2 * T
        small = view(o, N_SMALL); k_endT = view(o, 2, TB, P); s_ssd = view(o, TB, SJ * SP_); o += 2 * T
        xc = view(o, 6, T); o += 6 * T
        reset = view(o, T); o += T
        dtm = view(o, 4, T); o += 4 * T
        dta = view(o, TB, 2, SH); o += TB * 2 * SH
        ecum = view(o, 3, TB, SH); o += 3 * TB * SH
        ea = view(o, 2); o += 2

        q_hi = view(0, 2 * PH, T, dt=BF16)
        q_lo = view(4 * 1024, 2 * PH, T, dt=BF16)
        keys_hi = view(8 * 1024, 2 * PH, PK, dt=BF16)
        keys_lo = view(9 * 1024, 2 * PH, PK, dt=BF16)
        o = 10 * 1024
        s_cut = view(o, 2, PK); o += 2 * PK
        top_v = view(o, 2, PTOP); o += 2 * PTOP
        top_i = view(o, 2, PTOP, dt=U32); o += 2 * PTOP
        cand = view(o, PTOP, PTOP); o += PTOP * PTOP
        cand_cut = view(o, PTOP, PTOP); o += PTOP * PTOP
        best_v = view(o, PTOP); o += PTOP
        best_p = view(o, PTOP, dt=U32); o += PTOP
        best_k = view(o, 2, PTOP, dt=U32); o += 2 * PTOP
        pick = view(o, 2, PTOP, PTOP); o += 2 * PTOP * PTOP
        assert o <= 16 * 1024
        g_st = view(0, 2, PK, T // 8)
        slot_T = view(16 * 1024, 4, T)
        oh_b = view(18 * 1024, 2, 8, PK, dt=BF16)
        c_slot = view(19 * 1024, 4, T // 8)
        xn_flat = xn[:, :, :].rearrange("p t d -> p (t d)")
        u_st = xn_flat[:, 0:2048].rearrange("p (r j t) -> p r j t", r=2, j=2)
        key1 = xn_flat[:, 2048:2560]
        key2 = xn_flat[:, 2560:3072]
        score = xn_flat[:, 3072:3584]
        gate_t = xn_flat[:, 3584:4096]
        oh_a = xn_flat[:, 2048:4096].bitcast(BF16).rearrange("p (r t s k) -> p r t s k", r=2, t=8, s=2)
        ga_in = view(0, 2, 2, T)
        g_in = view(2048, 2, 7, 2, T // 8)
        h_f = view(4096, 2, 2, T)
        h_hi = view(6144, 2, 2, T, dt=BF16)
        h_lo = view(7168, 2, 2, T, dt=BF16)
        g_b16 = view(18 * 1024, T, dt=BF16)
        first_st = sb("first_st", [P, 2, 3, 4])
        soft = sb("soft", [P, 2, TB * PH])
        iota_f = sb("iota_f", [P, P])
        iota_b = sb("iota_b", [P, P], BF16)
        tok_i = sb("tok_i", [P, TB], I32)
        tok_f = sb("tok_f", [P, TB])
        zero_i = sb("zero_i", [P, 2], I32)
        act_dram = nc.dram_tensor("act_dram", (N_U, P, 2 * T), F32, kind="Internal").ap()
        gate_dram = nc.dram_tensor("gate_dram", (7, P, PK, T // 8), F32, kind="Internal").ap()

        c_hi = view(0, KT, T, dt=BF16)
        c_lo = view(2048, KT, T, dt=BF16)
        m1 = view(4096, KT, T)
        m_split = view(4096, KT, 2, T, dt=BF16)
        v_s = view(8192, TB, D)
        cu_s, cc_s, cb_s = (view(8192 + 1024 * n, 2, T) for n in range(3))
        z_s = view(8192 + 3072, T + 4)
        q_s = view(12288, 2, 2, T, dt=BF16)
        k_hi = view(13312, 2, 2, T, dt=BF16)
        k_lo = view(14336, 2, 2, T, dt=BF16)
        f_x, f_e = view(14336, T), view(14336 + T, T)
        p_s = [view(at, T) for at in (15360, 15872, 18944)]
        acc_s = view(15360, T)
        mix_s = view(15360, 2, T)
        pT_s = view(16384, 2, TB, P)
        cv_s = view(16384, 2, T)
        prod_s = view(16384, 2, T)
        cum_b = view(17408, T, dt=BF16)
        n_cum = view(15360, T)
        c_rest = view(16384, 2, T)
        sg_s = view(17920, 2, T)
        f_one = view(18944, T)
        head_b = sb("head_b", [P, AH], BF16)
        pk = view(0, TB, 2, D, dt=BF16)
        x_g = view(4096, 2, 2, D, dt=BF16)
        xeT = view(6144, 2, 2, KT, CAP, dt=BF16)
        o = 0
        sil = view(o, DE); o += DE
        hid_f = view(o, DE); o += DE
        hid_b = view(o, 2, DE, dt=BF16); o += DE
        hidT = view(o, 2, DE // P, CAP, dt=BF16); o += DE // P * CAP
        y_st = view(o, 2, D); o += 2 * D
        assert o <= TB * D
        y_g = view(0, TB, 2, D)
        o = TB * 2 * D
        lr = view(o, TB, SM_R); o += TB * SM_R
        lr_g = view(o, TB, 8); o += TB * 8
        g_max = view(o, TB, 8); o += TB * 8
        g_idx = view(o, TB, 8, dt=U32); o += TB * 8
        g_num = view(o, TB); o += TB
        g_one = view(o, TB, EG); o += TB * EG
        le_all = view(o, TB, EG, EPG); o += TB * NE
        le_sel = view(o, TB, EPG); o += TB * EPG
        e_max = view(o, TB, 8); o += TB * 8
        e_idx = view(o, TB, 8, dt=U32); o += TB * 8
        e_num = view(o, 2, TB); o += 2 * TB
        e_of = view(o, 2, TB); o += 2 * TB
        r_exp = view(o, TB, EG + 1); o += TB * (EG + 1)
        g_sum = view(o, TB); o += TB
        w_den = view(o, TB); o += TB
        w_tok = view(o, 2, TB); o += 2 * TB
        e_one = view(o, 2, TB, NE); o += 2 * TB * NE
        e_any = view(o, TB, NE); o += TB * NE
        e_rank = view(o, 2, TB, NE); o += 2 * TB * NE
        rank_f = view(o, 2, TB); o += 2 * TB
        rank_u = view(o, 2, TB, dt=U32); o += 2 * TB
        blk_u = view(o, 2, 2, TB, dt=U32); o += 4 * TB
        blk_f = view(o, 2, 2, TB); o += 4 * TB
        e_blk = view(o, 2, TB); o += 2 * TB
        to_y = view(o, 2, TB, dt=I32); o += 2 * TB
        row_one = view(o, 2, TB, CAP); o += 2 * TB * CAP
        now = view(o, 1); o += 1
        tok_now = view(o, 2, TB); o += 2 * TB
        tok_e = view(o, 2, TB, NE); o += 2 * TB * NE
        n_rows = view(o, 1); o += 1
        n_rows_i = view(o, 1, dt=I32); o += 1
        row_i = view(o, NE + 1, dt=I32); o += NE + 1
        idx = view(o, 2, dt=I32); o += 2
        ARENA_SLOTS = 4
        moe_st = ([w_st[:, s, :] for s in range(RING)] + [view(o + s * CW, CW) for s in range(ARENA_SLOTS)]
                  + [v[:, :, :].rearrange("p k t -> p (k t)").bitcast(F32) for v in (a_hi, a_lo)]
                  + [xn_flat[:, s * CW:(s + 1) * CW] for s in range(2)])
        x_dram = nc.dram_tensor("x_dram", (T, 2 * D), BF16, kind="Internal").ap()
        y_dram = nc.dram_tensor("y_dram", (PASSES * NE, CAP, D), F32, kind="Internal").ap()
        row = sb("row", [P, 2, D])
        n_max = sb("n_max", [P, 3])
        r_sum = sb("r_sum", [P, 4])
        r_inv = sb("r_inv", [P, 2])

        w_ld = [sem(f"w_ld{s}") for s in range(RING)]
        w_hi_done = sem("w_hi_done")
        w_lo_done = sem("w_lo_done")
        ft_done, ft_out = sem("ft_done"), sem("ft_out")
        tok_half, tok_done, tok_out = sem("tok_half"), sem("tok_done"), sem("tok_out")
        cols_ld, small_ld = sem("cols_ld"), sem("small_ld")
        x_ld = [sem(f"x_ld{tb}") for tb in range(TB)]
        small_hi_done, small_done = sem("small_hi_done"), sem("small_done")
        const_step, const_done = sem("const_step"), sem("const_done")
        res_done = sem("res_done")
        res2_done = sem("res2_done")
        sd_done, xn_done = sem("sd_done"), sem("xn_done")
        tp_done, tp_hi, tp_lo = sem("tp_done"), sem("tp_hi"), sem("tp_lo")
        sm_done, sm_out = sem("sm_done"), sem("sm_out")
        conv_done, silu_done = sem("conv_done"), sem("silu_done")
        gate_mm, gate_x, gate_ln, gate_cum, gate_exp = (sem(n) for n in ("gate_mm", "gate_x", "gate_ln", "gate_cum", "gate_exp"))
        dt_x, dt_ln, dt_done = sem("dt_x"), sem("dt_ln"), sem("dt_done")
        gla_qk, gla_kt, gla_ktc, gla_att, gla_attc, gla_st, gla_S = (
            sem(n) for n in ("gla_qk", "gla_kt", "gla_ktc", "gla_att", "gla_attc", "gla_st", "gla_S"))
        gla_o, gla_oc, gla_od, gla_sd, gla_y = (sem(n) for n in ("gla_o", "gla_oc", "gla_od", "gla_sd", "gla_y"))
        xt_tp, xt_c, dta_tp, dta_c, cum_mm, cum_exp = (sem(n) for n in ("xt_tp", "xt_c", "dta_tp", "dta_c", "cum_mm", "cum_exp"))
        xd_done, ssd_mm, ssd_L, ssd_W, ssd_st, ssd_S, ssd_y, ssd_yc, ssd_yd, ssd_sd = (
            sem(n) for n in ("xd_done", "ssd_mm", "ssd_L", "ssd_W", "ssd_st", "ssd_S", "ssd_y", "ssd_yc", "ssd_yd", "ssd_sd"))
        out_st = sem("out_st")
        row_ld, row_used = [sem(f"row_ld{b}") for b in range(2)], sem("row_used")
        f_mm, f_xs, f_ln, f_cum = (sem(n) for n in ("f_mm", "f_xs", "f_ln", "f_cum"))
        cv_mul, cv_hi, cv_lo = sem("cv_mul"), sem("cv_hi"), sem("cv_lo")
        sg_done, m1_done = sem("sg_done"), sem("m1_done")
        qk_hi, qk_out = sem("qk_hi"), sem("qk_out")
        at_s, at_max, at_p, at_t, at_tc, at_o, at_out = (sem(n) for n in ("at_s", "at_max", "at_p", "at_t", "at_tc", "at_o", "at_out"))
        mix_done, mix_hi, mix_lo = sem("mix_done"), sem("mix_hi"), sem("mix_lo")
        q_hi_done = sem("q_hi_done")
        u_done, u_out = sem("u_done"), sem("u_out")
        u_stored = [sem(f"u_stored{r}") for r in range(2)]
        s_done, s_out = sem("s_done"), sem("s_out")
        soft_x, soft_e, soft_done, slot_tp, slot_done = (sem(n) for n in ("soft_x", "soft_e", "soft_done", "slot_tp", "slot_done"))
        oh_done, g_done, g_out = sem("oh_done"), sem("g_done"), sem("g_out")
        g_stored = [sem(f"g_stored{b}") for b in range(2)]
        ga_ld = [sem(f"ga_ld{r}") for r in range(2)]
        g_ld = [sem(f"g_ld{r}") for r in range(2)]
        h_mul, h_hi_done, h_lo_done, v_done = (sem(n) for n in ("h_mul", "h_hi_done", "h_lo_done", "v_done"))
        peer_done = sem("peer_done")
        pk_hi, pk_lo, x_st = sem("pk_hi"), sem("pk_lo"), sem("x_st")
        rt_mm, rt_x, rt_e, rt_pick, rt_rank, rt_dest = (sem(n) for n in ("rt_mm", "rt_x", "rt_e", "rt_pick", "rt_rank", "rt_dest"))
        rt_all = sem("rt_all")
        rt_tok, rt_sum, rt_row = sem("rt_tok"), sem("rt_sum"), sem("rt_row")
        xe_ld = [sem(f"xe_ld{p}") for p in range(2)]
        xe_tp, xe_hi, xe_lo = sem("xe_tp"), sem("xe_hi"), sem("xe_lo")
        moe_ld = w_ld + [sem(f"moe_ld{s}") for s in range(RING, MOE_RING // 2)]
        moe_mm = sem("moe_mm")
        sil_done, hid_mul, hid_hi, hid_lo, hid_tp, hid_c = (sem(n) for n in ("sil_done", "hid_mul", "hid_hi", "hid_lo", "hid_tp", "hid_c"))
        y_out = sem("y_out")
        y_stored = [sem(f"y_stored{p}") for p in range(2)]
        yg_ld = [sem(f"yg_ld{tb}") for tb in range(TB)]
        end_done = sem("end_done")

        F_P1 = 0
        F_QUERY = F_P1 + 2 * N_P1F
        F_CONV = F_QUERY + 2 * N_QUERY
        F_QC = F_CONV + 2 * N_CONV
        F_AO = F_QC + 2 * N_QC
        f_of = lambda n: F_QC + 2 * (n - C_QC)
        G_P1, G_WOUT, G_V2, G_WO2 = 0, 3, 5, 7
        ao_gate = lambda j: F_AO + max(2 * j, 1)
        ao_out = lambda j: F_AO + min(2 * j + 3, 2 * KT)
        UNITS = [(h, qb) for h in range(AH) for qb in range(TB)]

        def used(n):
            for c, k, f in ((C_P1F, N_P1F, F_P1), (C_QUERY, N_QUERY, F_QUERY), (C_CONV, N_CONV, F_CONV), (C_QC, N_QC, F_QC)):
                if c <= n < c + k:
                    return ft_done, f + 2 * (n - c) + 2
            if C_AO <= n < C_AO + N_AO:
                return ft_done, ao_out(n - C_AO)
            if n == C_KEYS:
                return used(n - RING)
            if C_U <= n < C_U + N_U:
                return u_done, 2 + 2 * (n - C_U) + 2
            if C_V <= n < C_V + N_V:
                return v_done, 2 + n - C_V + 1
            for c, k, g in ((C_P1T, N_P1T, G_P1), (C_WOUT, N_WOUT, G_WOUT), (C_V2, N_V2, G_V2), (C_WO2, N_WO2, G_WO2)):
                if c <= n < c + k:
                    at = g + (n - c) // 2 + 1
                    return (tok_done, TB * at) if (n - c) % 2 else (tok_half, at)

        PASS = N_MOE
        moe = lambda r, i, c: r * NE + 2 * i + c
        pairs_of = lambda r, i, c: r * (NE // 2) + i + c // 2

        def moe_loads(r, i, pair):
            before = C_MOE // RING if pair < RING else 0
            return 16 * (2 * (r * (PASS // MOE_RING) + i) + (before + 2))

        def wait(eng, semaphore, count):
            if not isinstance(count, int) or count > 0:
                eng.wait_ge(semaphore, count)

        def every_expert(first, step, last, looped=NE - 2):
            def one_pass(eng, r):
                first(r)
                with eng.Fori(0, looped // 2) as i:
                    for c in (1, 2):
                        step(r, i, c)
                last(r)
            return one_pass

        def more_passes(eng, one_pass, gather=None):
            eng.wait_ge(rt_dest, 1)
            with eng.If(eng.value_load(n_rows_i[0:1, 0:1], min_val=0, max_val=T) > CAP):
                with eng.Fori(1, PASSES) as r:
                    one_pass(eng, r)
                if gather:
                    gather(PASSES)
            if gather:
                with eng.Else():
                    gather(1)

        block = ctx.enter_context(nc.Block())

        @block.sync
        def _(sp):
            for tb in range(TB):
                sp.dma_start(res[:, tb, :], x_in[tb * P:(tb + 1) * P, :]).then_inc(x_ld[tb], 16)
            sp.dma_start(cols[:, :], cols_in).then_inc(cols_ld, 16)
            for n in range(RING):
                sp.dma_start(w_st[:, n, :], w_all[n]).then_inc(w_ld[n], 16)
            sp.dma_start(small, small_in).then_inc(small_ld, 16)
            with sp.Fori(1, C_MOE // RING) as i:
                for s in range(RING):
                    sp.wait_ge(w_lo_done, i * RING + (s + 1 - RING))
                    sp.dma_start(w_st[:, s, :], w_all[i * RING + s]).then_inc(w_ld[s], 16)

            def one_pass(eng, r):
                for s in range(MOE_RING):
                    if s < RING:
                        sp.wait_ge(w_lo_done, C_MOE + r * PASS + (s + 1 - RING))
                    elif not isinstance(r, int):
                        sp.wait_ge(w_lo_done, C_MOE + r * PASS + (s + 1 - MOE_RING))
                    elif s < RING + ARENA_SLOTS:
                        sp.wait_ge(mix_lo, KT)
                    elif s < MOE_RING - 2:
                        sp.wait_ge(rt_mm, 1)
                    else:
                        sp.wait_ge(pk_lo, TB)
                        for p in range(2):
                            sp.wait_ge(xe_ld[p], 16)
                    sp.dma_start(moe_st[s], w_all[C_MOE + s]).then_inc(moe_ld[s // 2], 16)
                with sp.Fori(1, PASS // MOE_RING) as i:
                    for s in range(MOE_RING):
                        sp.wait_ge(w_lo_done, C_MOE + r * PASS + i * MOE_RING + (s + 1 - MOE_RING))
                        if s % 2 == 0:
                            pair = (s // 2 - 2) % (MOE_RING // 2)
                            sp.wait_ge(moe_ld[pair], moe_loads(r, i if s >= 4 else i - 1, pair))
                        sp.dma_start(moe_st[s], w_all[C_MOE + i * MOE_RING + s]).then_inc(moe_ld[s // 2], 16)

            one_pass(sp, 0)
            more_passes(sp, one_pass)
            for tb in range(TB):
                sp.wait_ge(end_done, tb + 1)
                sp.dma_start(out[tb * P:(tb + 1) * P, :], xn[:, tb, :]).then_inc(out_st, 16)
            sp.wait_ge(out_st, 16 * TB)

        @block.gpsimd
        def _(pool):
            def load_row(n):
                if n >= 2:
                    pool.wait_ge(row_used, n - 1)
                pool.dma_start(row[:, n % 2, :], rows_in[n].to_broadcast([P, D])).then_inc(row_ld[n % 2], 16)

            load_row(0)
            pool.memset(ident[:, :], 0.0)
            pool.memset(ones[:, :], 1.0)
            pool.memset(eps[:, :], EPS)
            pool.memset(reset[:, :], 1.0)
            pool.memset(neg_gt[:, :], 0.0).then_inc(const_step, 1)
            pool.wait_ge(const_step, 1)
            pool.affine_select(out=ident[:, :], in_=ident[:, :], compare_op=ALU.not_equal, fill=1.0, base=0,
                               pattern=[[-1, P]], channel_multiplier=1)
            pool.affine_select(out=tri_le[:, :], in_=ones[:, :], compare_op=ALU.is_ge, fill=0.0, base=0,
                               pattern=[[1, P]], channel_multiplier=-1)
            pool.affine_select(out=tri_gt[:, :], in_=ones[:, :], compare_op=ALU.is_gt, fill=0.0, base=0,
                               pattern=[[-1, P]], channel_multiplier=1)
            pool.affine_select(out=neg_gt[:, :], in_=neg_gt[:, :], compare_op=ALU.is_ge, fill=NEG, base=0,
                               pattern=[[1, P]], channel_multiplier=-1)
            pool.memset(reset[:, :].rearrange("p (c i) -> p c i", i=GC)[:, :, 0:1], 0.0)
            pool.memset(xbc[:, :, 0:4], 0.0).then_inc(const_step, 1)
            pool.wait_ge(const_step, 2)
            pool.tensor_scalar(tri_neg[:, :], tri_le[:, :], -1.0, None, ALU.mult)
            pool.iota(iota_i[:, :], [[1, P]], base=0, channel_multiplier=0)
            pool.iota(tok_i[:, :], [[P, TB]], base=0, channel_multiplier=1)
            pool.memset(zero_i[:, :], 0)
            pool.tensor_copy(neg_gt_b[:, :], neg_gt[:, :])
            pool.tensor_copy(ident_b[:, :], ident[:, :]).then_inc(const_step, 1)
            pool.wait_ge(const_step, 3)
            pool.tensor_copy(iota_f[:, :], iota_i[:, :])
            pool.tensor_copy(tok_f[:, :], tok_i[:, :])
            pool.tensor_copy(iota_b[:, :], iota_i[:, :]).then_inc(const_done, 1)

            for n in range(1, 4):
                load_row(n)
            for r in range(2):
                pool.dma_start(first_st[:, r, 0, :], cols_in[:, 0:4]).then_inc(u_stored[r], 16)
                pool.dma_start(first_st[:, r, 1, :], cols_in[:, 0:4]).then_inc(g_stored[r], 16)
                pool.dma_start(first_st[:, r, 2, :], cols_in[:, 0:4]).then_inc(y_stored[r], 16)

            def store_activations(i, c):
                pool.wait_ge(u_out, 16 * i + 2 * c + 4)
                pool.dma_start(act_dram[i * 8 + c], u_st[:, c % 2, :, :].rearrange("p j t -> p (j t)")).then_inc(u_stored[c % 2], 16)

            with pool.Fori(0, 4) as i:
                for c in range(8):
                    store_activations(i, c)
            def store_gates(i, b):
                pool.wait_ge(g_out, 4 + 2 * (16 * (i - 4) + 8 * b + 8))
                pool.dma_start(gate_dram[(i - 4) * 2 + b], g_st[:, b, :, :]).then_inc(g_stored[b], 16)

            with pool.Fori(4, 7) as i:
                for c in range(8):
                    store_activations(i, c)
                    if c % 4 == 3:
                        store_gates(i, c // 4)
            for c in range(8):
                store_activations(7, c)
                if c == 3:
                    store_gates(7, 0)
            pool.wait_ge(g_stored[0], 16 * 5)
            pool.wait_ge(g_stored[1], 16 * 4)

            def load_experts(i, c):
                n = i * 4 + c
                pool.dma_start(ga_in[:, c % 2, :, :].rearrange("p j t -> p (j t)"), act_dram[n]).then_inc(ga_ld[c % 2], 16)
                pairs = gate_dram.rearrange("g p (n j) t -> n p g (j t)", j=2)
                pool.dma_start(g_in[:, c % 2, :, :, :].rearrange("p g j t -> p g (j t)"), pairs[n]).then_inc(g_ld[c % 2], 16)

            load_experts(0, 0)
            load_experts(0, 1)
            for r in range(2):
                pool.wait_ge(u_stored[r], 16 * (N_U // 2 + 1))
            with pool.Fori(0, N_V // 4 - 1) as i:
                for c in range(2, 6):
                    pool.wait_ge(h_mul, i * 4 + (c - 1))
                    load_experts(i, c)
            for c in range(2, 4):
                pool.wait_ge(h_mul, N_V - 4 + c - 1)
                load_experts(N_V // 4 - 1, c)
            load_row(4)
            load_row(5)
            for tb in range(TB):
                pool.wait_ge(xn_done, 5 * TB + tb + 1)
                pool.tensor_copy(pk[:, tb, 0, :], xn[:, tb, :]).then_inc(pk_hi, 1)
                pool.wait_ge(pk_hi, tb + 1)
                pool.tensor_tensor(pk[:, tb, 1, :], xn[:, tb, :], pk[:, tb, 0, :], ALU.subtract).then_inc(pk_lo, 1)
                pool.wait_ge(pk_lo, tb + 1)
                pool.dma_start(x_dram[tb * P:(tb + 1) * P, :], pk[:, tb, :, :].rearrange("p a d -> p (a d)")).then_inc(x_st, 16)
            pool.wait_ge(x_st, 16 * TB)

            def gather(p):
                pool.indirect_dma_start(x_g[0:CAP, p, :, :].rearrange("p a d -> p (a d)"), None, x_dram,
                                        bass.IndirectOffsetOnAxis(ap=idx[0:CAP, p:p + 1], axis=0)).then_inc(xe_ld[p], 16)

            def next_rows(i, c):
                pool.tensor_tensor(idx[0:CAP, c % 2:c % 2 + 1], row_i[0:CAP, bass.ds(2 * i + c, 1)], zero_i[0:CAP, 0:1], ALU.add)

            def gather_next(r, i, c):
                pool.wait_ge(xe_tp, 2 * moe(r, i, c) + 2)
                next_rows(i, c + 1)
                gather(c % 2)
                pool.drain()

            def store(r, i, c):
                pool.wait_ge(y_out, moe(r, i, c) + 2)
                pool.dma_start(y_dram[moe(r, i, c)], y_st[0:CAP, c % 2, :]).then_inc(y_stored[c % 2], 16)

            pool.memset(row_i[:, NE:NE + 1], 0)

            def first(r):
                pool.wait_ge(rt_row, r + 1)
                pool.tensor_tensor(idx[0:CAP, 0:2], row_i[0:CAP, 0:2], zero_i[0:CAP, :], ALU.add)
                pool.drain()
                gather(0)
                gather(1)
                pool.drain()
                next_rows(0, 2)
                pool.drain()
                gather_next(r, 0, 2)

            def step(r, i, c):
                gather_next(r, i, c + 2)
                store(r, i, c - 1)

            def last(r):
                step(r, 0, NE - 3)
                for e in range(NE - 3, NE):
                    store(r, 0, e)
                for p in range(2):
                    pool.wait_ge(y_stored[p], 16 * (pairs_of(r, 0, NE) + 1))

            one_pass = every_expert(first, step, last, NE - 4)
            one_pass(pool, 0)

            def gather_outputs(passes):
                for tb in range(TB):
                    for s in range(2):
                        pool.indirect_dma_start(y_g[:, tb, s, :], None, y_dram[0:passes * NE].rearrange("q r d -> (q r) d"),
                                                bass.IndirectOffsetOnAxis(ap=to_y[:, s, tb:tb + 1], axis=0)).then_inc(yg_ld[tb], 16)

            more_passes(pool, one_pass, gather_outputs)

        @block.tensor
        def _(pe):
            def chunk(n):
                pe.wait_ge(w_lo_done, n + 1)

            def mm3(dst, l_hi, l_lo, r_hi, r_lo, start, stop):
                pe.matmul(dst, l_hi, r_hi, start=start, stop=False)
                pe.matmul(dst, l_hi, r_lo, start=False, stop=False)
                return pe.matmul(dst, l_lo, r_hi, start=False, stop=stop)

            def feature_tile(f, n, half, r_hi, r_lo, bank=None):
                chunk(n)
                if bank is None and f >= 4:
                    pe.wait_ge(ft_out, f - 3)
                dst = ps[:, 4 + f % 4 if bank is None else bank, :]
                for kt in range(KT):
                    w = slice(half * D + kt * P, half * D + (kt + 1) * P)
                    last = mm3(dst, w_hi[:, n % RING, w], w_lo[:, n % RING, w], r_hi[:, kt, :], r_lo[:, kt, :],
                               kt == 0, kt == KT - 1)
                last.then_inc(ft_done, 1)

            def token_tiles(n, bank, l_hi, l_lo, split=None, before=0):
                for part in range(2):
                    if split is not None:
                        pe.wait_ge(split, before + (part + 1) * KT // 2)
                    chunk(n + part)
                    for tb in range(TB):
                        rows = slice(tb * P, (tb + 1) * P)
                        for k in range(4):
                            kt = part * 4 + k
                            w = slice(k * 512, (k + 1) * 512)
                            last = mm3(ps[:, bank + tb, :], l_hi[:, kt, rows], l_lo[:, kt, rows],
                                       w_hi[:, (n + part) % RING, w], w_lo[:, (n + part) % RING, w],
                                       kt == 0, kt == KT - 1)
                        if part == 1:
                            last.then_inc(tok_done, 1)
                        elif tb == TB - 1:
                            last.then_inc(tok_half, 1)

            def transpose_rows(use, by_block=True):
                for n in range(KT):
                    g = KT * use + n
                    if g >= 2:
                        pe.wait_ge(tp_lo, g - 1)
                    for m in range(4):
                        tb, kt = (n // 2, (n % 2) * 4 + m) if by_block else (m, n)
                        if kt == 0:
                            pe.wait_ge(xn_done, TB * use + tb + 1)
                        last = pe.transpose(ps[:, g % 2, m * P:(m + 1) * P], xn[:, tb, kt * P:(kt + 1) * P], ident[:, :])
                    last.then_inc(tp_done, 1)

            pe.wait_ge(const_done, 1)
            transpose_rows(0)
            pe.wait_ge(tp_lo, KT)
            pe.wait_ge(small_done, 1)
            for kt in range(KT):
                w = slice(O_IN + kt * SM_IN, O_IN + (kt + 1) * SM_IN)
                last = mm3(ps[0:SM_IN, 2, :], small_hi[:, w], small_lo[:, w], a_hi[:, kt, :], a_lo[:, kt, :], kt == 0, kt == KT - 1)
            last.then_inc(sm_done, 1)
            for m in range(2 * N_P1F):
                feature_tile(F_P1 + m, C_P1F + m // 2, m % 2, a_hi, a_lo)
                if m == 1:
                    pe.wait_ge(sm_out, 1)
                    for j in range(2):
                        pe.matmul(ps[:, j, :], small[0:GRANK, O_G2 + j * P:O_G2 + (j + 1) * P], sm[0:GRANK, :],
                                  start=True, stop=True).then_inc(gate_mm, 1)
                if m == 4:
                    pe.wait_ge(dt_done, 1)
                    for tb in range(TB):
                        for s in range(2):
                            last = pe.transpose(ps[:, 3, (tb * 2 + s) * SH:(tb * 2 + s + 1) * SH],
                                                dtm[DT0:DT0 + SH, 2 + s, tb * P:(tb + 1) * P], ident[DT0:DT0 + SH, DT0:DT0 + SH])
                    last.then_inc(dta_tp, 1)
                if m == 6:
                    pe.wait_ge(dta_c, 1)
                    for s, tri in enumerate((tri_le, tri_gt, ones)):
                        last = pe.matmul(ps[:, 3, s * TB * SH:(s + 1) * TB * SH].rearrange("p (t h) -> p t h", t=TB), tri[:, :], dta[:, :, 1, :], start=True, stop=True)
                    last.then_inc(cum_mm, 1)
            pe.wait_ge(gate_x, 2)
            pe.wait_ge(cum_exp, 1)
            token_tiles(C_P1T, 0, a_hi, a_lo)
            pe.wait_ge(ft_out, F_P1 + 2 * N_P1F)
            for j in range(2):
                pe.wait_ge(gla_qk, j + 1)
                for tb in range(TB):
                    last = pe.transpose(ps[:, 6 + j, tb * P:(tb + 1) * P], k_end[:, j, tb * P:(tb + 1) * P], ident[:, :])
                last.then_inc(gla_kt, 1)
            for hh in range(2):
                for c in range(NGC):
                    for j in range(2):
                        rows, t0 = slice(hh * GDK, (hh + 1) * GDK), c * GC
                        last = pe.matmul(ps[(c % 2) * GC:(c % 2 + 1) * GC, 4 + hh, ((c // 2) * 2 + j) * GC:((c // 2) * 2 + j + 1) * GC],
                                         qk[rows, 2 + j, t0:t0 + GC], qk[rows, j, t0:t0 + GC], start=True, stop=True)
                last.then_inc(gla_att, 1)
            pe.wait_ge(tok_out, TB)
            token_tiles(C_P1T + 2, 0, a_hi, a_lo)
            pe.wait_ge(gla_ktc, 2)
            pe.wait_ge(gla_attc, 2)
            for j in range(2):
                for c in range(NGC):
                    rows = slice((c % 2) * GC, (c % 2 + 1) * GC)
                    for hh in range(2):
                        h = 2 * j + hh
                        last = pe.matmul(ps[hh * GDK:(hh + 1) * GDK, 4 + j * 2 + c % 2, (c // 2) * GDV:(c // 2 + 1) * GDV],
                                         k_endT[rows, j, c // 2, hh * GDK:(hh + 1) * GDK],
                                         vT[rows, c // 2, h * GDV:(h + 1) * GDV], start=True, stop=True)
                last.then_inc(gla_st, 1)
            pe.wait_ge(tok_out, 2 * TB)
            token_tiles(C_P1T + 4, 0, a_hi, a_lo)
            pe.wait_ge(gla_S, 1)
            pe.wait_ge(tok_out, 3 * TB)
            for tb in range(TB):
                b = (tb % 2) * 3
                if tb >= 2:
                    pe.wait_ge(gla_od, tb - 1)
                for par in range(2):
                    rows, c = slice(par * GC, (par + 1) * GC), 2 * tb + par
                    for h in range(GH):
                        j, hh = h // 2, h % 2
                        pe.matmul(ps[rows, b, h * GDV:(h + 1) * GDV], att_s[rows, hh, 2 * tb + j, :],
                                  vT[rows, tb, h * GDV:(h + 1) * GDV], start=True, stop=True)
                        dk = slice(hh * GDK, (hh + 1) * GDK)
                        last = pe.matmul(ps[rows, b + 1 + hh, j * GDV:(j + 1) * GDV], qk[dk, j, c * GC:(c + 1) * GC],
                                         s_gla[dk, j, c, :], start=True, stop=True)
                last.then_inc(gla_o, 1)

            pe.wait_ge(silu_done, 6)
            for tb in range(TB + 1):
                if tb >= 2:
                    pe.wait_ge(xt_c, tb - 1)
                for m in range(4):
                    src = xc[:, m, tb * P:(tb + 1) * P] if tb < TB else xc[:, 4, m * P:(m + 1) * P]
                    last = pe.transpose(ps[:, 6 + tb % 2, m * P:(m + 1) * P], src, ident[:, :])
                last.then_inc(xt_tp, 1)
            pe.wait_ge(xt_c, TB + 1)
            pe.wait_ge(gla_od, TB)
            for tb in range(TB):
                t0 = slice(tb * P, (tb + 1) * P)
                if tb >= 1:
                    pe.wait_ge(ssd_W, 2 * tb)
                for g in range(SG):
                    for jj in range(SJ):
                        a_col = dta[:, tb, 1, g * SJ + jj:g * SJ + jj + 1].to_broadcast([P, P])
                        dst = ps[:, g, jj * P:(jj + 1) * P]
                        pe.matmul(dst, a_col, tri_le[:, :], start=True, stop=False)
                        pe.matmul(dst, tri_neg[:, :], a_col, start=False, stop=False)
                        pe.matmul(dst, ident_b[:, :], neg_gt_b[:, :], start=False, stop=True)
                    n = slice(g * SN, (g + 1) * SN)
                    pe.matmul(ps[:, 2 + g, 0:P], xc[n, 4, t0], xc[n, 5, t0], start=True, stop=True).then_inc(ssd_mm, 1)
                pe.wait_ge(xd_done, tb + 1)
                if tb >= 1:
                    pe.wait_ge(ssd_S, tb)
                for g in range(SG):
                    last = pe.matmul(ps[g * SN:(g + 1) * SN, 6, 0:SJ * SP_], bt[:, tb, g * SN:(g + 1) * SN],
                                     xdte[:, tb, g * SJ * SP_:(g + 1) * SJ * SP_], start=True, stop=True)
                last.then_inc(ssd_st, 1)
                if tb == 0:
                    pe.wait_ge(ssd_S, 1)
                else:
                    pe.wait_ge(ssd_yd, tb)
                for g in range(SG):
                    n = slice(g * SN, (g + 1) * SN)
                    pe.matmul(ps[:, 7 - 3 * g, 0:SJ * SP_], xc[n, 5, t0], s_ssd[n, tb, :], start=True, stop=True)
                pe.wait_ge(ssd_W, 2 * tb + 2)
                for h in range(SH):
                    last = pe.matmul(ps[:, 5, h * SP_:(h + 1) * SP_], w_s[:, h // SJ, (h % SJ) * P:(h % SJ + 1) * P],
                                     xdt[:, tb, h * SP_:(h + 1) * SP_], start=True, stop=True)
                last.then_inc(ssd_y, 1)

            pe.wait_ge(ssd_yd, TB)
            transpose_rows(1, by_block=False)
            token_tiles(C_WOUT, 4, a_hi, a_lo, tp_lo, KT)
            token_tiles(C_WOUT + 2, 0, a_hi, a_lo)

            transpose_rows(2)
            pe.wait_ge(tp_lo, 3 * KT)
            for m in range(2 * N_QUERY):
                feature_tile(F_QUERY + m, C_QUERY + m // 2, m % 2, a_hi, a_lo)

            def expert_tile(i, c, t):
                n = C_U + 8 * i + c
                if t == 0:
                    chunk(n)
                pe.wait_ge(u_out, 16 * i + 2 * c + t + 1)
                for kt in range(KT):
                    w = slice(t * D + kt * P, t * D + (kt + 1) * P)
                    last = mm3(ps[:, t, :], w_hi[:, c % RING, w], w_lo[:, c % RING, w], a_hi[:, kt, :], a_lo[:, kt, :],
                               kt == 0, kt == KT - 1)
                last.then_inc(u_done, 1)

            pe.wait_ge(ft_out, F_QUERY + 2 * N_QUERY)
            pe.drain().then_inc(u_done, 2)
            with pe.Fori(0, 4) as i:
                for c in range(8):
                    pe.wait_ge(s_out, 8 * i + c + 1)
                    for half in range(2):
                        q = 2 * c + half
                        rows = bass.ts(i, P)
                        last = mm3(ps[:, 2 + c % 2, half * PK:(half + 1) * PK], q_hi[:, q, rows], q_lo[:, q, rows],
                                   keys_hi[:, q, :], keys_lo[:, q, :], True, True)
                    last.then_inc(s_done, 1)
                    for t in range(2):
                        expert_tile(i, c, t)
            pe.wait_ge(soft_done, 1)
            for a, src in enumerate((key1, key2, score)):
                for tb in range(TB):
                    last = pe.transpose(ps[:, 4 + a, tb * P:(tb + 1) * P], src[:, tb * P:(tb + 1) * P], ident[:, :])
            last.then_inc(slot_tp, 1)
            pe.wait_ge(slot_done, 1)
            pe.drain().then_inc(g_done, 4)
            with pe.Fori(4, 8) as i:
                for c in range(8):
                    for t in range(2):
                        expert_tile(i, c, t)
                        at = 2 * c + t
                        pe.wait_ge(oh_done, 16 * (i - 4) + at + 1)
                        pe.wait_ge(g_out, 2 * (16 * (i - 4) + at) + 2)
                        for r in range(8):
                            dst = ps[:, 2 + 2 * (at % 2) + r // 4, (r % 4) * PK:(r % 4 + 1) * PK]
                            pe.matmul(dst, oh_b[:, at % 2, r, :], oh_a[:, at % 2, r, 0, :], start=True, stop=False)
                            last = pe.matmul(dst, oh_b[:, at % 2, r, :], oh_a[:, at % 2, r, 1, :], start=False, stop=True)
                            if r % 4 == 3:
                                last.then_inc(g_done, 1)
            pe.wait_ge(u_out, 2 + 2 * N_U)
            pe.wait_ge(g_out, 4 + 2 * 64)
            for b in range(8):
                pe.matmul(ps[:, b, :], ident[:, :], res[:, b // 2, (b % 2) * 512:(b % 2 + 1) * 512], start=True, stop=False)
            pe.drain().then_inc(v_done, 2)

            def values(i, c, done=None):
                chunk(C_V + 4 * i + c)
                pe.wait_ge(h_lo_done, 4 * i + c + 1)
                for tb in range(TB):
                    rows = slice(tb * P, (tb + 1) * P)
                    for j in range(2):
                        for part in range(2):
                            w = slice(j * D + part * 512, j * D + (part + 1) * 512)
                            last = mm3(ps[:, 2 * tb + part, :], h_hi[:, c % 2, j, rows], h_lo[:, c % 2, j, rows],
                                       w_hi[:, c, w], w_lo[:, c, w], False, done is not None and j == 1)
                            if done is not None and j == 1:
                                last.then_inc(done, 1)
                return last

            with pe.Fori(0, N_V // 4 - 1) as i:
                for c in range(4):
                    values(i, c).then_inc(v_done, 1)
            for c in range(3):
                values(N_V // 4 - 1, c).then_inc(v_done, 1)
            values(N_V // 4 - 1, 3, peer_done)
            pe.drain().then_inc(v_done, 1)

            transpose_rows(3)
            pe.wait_ge(tp_lo, 4 * KT)
            for kt in range(KT):
                w = slice(O_F + kt * SM_F, O_F + (kt + 1) * SM_F)
                last = mm3(ps[0:SM_F, 2, :], small_hi[:, w], small_lo[:, w], a_hi[:, kt, :], a_lo[:, kt, :], kt == 0, kt == KT - 1)
            last.then_inc(f_mm, 1)
            for m in range(2 * N_CONV):
                feature_tile(F_CONV + m, C_CONV + m // 2, m % 2, a_hi, a_lo)
            token_tiles(C_V2, 0, a_hi, a_lo)
            pe.wait_ge(ft_out, F_CONV + 2 * N_CONV)
            token_tiles(C_V2 + 2, 4, a_hi, a_lo)

            def tile_between(j, step):
                tile, kt = (step // KT if j + 1 < AH // 2 else 2 + step // KT), step % KT
                n, half = (CHUNK_QK(j + 1) if tile < 2 else CHUNK_CO(j)), tile % 2
                r_hi, r_lo = (c_hi, c_lo) if tile == 3 else (a_hi, a_lo)
                if kt == 0:
                    chunk(n)
                    if tile >= 2 and j + 1 < AH // 2:
                        pe.wait_ge(qk_out, 2 * (j + 1) + half + 1)
                    elif j:
                        pe.wait_ge(m1_done if half else sg_done, j)
                    if (j, tile) == (0, 3):
                        pe.wait_ge(cv_lo, KT)
                w = slice(half * D + kt * P, half * D + (kt + 1) * P)
                last = mm3(ps[:, 6 + half, :], w_hi[:, n % RING, w], w_lo[:, n % RING, w], r_hi[:, kt, :], r_lo[:, kt, :],
                           kt == 0, kt == KT - 1)
                if kt == KT - 1:
                    last.then_inc(ft_done, 1)

            pe.wait_ge(tok_out, TB * (G_V2 - 2 + 2))
            pe.wait_ge(f_cum, 1)
            for half in range(2):
                feature_tile(F_QC + half, CHUNK_QK(0), half, a_hi, a_lo, bank=6 + half)
            score_bank = (0, 1, 5)
            for u in range(len(UNITS) + 3):
                if u < len(UNITS):
                    h, qb = UNITS[u]
                    j, hh, n = h // 2, h % 2, (qb + 1) * P
                    if (hh, qb) == (0, 0):
                        pe.wait_ge(qk_out, 2 * j + 2)
                    if u >= 3:
                        pe.wait_ge(at_p, u - 2)
                    bank = score_bank[u % 3]
                    dst = ps[:, bank, 0:n]
                    for keys in (k_hi, k_lo):
                        pe.matmul(dst, q_s[:, j % 2, hh, qb * P:n], keys[:, j % 2, hh, 0:n], start=keys is k_hi, stop=False)
                    pe.matmul(dst, head_b[:, h:h + 1].to_broadcast([P, P]), cum_b[:, 0:n], start=False, stop=False)
                    pe.matmul(ps[:, bank, qb * P:n], neg_gt_b[:, :], ident_b[:, :], start=False, stop=True).then_inc(at_s, 1)
                    steps = 4 if j + 1 < AH // 2 else 2
                    for step in range(steps):
                        tile_between(j, steps * (hh * TB + qb) + step)
                if 2 <= u < len(UNITS) + 2:
                    v = u - 2
                    pe.wait_ge(at_p, v + 1)
                    if v >= 2:
                        pe.wait_ge(at_tc, v - 1)
                    for kb in range(UNITS[v][1] + 1):
                        last = pe.transpose(ps[:, 2 + v % 2, kb * P:(kb + 1) * P], p_s[v % 3][:, kb * P:(kb + 1) * P], ident[:, :])
                    last.then_inc(at_t, 1)
                if u >= 3:
                    v = u - 3
                    h, qb = UNITS[v]
                    pe.wait_ge(at_tc, v + 1)
                    if v >= 1:
                        pe.wait_ge(at_out, v)
                    for kb in range(qb + 1):
                        last = pe.matmul(ps[:, 4, 0:ADH], pT_s[:, v % 2, kb, :], v_s[:, kb, h * ADH:(h + 1) * ADH],
                                         start=kb == 0, stop=kb == qb)
                    last.then_inc(at_o, 1)
            pe.wait_ge(sg_done, KT)
            def gate_tile(j):
                feature_tile(ao_gate(j) - 1, C_AO + j, 0, a_hi, a_lo, bank=6 - 2 * (j % 2))

            gate_tile(0)
            transpose_rows(4)
            pe.wait_ge(at_out, len(UNITS))
            gate_tile(1)
            pe.wait_ge(tp_lo, 5 * KT)
            pe.wait_ge(m1_done, KT)
            for j in range(KT):
                if 1 <= j < KT - 1:
                    pe.wait_ge(sg_done, KT + j)
                    gate_tile(j + 1)
                if j >= 2:
                    pe.wait_ge(mix_done, j - 1)
                feature_tile(ao_out(j) - 1, C_AO + j, 1, c_hi, c_lo, bank=7 - 2 * (j % 2))
            token_tiles(C_WO2, 0, m_split[:, :, 0, :], m_split[:, :, 1, :], mix_lo)
            token_tiles(C_WO2 + 2, 4, m_split[:, :, 0, :], m_split[:, :, 1, :])

            pe.drain().then_inc(moe_mm, RING)
            transpose_rows(5)
            pe.wait_ge(tp_lo, 6 * KT)
            for tb in range(TB):
                for kt in range(KT):
                    rows, w = slice(tb * P, (tb + 1) * P), slice(O_R + kt * SM_R, O_R + (kt + 1) * SM_R)
                    last = mm3(ps[:, 2, tb * SM_R:(tb + 1) * SM_R], a_hi[:, kt, rows], a_lo[:, kt, rows], small_hi[:, w], small_lo[:, w],
                               kt == 0, kt == KT - 1)
            last.then_inc(rt_mm, 1)
            pe.wait_ge(rt_pick, 1)
            pe.matmul(ps[:, 3, 0:TB * NE].rearrange("p (t e) -> p t e", e=NE), tri_le[:, :], e_any, start=True, stop=False)
            for b in range(TB - 1):
                last = pe.matmul(ps[:, 3, (b + 1) * NE:TB * NE].rearrange("p (t e) -> p t e", e=NE), ones[:, :],
                                 e_any[:, b, :].unsqueeze(1).to_broadcast([P, TB - 1 - b, NE]), start=False, stop=b == TB - 2)
            last.then_inc(rt_rank, 1)
            for b in range(TB):
                last = pe.matmul(ps[:, 4, 0:NE], ones[:, :], e_any[:, b, :], start=b == 0, stop=b == TB - 1)
            last.then_inc(rt_all, 1)
            pe.drain().then_inc(xe_tp, 4)

            def expert_rows(r, i, c):
                pe.wait_ge(xe_ld[c % 2], 16 * (pairs_of(r, i, c) + 1))
                wait(pe, xe_hi, moe(r, i, c))
                wait(pe, xe_lo, moe(r, i, c))
                for a in range(2):
                    for kt in range(KT):
                        last = pe.matmul(ps[:, 6 + a, kt * CAP:(kt + 1) * CAP], x_g[0:CAP, c % 2, a, kt * P:(kt + 1) * P],
                                         ident_b[0:CAP, 0:CAP], start=True, stop=True)
                    last.then_inc(xe_tp, 1)

            def expert_in(r, i, c, k, bank):
                for part in range(2):
                    chunk(C_MOE + r * PASS + 12 * i + (k + part))
                    for j in range(4):
                        kt, w = part * 4 + j, slice(j * DE, (j + 1) * DE)
                        last = mm3(ps[0:CAP, bank, :], xeT[:, c % 2, 0, kt, :], xeT[:, c % 2, 1, kt, :],
                                   w_hi[:, (k + part) % RING, w], w_lo[:, (k + part) % RING, w], kt == 0, kt == KT - 1)
                    last.then_inc(moe_mm, 1)

            def expert_gate(r, i, c):
                wait(pe, sil_done, moe(r, i, c))
                pe.wait_ge(xe_hi, moe(r, i, c) + 1)
                pe.wait_ge(xe_lo, moe(r, i, c) + 1)
                expert_in(r, i, c, 6 * c - 2 if c else 0, 0)

            def expert_up(r, i, c):
                wait(pe, hid_mul, moe(r, i, c))
                expert_in(r, i, c, 6 * c + 2, 1)

            def expert_hidden(r, i, c):
                pe.wait_ge(hid_lo, moe(r, i, c) + 1)
                for a in range(2):
                    for f in range(DE // P):
                        n = a * (DE // P) + f
                        last = pe.matmul(ps[:, 4, n * CAP:(n + 1) * CAP], hid_b[0:CAP, a, f * P:(f + 1) * P], ident_b[0:CAP, 0:CAP],
                                         start=True, stop=True)
                last.then_inc(hid_tp, 1)

            def expert_down(r, i, c, k):
                pe.wait_ge(hid_c, moe(r, i, c) + 1)
                pe.wait_ge(y_out, moe(r, i, c) + 1)
                for part in range(2):
                    chunk(C_MOE + r * PASS + 12 * i + (k + part))
                    for half in range(2):
                        for j in range(2):
                            f, w = part * 2 + j, slice(j * D + half * 512, j * D + (half + 1) * 512)
                            last = mm3(ps[0:CAP, 2 + half, :], hidT[:, 0, f, :], hidT[:, 1, f, :],
                                       w_hi[:, (k + part) % RING, w], w_lo[:, (k + part) % RING, w], f == 0, f == DE // P - 1)
                    last.then_inc(moe_mm, 1)

            def first(r):
                pe.wait_ge(rt_tok, r + 1)
                for n in range(2 * TB):
                    last = pe.matmul(ps[0:CAP, 5, 0:NE], row_one[:, n // TB, n % TB, :], tok_e[:, n // TB, n % TB, :], start=n == 0, stop=n == 2 * TB - 1)
                last.then_inc(rt_sum, 1)
                expert_rows(r, 0, 0)
                expert_gate(r, 0, 0)
                expert_rows(r, 0, 1)
                expert_up(r, 0, 0)

            def step(r, i, c, more=True):
                expert_gate(r, i, c)
                expert_hidden(r, i, c - 1)
                if more:
                    expert_rows(r, i, c + 1)
                expert_down(r, i, c - 1, 6 * c)
                expert_up(r, i, c)

            def last(r):
                step(r, 0, NE - 1, more=False)
                expert_hidden(r, 0, NE - 1)
                expert_down(r, 0, NE - 1, 6 * NE - 2)

            one_pass = every_expert(first, step, last)
            one_pass(pe, 0)
            more_passes(pe, one_pass)

        @block.scalar
        def _(act):
            split = [0]

            def hi(n, dst=None):
                act.wait_ge(w_ld[n % RING], 16 * (n // RING + 1))
                if n >= RING:
                    act.wait_ge(*used(n - RING))
                dst = w_hi[:, n % RING, :] if n != C_KEYS else keys_hi.rearrange("p q k -> p (q k)")
                act.activation(dst, w_st[:, n % RING, :], ACT.Copy).then_inc(w_hi_done, 1)

            def ahead(n):
                while split[0] <= min(n + AHEAD, C_MOE - 1):
                    hi(split[0])
                    split[0] += 1

            def norm(use, tb, ready, count, src=None):
                act.wait_ge(ready, count)
                act.activation(xn[:, tb, :], res[:, tb, :] if src is None else src, ACT.Square, accum_out=ss[:, tb:tb + 1])
                act.drain()
                act.activation(sd[:, tb:tb + 1], ss[:, tb:tb + 1], ACT.Sqrt, scale=1.0 / D, bias=eps[:, :]).then_inc(sd_done, 1)

            def transposed(use, weight=None, dst=a_hi, blocks=range(TB)):
                for n in range(2 * blocks[0], 2 * blocks[-1] + 2):
                    act.wait_ge(tp_done, KT * use + n + 1)
                    if weight is None:
                        act.activation(dst[:, (n % 2) * 4:(n % 2) * 4 + 4, (n // 2) * P:(n // 2 + 1) * P],
                                       ps[:, n % 2, :].rearrange("p (k t) -> p k t", k=4), ACT.Copy).then_inc(tp_hi, 1)
                    else:
                        act.activation(dst[:, n, :], ps[:, n % 2, :], ACT.Copy, scale=weight(n)).then_inc(tp_hi, 1)

            act.wait_ge(const_done, 1)
            for tb in range(TB):
                if tb == TB - 1:
                    transposed(0, blocks=[0])
                norm(0, tb, x_ld[tb], 16)
            ahead(-AHEAD)
            transposed(0, blocks=range(1, TB))
            ahead(-1)
            act.wait_ge(small_ld, 16)
            act.activation(small_hi[:, :], small[:, 0:N_SPLIT], ACT.Copy).then_inc(small_hi_done, 1)
            act.wait_ge(cols_ld, 16)
            act.wait_ge(sm_done, 1)
            act.activation(sm[0:SM_IN, :], ps[0:SM_IN, 2, :], ACT.Copy).then_inc(sm_out, 1)
            d = slice(DT0, DT0 + SH)
            for m in range(2 * N_P1F):
                ahead(C_P1F + m // 2)
                act.wait_ge(ft_done, F_P1 + m + 1)
                bank = ps[:, 4 + (F_P1 + m) % 4, :]
                if m < 4:
                    act.activation(qk[:, m, :], bank, ACT.Copy, scale=GDK ** -0.5 if m < 2 else 1.0).then_inc(ft_out, 1)
                else:
                    act.activation(xbc[:, m - 4, 4:], bank, ACT.Copy).then_inc(ft_out, 1)
                if m == 2:
                    act.wait_ge(dt_x, 1)
                    act.activation(dtm[d, 1, :], dtm[d, 0, :], ACT.Abs)
                    act.wait_ge(gate_x, 2)
                    for j in range(2):
                        act.activation(e_pos[:, j, :], g_cum[:, j, :], ACT.Abs)
                    act.activation(ea[d, 0:1], col("a_log")[d, :], ACT.Exp)
                    act.drain()
                    act.activation(dtm[d, 1, :], dtm[d, 1, :], ACT.Exp, scale=-1.0)
                    for j in range(2):
                        act.activation(e_pos[:, j, :], e_pos[:, j, :], ACT.Exp, scale=-1.0)
                    act.drain()
                    act.activation(dtm[d, 1, :], dtm[d, 1, :], ACT.Ln, bias=ones[d, 0:1]).then_inc(dt_ln, 1)
                    for j in range(2):
                        act.activation(e_pos[:, j, :], e_pos[:, j, :], ACT.Ln, bias=ones[:, 0:1]).then_inc(gate_ln, 1)
                if m == 5:
                    act.wait_ge(dta_tp, 1)
                    act.activation(dta.rearrange("p t s h -> p (t s h)"), ps[:, 3, 0:TB * 2 * SH], ACT.Copy).then_inc(dta_c, 1)
                if m == 7:
                    act.wait_ge(cum_mm, 1)
                    act.activation(ecum.rearrange("p s t h -> p (s t h)"), ps[:, 3, 0:3 * TB * SH], ACT.Exp).then_inc(cum_exp, 1)
                    for j in range(2):
                        act.wait_ge(gate_cum, j + 1)
                        act.activation(e_pos[:, j, :], g_cum[:, j, :], ACT.Exp)
                        act.activation(e_neg[:, j, :], g_cum[:, j, :], ACT.Exp, scale=-1.0)
                        act.activation(lg[:, j, :], lg[:, j, :], ACT.Exp).then_inc(gate_exp, 1)
            for g in range(3):
                ahead(C_P1T + 2 * g)
                if g == 1:
                    for j in range(2):
                        act.wait_ge(gla_kt, j + 1)
                        act.activation(k_endT[:, j, :, :].rearrange("p t d -> p (t d)"), ps[:, 6 + j, :], ACT.Copy).then_inc(gla_ktc, 1)
                    for m in range(6):
                        act.wait_ge(conv_done, m + 1)
                        act.activation(xc[:, m, :], xc[:, m, :], ACT.Silu).then_inc(silu_done, 1)
                act.wait_ge(tok_half, G_P1 + g + 1)
                ahead(C_P1T + 2 * g + 1)
                for tb in range(TB):
                    act.wait_ge(tok_done, TB * (G_P1 + g) + tb + 1)
                    if g == 0:
                        act.activation(vT[:, tb, :], ps[:, tb, :], ACT.Copy).then_inc(tok_out, 1)
                    else:
                        act.activation(xn[:, tb, (g - 1) * 512:g * 512], ps[:, tb, :], ACT.Silu).then_inc(tok_out, 1)
            for tb in range(TB):
                act.wait_ge(gla_o, tb + 1)
                if tb >= 2:
                    act.wait_ge(gla_y, tb - 1)
                act.activation(o_s[:, tb % 2, :], ps[:, (tb % 2) * 3, :], ACT.Copy).then_inc(gla_oc, 1)
                act.wait_ge(gla_od, tb + 1)
                for h in range(GH):
                    act.activation(y_t[:, 0, h * GDV:(h + 1) * GDV], o_s[:, tb % 2, h * GDV:(h + 1) * GDV], ACT.Square, accum_out=ss[:, h:h + 1])
                act.drain()
                act.activation(sd[:, 0:GH], ss[:, 0:GH], ACT.Sqrt, scale=1.0 / GDV, bias=eps[:, :]).then_inc(gla_sd, 1)
            for tb in range(TB + 1):
                act.wait_ge(xt_tp, tb + 1)
                dst = xt[:, tb, :] if tb < TB else bt.rearrange("p t n -> p (t n)")
                act.activation(dst, ps[:, 6 + tb % 2, :], ACT.Copy).then_inc(xt_c, 1)
            for tb in range(TB):
                for g in range(SG):
                    act.wait_ge(ssd_mm, 2 * tb + g + 1)
                    if tb >= 1:
                        act.wait_ge(ssd_W, 2 * (tb - 1) + g + 1)
                    act.activation(l_s[:, g, :], ps[:, g, :], ACT.Exp).then_inc(ssd_L, 1)
                act.wait_ge(ssd_yc, tb + 1)
                for g in range(SG):
                    gs = slice(GW + g * SJ * SP_, GW + (g + 1) * SJ * SP_)
                    act.activation(o_s[:, g, 0:SJ * SP_], xn[:, tb, gs], ACT.Square, accum_out=ss[:, tb * SG + g:tb * SG + g + 1])
                act.drain()
            act.activation(sd[:, 0:TB * SG], ss[:, 0:TB * SG], ACT.Sqrt, scale=1.0 / (SJ * SP_), bias=eps[:, :]).then_inc(ssd_sd, 1)
            transposed(1, lambda kt: col("gla_norm") if kt < 4 else col("ssd_norm", kt - 4))
            for g in range(2):
                ahead(C_WOUT + 2 * g)
                act.wait_ge(tok_half, G_WOUT + g + 1)
                ahead(C_WOUT + 2 * g + 1)

            for tb in range(TB):
                if tb == TB - 1:
                    transposed(2, blocks=[0])
                norm(1, tb, res_done, tb + 1)
            transposed(2, blocks=range(1, TB))
            for m in range(2 * N_QUERY):
                ahead(C_QUERY + m // 2)
                act.wait_ge(ft_done, F_QUERY + m + 1)
                act.activation(q_hi[:, m, :], ps[:, 4 + (F_QUERY + m) % 4, :], ACT.Copy).then_inc(q_hi_done, 1)
            ahead(C_KEYS)
            act.drain().then_inc(u_out, 2)

            def hi_in_loop(c, arrived, done, count):
                s = (c + AHEAD) % RING
                act.wait_ge(w_ld[s], arrived)
                act.wait_ge(done, count)
                act.activation(w_hi[:, s, :], w_st[:, s, :], ACT.Copy).then_inc(w_hi_done, 1)

            def gelu_tile(i, c, t):
                if t == 0:
                    act.wait_ge(u_stored[c % 2], 16 * (4 * i + c // 2 + 1))
                act.wait_ge(u_done, 16 * i + 2 * c + t + 3)
                act.activation(u_st[:, c % 2, t, :], ps[:, t, :], ACT.Gelu).then_inc(u_out, 1)

            with act.Fori(0, 4) as i:
                for c in range(8):
                    hi_in_loop(c, 16 * (C_U // RING + 2 * i + (c + AHEAD) // RING + 1), u_done, 16 * i + 2 * c + 2)
                    for t in range(2):
                        gelu_tile(i, c, t)
            act.wait_ge(soft_x, 1)
            act.activation(gate_t, gate_t, ACT.Exp).then_inc(soft_e, 1)
            act.drain().then_inc(g_out, 4)
            with act.Fori(4, 8) as i:
                for c in range(8):
                    hi_in_loop(c, 16 * (C_U // RING + 2 * i + (c + AHEAD) // RING + 1), u_done, 16 * i + 2 * c + 2)
                    for t in range(2):
                        gelu_tile(i, c, t)
                        at = 2 * c + t
                        b, first = at // 8, (at % 8) * 8
                        if at % 8 == 0:
                            act.wait_ge(g_stored[b], 16 * (i - 3))
                        for bank in range(2):
                            act.wait_ge(g_done, 2 * (16 * (i - 4) + at) + bank + 5)
                            tok = slice(first + bank * 4, first + bank * 4 + 4)
                            act.activation(g_st[:, b, :, tok].rearrange("p k t -> p t k"),
                                           ps[:, 2 + 2 * (at % 2) + bank, :].rearrange("p (t k) -> p t k", t=4), ACT.Copy).then_inc(g_out, 1)
            with act.Fori(0, N_V // 4) as i:
                for c in range(4):
                    act.wait_ge(h_mul, 4 * i + c + 1)
                    act.wait_ge(v_done, 4 * i + c + 1)
                    act.activation(h_hi[:, c % 2, :, :], h_f[:, c % 2, :, :], ACT.Copy).then_inc(h_hi_done, 1)
                    hi_in_loop(c, 16 * (C_V // RING + i + (c + AHEAD) // RING + 1), v_done, 4 * i + c + 2)
            split[0] = C_CONV + AHEAD

            for t in range(TB + 1):
                if t < TB:
                    norm(2, t, peer_done, 2 * t + 2, ps[:, 2 * t:2 * t + 2, :].rearrange("p b n -> p (b n)"))
                if t >= 1:
                    norm(3, t - 1, res2_done, t)
                if t >= 2:
                    transposed(3, blocks=[t - 2])
            transposed(3, blocks=[TB - 1])
            act.wait_ge(f_xs, 1)
            act.activation(f_e[0:AH, :], f_x[0:AH, :], ACT.Abs)
            act.drain()
            act.activation(f_e[0:AH, :], f_e[0:AH, :], ACT.Exp, scale=-1.0)
            act.drain()
            act.activation(f_e[0:AH, :], f_e[0:AH, :], ACT.Ln, bias=ones[0:AH, 0:1]).then_inc(f_ln, 1)

            def conv_hi(j):
                act.wait_ge(cv_mul, j + 1)
                act.activation(c_hi[:, j, :], cv_s[:, j % 2, :], ACT.Copy).then_inc(cv_hi, 1)

            for j in range(KT):
                for a, dst in enumerate((cu_s, cc_s, cb_s)):
                    m = 3 * j + a
                    ahead(C_CONV + m // 2)
                    act.wait_ge(ft_done, F_CONV + m + 1)
                    if j >= 2:
                        act.wait_ge(cv_mul, j - 1)
                    act.activation(dst[:, j % 2, :], ps[:, 4 + (F_CONV + m) % 4, :], ACT.Copy).then_inc(ft_out, 1)
                if j:
                    conv_hi(j - 1)
            conv_hi(KT - 1)
            for g in range(2):
                ahead(C_V2 + 2 * g)
                act.wait_ge(tok_half, G_V2 + g + 1)
                ahead(C_V2 + 2 * g + 1)
                for tb in range(TB):
                    act.wait_ge(tok_done, TB * (G_V2 + g) + tb + 1)
                    act.activation(v_s[:, tb, g * 512:(g + 1) * 512], ps[:, 4 * g + tb, :], ACT.Copy).then_inc(tok_out, 1)

            def copy_queries(j):
                act.wait_ge(ft_done, f_of(CHUNK_QK(j)) + 1)
                if j >= 2:
                    act.wait_ge(at_s, 8 * (j - 1))
                for hh in range(2):
                    rows = slice(hh * ADH, (hh + 1) * ADH)
                    last = act.activation(q_s[rows, j % 2, hh, :], ps[rows, 6, :], ACT.Copy, scale=ADH ** -0.5)
                last.then_inc(qk_hi, 1)

            def copy_keys(j):
                act.wait_ge(ft_done, f_of(CHUNK_QK(j)) + 2)
                for hh in range(2):
                    for half in range(2):
                        last = act.activation(k_hi[half * ADH:(half + 1) * ADH, j % 2, hh, :], ps[hh * ADH:(hh + 1) * ADH, 7, :], ACT.Copy)
                last.then_inc(qk_hi, 1)

            def conv_gate(j):
                act.wait_ge(ft_done, f_of(CHUNK_CO(j)) + 1)
                if j >= 2:
                    act.wait_ge(m1_done, j - 1)
                act.activation(sg_s[:, j % 2, :], ps[:, 6, :], ACT.Sigmoid).then_inc(sg_done, 1)

            act.wait_ge(f_cum, 1)
            copy_queries(0)
            copy_keys(0)
            for u, (h, qb) in enumerate(UNITS):
                n = (qb + 1) * P
                j, at = h // 2, u % 8
                act.wait_ge(at_max, u + 1)
                if u >= 3:
                    act.wait_ge(at_t, u - 2)
                if u >= 4:
                    act.wait_ge(at_out, u - 3)
                act.activation(p_s[u % 3][:, 0:n], ps[:, (0, 1, 5)[u % 3], 0:n], ACT.Exp, bias=n_max[:, u % 3:u % 3 + 1],
                               accum_out=r_sum[:, u % 4:u % 4 + 1]).then_inc(at_p, 1)
                if j + 1 < AH // 2:
                    if at == 0:
                        ahead(CHUNK_QK(j + 1))
                    if at == 2:
                        copy_queries(j + 1)
                    if at == 4:
                        copy_keys(j + 1)
                    if at == 5:
                        ahead(CHUNK_CO(j))
                    if at == 6:
                        conv_gate(j)
                else:
                    if at == 0:
                        ahead(CHUNK_CO(j))
                    if at == 4:
                        conv_gate(j)
            transposed(4, dst=c_hi)

            def mix_high(j):
                act.wait_ge(mix_done, j + 1)
                act.activation(m_split[:, j, 0, :], mix_s[:, j % 2, :], ACT.Copy).then_inc(mix_hi, 1)

            for j in range(KT):
                ahead(C_AO + j)
                act.wait_ge(ft_done, ao_gate(j))
                if j >= 2:
                    act.wait_ge(mix_done, j - 1)
                act.activation(sg_s[:, j % 2, :], ps[:, 6 - 2 * (j % 2), :], ACT.Sigmoid).then_inc(sg_done, 1)
                if j:
                    mix_high(j - 1)
            mix_high(KT - 1)
            for g in range(2):
                ahead(C_WO2 + 2 * g)
                act.wait_ge(tok_half, G_WO2 + g + 1)
                ahead(C_WO2 + 2 * g + 1)

            for tb in range(TB):
                if tb == TB - 1:
                    transposed(5, blocks=[0])
                norm(4, tb, res_done, TB + tb + 1)
            transposed(5, blocks=range(1, TB))

            def hi_of(r, i, k):
                s = k % RING
                pair = k % MOE_RING // 2
                act.wait_ge(moe_ld[pair], moe_loads(r, i + k // MOE_RING, pair))
                act.wait_ge(moe_mm, r * PASS + 12 * i + (k + 1))
                act.activation(w_hi[:, s, :], moe_st[k % MOE_RING], ACT.Copy).then_inc(w_hi_done, 1)

            def rows_hi(r, i, c):
                act.wait_ge(xe_tp, 2 * moe(r, i, c) + 5)
                act.activation(xeT[:, c % 2, 0, :, :].rearrange("p k t -> p (k t)"), ps[:, 6, 0:KT * CAP], ACT.Copy).then_inc(xe_hi, 1)

            def silu(r, i, c, k):
                wait(act, hid_mul, moe(r, i, c))
                act.wait_ge(moe_mm, r * PASS + 12 * i + (k + 2 + RING))
                act.activation(sil[0:CAP, :], ps[0:CAP, 0, :], ACT.Silu).then_inc(sil_done, 1)

            def hidden_hi(r, i, c):
                act.wait_ge(hid_mul, moe(r, i, c) + 1)
                act.activation(hid_b[0:CAP, 0, :], hid_f[0:CAP, :], ACT.Copy).then_inc(hid_hi, 1)

            def hidden_copy(r, i, c):
                act.wait_ge(hid_tp, moe(r, i, c) + 1)
                act.activation(hidT.rearrange("p a f t -> p (a f t)"), ps[:, 4, 0:2 * DE // P * CAP], ACT.Copy).then_inc(hid_c, 1)

            def outputs(r, i, c, k):
                act.wait_ge(moe_mm, r * PASS + 12 * i + (k + 2 + RING))
                act.wait_ge(y_stored[c % 2], 16 * (pairs_of(r, i, c) + 1))
                act.activation(y_st[0:CAP, c % 2, :].rearrange("p (b n) -> p b n", b=2), ps[0:CAP, 2:4, :], ACT.Copy).then_inc(y_out, 1)

            def first(r):
                if not isinstance(r, int):
                    for k in range(AHEAD):
                        hi_of(r, 0, k)
                rows_hi(r, 0, 0)
                hi_of(r, 0, 3)
                hi_of(r, 0, 4)
                silu(r, 0, 0, 0)
                rows_hi(r, 0, 1)
                hi_of(r, 0, 5)
                hi_of(r, 0, 6)

            def step(r, i, c, more=True):
                k = 6 * c - 2
                hidden_hi(r, i, c - 1)
                hi_of(r, i, k + 3)
                silu(r, i, c, k)
                hidden_copy(r, i, c - 1)
                if more:
                    rows_hi(r, i, c + 1)
                hi_of(r, i, k + 4)
                hi_of(r, i, k + 5)
                hi_of(r, i, k + 6)
                outputs(r, i, c - 1, k + 2)
                hi_of(r, i, k + 7)
                if more:
                    hi_of(r, i, k + 8)

            def last(r):
                step(r, 0, NE - 1, more=False)
                hidden_hi(r, 0, NE - 1)
                hidden_copy(r, 0, NE - 1)
                outputs(r, 0, NE - 1, PASS - 2)

            one_pass = every_expert(first, step, last)
            for k in range(AHEAD):
                hi_of(0, 0, k)
            act.wait_ge(rt_x, 1)
            act.activation(r_exp, r_exp, ACT.Exp).then_inc(rt_e, 1)
            act.drain().then_inc(y_out, 1)
            one_pass(act, 0)
            more_passes(act, one_pass)
            for tb in range(TB):
                norm(5, tb, res_done, 2 * TB + tb + 1)

        @block.vector
        def _(dve):
            split = [0]

            def lo(n):
                dve.wait_ge(w_hi_done, n + 1)
                lo_n, hi_n = w_lo[:, n % RING, :], w_hi[:, n % RING, :]
                if n == C_KEYS:
                    lo_n, hi_n = (v.rearrange("p q k -> p (q k)") for v in (keys_lo, keys_hi))
                dve.tensor_tensor(lo_n, w_st[:, n % RING, :], hi_n, ALU.subtract).then_inc(w_lo_done, 1)

            def ahead(n):
                while split[0] <= min(n + AHEAD, C_MOE - 1):
                    lo(split[0])
                    split[0] += 1

            def normalise(use, tb, dst=xn, done=xn_done, src=None):
                dve.wait_ge(sd_done, TB * use + tb + 1)
                dve.reciprocal(rstd[:, tb:tb + 1], sd[:, tb:tb + 1])
                dve.drain()
                if tb == 0:
                    dve.wait_ge(row_ld[use % 2], 16 * (use // 2 + 1))
                dve.scalar_tensor_tensor(dst[:, tb, :], res[:, tb, :] if src is None else src, rstd[:, tb:tb + 1], row[:, use % 2, :], ALU.mult, ALU.mult).then_inc(done, 1)
                if tb == TB - 1:
                    dve.drain().then_inc(row_used, 1)

            def transposed(use, weight=None, dst_hi=a_hi, dst_lo=a_lo, blocks=range(TB)):
                for n in range(2 * blocks[0], 2 * blocks[-1] + 2):
                    dve.wait_ge(tp_hi, KT * use + n + 1)
                    if weight is None:
                        part = (slice(None), slice((n % 2) * 4, (n % 2) * 4 + 4), slice((n // 2) * P, (n // 2 + 1) * P))
                        dve.tensor_tensor(dst_lo[part], ps[:, n % 2, :].rearrange("p (k t) -> p k t", k=4), dst_hi[part], ALU.subtract).then_inc(tp_lo, 1)
                    else:
                        dve.scalar_tensor_tensor(dst_lo[:, n, :], ps[:, n % 2, :], weight(n), dst_hi[:, n, :],
                                                 ALU.mult, ALU.subtract).then_inc(tp_lo, 1)

            dve.wait_ge(const_done, 1)
            for half in range(2):
                rows = slice(half * GC, (half + 1) * GC)
                dve.tensor_copy(mask64[rows, :], tri_le[rows, rows])
            for tb in range(TB):
                if tb == TB - 1:
                    transposed(0, blocks=[0])
                normalise(0, tb)
            ahead(-AHEAD)
            transposed(0, blocks=range(1, TB))
            dve.wait_ge(cols_ld, 16)
            ahead(-1)
            dve.wait_ge(small_hi_done, 1)
            dve.tensor_tensor(small_lo[:, :], small[:, 0:N_SPLIT], small_hi[:, :], ALU.subtract).then_inc(small_done, 1)
            d = slice(DT0, DT0 + SH)
            for m in range(2 * N_P1F):
                ahead(C_P1F + m // 2)
                if m == 1:
                    dve.wait_ge(sm_out, 1)
                    dve.tensor_scalar(dtm[d, 0, :], sm[d, :], col("dt_b")[d, :], None, ALU.add).then_inc(dt_x, 1)
                    for j in range(2):
                        dve.wait_ge(gate_mm, j + 1)
                        dve.tensor_scalar(g_cum[:, j, :], ps[:, j, :], col("gla_b", j), None, ALU.add).then_inc(gate_x, 1)
                    dve.drain()
                    for j in range(2):
                        dve.tensor_scalar(lg[:, j, :], g_cum[:, j, :], 0.0, 1.0 / GATE_NORM, ALU.min, ALU.mult)
                if m == 3:
                    dve.wait_ge(dt_ln, 1)
                    dve.scalar_tensor_tensor(dtm[d, 2, :], dtm[d, 0, :], 0.0, dtm[d, 1, :], ALU.max, ALU.add)
                    dve.drain()
                    dve.tensor_scalar(dtm[d, 3, :], dtm[d, 2, :], ea[d, 0:1], -1.0, ALU.mult, ALU.mult).then_inc(dt_done, 1)
                    for j in range(2):
                        dve.wait_ge(gate_ln, j + 1)
                        dve.scalar_tensor_tensor(lg[:, j, :], e_pos[:, j, :], -1.0 / GATE_NORM, lg[:, j, :], ALU.mult, ALU.add)
                        dve.drain()
                        dve.tensor_tensor_scan(g_cum[:, j, :], reset[:, :], lg[:, j, :], 0.0, ALU.mult, ALU.add)
                        dve.drain()
                        by_chunk = g_cum[:, j, :].rearrange("p (c i) -> p c i", i=GC)
                        dve.tensor_tensor(lg[:, j, :].rearrange("p (c i) -> p c i", i=GC), by_chunk[:, :, GC - 1:GC].to_broadcast([P, NGC, GC]),
                                          by_chunk, ALU.subtract).then_inc(gate_cum, 1)
                if m >= 4:
                    f = m - 4
                    dve.wait_ge(ft_out, F_P1 + m + 1)
                    dve.tensor_scalar(xc[:, f, :], xbc[:, f, 1:1 + T], col("conv_w", f * SCONV), col("conv_b", f), ALU.mult, ALU.add)
                    for k in range(1, SCONV):
                        dve.drain()
                        last = dve.scalar_tensor_tensor(xc[:, f, :], xbc[:, f, 1 + k:1 + k + T], col("conv_w", f * SCONV + k),
                                                        xc[:, f, :], ALU.mult, ALU.add)
                    last.then_inc(conv_done, 1)
            for j in range(2):
                dve.wait_ge(gate_exp, j + 1)
                dve.tensor_tensor(qk[:, j, :], qk[:, j, :], e_pos[:, j, :], ALU.mult)
                dve.tensor_tensor(k_end[:, j, :], qk[:, 2 + j, :], lg[:, j, :], ALU.mult)
                dve.tensor_tensor(qk[:, 2 + j, :], qk[:, 2 + j, :], e_neg[:, j, :], ALU.mult).then_inc(gla_qk, 1)
            ahead(C_P1T)
            ahead(C_P1T + 1)
            for hh in range(2):
                dve.wait_ge(gla_att, hh + 1)
                dve.tensor_tensor(att_s[:, hh, :, :], ps[:, 4 + hh, :].rearrange("p (c i) -> p c i", i=GC),
                                  mask64[:, :].unsqueeze(1).to_broadcast([P, 8, GC]), ALU.mult).then_inc(gla_attc, 1)
            dve.memset(s_gla[:, :, 0, :], 0.0)
            ahead(C_P1T + 2)
            ahead(C_P1T + 3)
            ahead(C_P1T + 4)
            dve.drain()
            for c in range(NGC - 1):
                for j in range(2):
                    if c == 0:
                        dve.wait_ge(gla_st, 2)
                    last = dve.scalar_tensor_tensor(s_gla[:, j, c + 1, :], s_gla[:, j, c, :], e_pos[:, j, c * GC + GC - 1:c * GC + GC],
                                                    ps[:, 4 + j * 2 + c % 2, (c // 2) * GDV:(c // 2 + 1) * GDV], ALU.mult, ALU.add)
                if c < NGC - 2:
                    dve.drain()
            last.then_inc(gla_S, 1)
            ahead(C_P1T + 5)
            for tb in range(TB):
                b = (tb % 2) * 3
                dve.wait_ge(gla_oc, tb + 1)
                pairs = o_s[:, tb % 2, :].rearrange("p (j h v) -> p j h v", j=2, h=2)
                for hh in range(2):
                    last = dve.tensor_tensor(pairs[:, :, hh, :], pairs[:, :, hh, :],
                                             ps[:, b + 1 + hh, 0:2 * GDV].rearrange("p (j v) -> p j v", j=2), ALU.add)
                last.then_inc(gla_od, 1)
                dve.wait_ge(gla_sd, tb + 1)
                dve.reciprocal(rstd[:, 0:GH], sd[:, 0:GH])
                dve.drain()
                for h in range(GH):
                    hs = slice(h * GDV, (h + 1) * GDV)
                    last = dve.scalar_tensor_tensor(xn[:, tb, hs], o_s[:, tb % 2, hs], rstd[:, h:h + 1], xn[:, tb, hs], ALU.mult, ALU.mult)
                last.then_inc(gla_y, 1)

            dve.wait_ge(xt_c, TB + 1)
            dve.memset(s_ssd[:, 0, :], 0.0)
            for tb in range(TB):
                heads = lambda v: v.rearrange("p (h e) -> p h e", e=SP_)
                dve.tensor_tensor(heads(xdt[:, tb, :]), heads(xt[:, tb, :]), dta[:, tb, 0, :].unsqueeze(2).to_broadcast([P, SH, SP_]), ALU.mult)
                dve.drain()
                dve.tensor_tensor(heads(xdte[:, tb, :]), heads(xdt[:, tb, :]), ecum[:, 1, tb, :].unsqueeze(2).to_broadcast([P, SH, SP_]),
                                  ALU.mult).then_inc(xd_done, 1)
                if tb == 0:
                    dve.drain().then_inc(ssd_S, 1)
                for g in range(SG):
                    dve.wait_ge(ssd_L, 2 * tb + g + 1)
                    if tb >= 1:
                        dve.wait_ge(ssd_y, tb)
                    dve.tensor_tensor(w_s[:, g, :].rearrange("p (j l) -> p j l", j=SJ), l_s[:, g, :].rearrange("p (j l) -> p j l", j=SJ),
                                      ps[:, 2 + g, 0:P].unsqueeze(1).to_broadcast([P, SJ, P]), ALU.mult).then_inc(ssd_W, 1)
                dve.wait_ge(ssd_st, tb + 1)
                if tb < TB - 1:
                    for g in range(SG):
                        n = slice(g * SN, (g + 1) * SN)
                        dve.tensor_tensor(heads(s_ssd[n, tb + 1, :]), heads(s_ssd[n, tb, :]),
                                          ecum[n, 2, tb, g * SJ:(g + 1) * SJ].unsqueeze(2).to_broadcast([SN, SJ, SP_]), ALU.mult)
                    dve.drain()
                    dve.tensor_tensor(s_ssd[:, tb + 1, :], s_ssd[:, tb + 1, :], ps[:, 6, 0:SJ * SP_], ALU.add).then_inc(ssd_S, 1)
                dve.wait_ge(ssd_y, tb + 1)
                dve.tensor_tensor(heads(y_t[:, 1, :]), heads(xt[:, tb, :]), col("d_skip", 0, SH).unsqueeze(2).to_broadcast([P, SH, SP_]), ALU.mult)
                for g in range(SG):
                    gs = slice(g * SJ * SP_, (g + 1) * SJ * SP_)
                    dve.tensor_tensor(heads(y_t[:, 0, gs]), heads(ps[:, 7 - 3 * g, 0:SJ * SP_]),
                                      ecum[:, 0, tb, g * SJ:(g + 1) * SJ].unsqueeze(2).to_broadcast([P, SJ, SP_]), ALU.mult)
                dve.drain()
                dve.tensor_tensor(y_t[:, 1, :], y_t[:, 1, :], y_t[:, 0, :], ALU.add)
                dve.drain()
                dve.tensor_tensor(y_t[:, 1, :], y_t[:, 1, :], ps[:, 5, :], ALU.add).then_inc(ssd_yd, 1)
                dve.drain()
                dve.tensor_tensor(xn[:, tb, GW:], y_t[:, 1, :], xn[:, tb, GW:], ALU.mult).then_inc(ssd_yc, 1)
                dve.drain()
            dve.wait_ge(ssd_sd, 1)
            dve.reciprocal(rstd[:, 0:TB * SG], sd[:, 0:TB * SG])
            dve.drain()
            for tb in range(TB):
                gs = xn[:, tb, GW:].rearrange("p (g n) -> p g n", g=SG)
                dve.tensor_tensor(gs, gs, rstd[:, tb * SG:(tb + 1) * SG].unsqueeze(2).to_broadcast([P, SG, SJ * SP_]), ALU.mult).then_inc(xn_done, 1)
            transposed(1, lambda kt: col("gla_norm") if kt < 4 else col("ssd_norm", kt - 4))
            for g in range(2):
                ahead(C_WOUT + 2 * g)
                ahead(C_WOUT + 2 * g + 1)
                for tb in range(TB):
                    dve.wait_ge(tok_done, TB * (G_WOUT + g) + tb + 1)
                    s = slice(g * 512, (g + 1) * 512)
                    last = dve.tensor_tensor(res[:, tb, s], res[:, tb, s], ps[:, 4 - 4 * g + tb, :], ALU.add)
                    if g == 1:
                        last.then_inc(res_done, 1)
                        if tb:
                            normalise(1, tb - 1)
            transposed(2, blocks=[0])
            normalise(1, TB - 1)

            transposed(2, blocks=range(1, TB))
            for m in range(2 * N_QUERY):
                ahead(C_QUERY + m // 2)
                dve.wait_ge(q_hi_done, m + 1)
                dve.tensor_tensor(q_lo[:, m, :], ps[:, 4 + (F_QUERY + m) % 4, :], q_hi[:, m, :], ALU.subtract).then_inc(ft_out, 1)
            ahead(C_KEYS)
            dve.drain().then_inc(s_out, 2)

            def lo_in_loop(c, n):
                s = (c + AHEAD) % RING
                dve.wait_ge(w_hi_done, n + 1)
                dve.tensor_tensor(w_lo[:, s, :], w_st[:, s, :], w_hi[:, s, :], ALU.subtract).then_inc(w_lo_done, 1)

            def best_keys(i, h):
                s_ps = ps[:, 2 + h % 2, 0:2 * PK].rearrange("p (a k) -> p a k", a=2)
                for a in range(2):
                    dve.max(top_v[:, a, 0:8], s_ps[:, a, :])
                dve.drain()
                for a in range(2):
                    dve.max_index(top_i[:, a, 0:8], top_v[:, a, 0:8], s_ps[:, a, :])
                    last = dve.match_replace(s_cut[:, a, :], top_v[:, a, 0:8], s_ps[:, a, :], LOWEST)
                last.then_inc(s_out, 1)
                dve.drain()
                for a in range(2):
                    dve.max(top_v[:, a, 8:16], s_cut[:, a, :])
                dve.drain()
                for a in range(2):
                    dve.max_index(top_i[:, a, 8:16], top_v[:, a, 8:16], s_cut[:, a, :])
                square = [P, PTOP, PTOP]
                dve.tensor_tensor(cand, top_v[:, 0, :].unsqueeze(2).to_broadcast(square), top_v[:, 1, :].unsqueeze(1).to_broadcast(square), ALU.add)
                dve.drain()
                flat, flat_cut = cand.rearrange("p a b -> p (a b)"), cand_cut.rearrange("p a b -> p (a b)")
                dve.max(best_v[:, 0:8], flat)
                dve.drain()
                dve.max_index(best_p[:, 0:8], best_v[:, 0:8], flat)
                dve.match_replace(flat_cut, best_v[:, 0:8], flat, LOWEST)
                dve.drain()
                dve.max(best_v[:, 8:16], flat_cut)
                dve.drain()
                dve.max_index(best_p[:, 8:16], best_v[:, 8:16], flat_cut)
                dve.drain()
                dve.tensor_scalar(best_k[:, 0, :], best_p, 4, None, ALU.logical_shift_right)
                dve.tensor_scalar(best_k[:, 1, :], best_p, PTOP - 1, None, ALU.bitwise_and)
                at = slice(h * PTOP, (h + 1) * PTOP)
                dve.tensor_copy(score.rearrange("p (t s) -> p t s", t=TB)[:, i, at], best_v)
                dve.drain()
                for a in range(2):
                    dve.tensor_tensor(pick[:, a, :, :], best_k[:, a, :].unsqueeze(2).to_broadcast(square),
                                      iota_f[:, 0:PTOP].unsqueeze(1).to_broadcast(square), ALU.is_equal)
                dve.drain()
                for a in range(2):
                    dve.tensor_tensor(pick[:, a, :, :], pick[:, a, :, :], top_i[:, a, :].unsqueeze(1).to_broadcast(square), ALU.mult)
                dve.drain()
                for a, key in enumerate((key1, key2)):
                    dve.tensor_reduce(key.rearrange("p (t s) -> p t s", t=TB)[:, i, at], pick[:, a, :, :], AX_X, ALU.add)

            with dve.Fori(0, 4) as i:
                for c in range(8):
                    dve.wait_ge(s_done, 8 * i + c + 1)
                    lo_in_loop(c, C_U + 8 * i + c + AHEAD)
                    best_keys(i, c)
            dve.drain()
            by_head = lambda v: v.rearrange("p (h s) -> p h s", s=PTOP)
            whole = [P, TB * PH, PTOP]
            dve.tensor_tensor(by_head(gate_t), by_head(score), by_head(score)[:, :, 0:1].to_broadcast(whole), ALU.subtract).then_inc(soft_x, 1)
            dve.wait_ge(soft_e, 1)
            dve.tensor_reduce(soft[:, 0, :], by_head(gate_t), AX_X, ALU.add)
            dve.drain()
            dve.reciprocal(soft[:, 1, :], soft[:, 0, :])
            dve.drain()
            dve.tensor_tensor(by_head(score), by_head(gate_t), soft[:, 1, :].unsqueeze(2).to_broadcast(whole), ALU.mult).then_inc(soft_done, 1)
            dve.wait_ge(slot_tp, 1)
            dve.tensor_copy(slot_T[:, 0, :], ps[:, 4, :])
            dve.tensor_copy(slot_T[:, 1, :], ps[:, 5, :])
            dve.tensor_copy(g_b16, ps[:, 6, :])
            dve.drain()
            dve.tensor_copy(slot_T[:, 2, :], g_b16)
            dve.tensor_tensor(slot_T[:, 3, :], ps[:, 6, :], g_b16, ALU.subtract).then_inc(slot_done, 1)
            dve.drain()
            with dve.Fori(4, 8) as i:
                for c in range(8):
                    if c % 4 == 0:
                        first = (i - 4) * P + (c // 4) * 64
                        dve.drain()
                        dve.tensor_copy(c_slot, slot_T[:, :, bass.ds(first, 64)])
                        dve.drain()
                    for t in range(2):
                        if t == 1:
                            lo_in_loop(c, C_U + 8 * i + c + AHEAD)
                        at = 2 * c + t
                        dve.wait_ge(g_done, 2 * (16 * (i - 4) + at) + 2)
                        toks = slice((at % 8) * 8, (at % 8) * 8 + 8)
                        dve.tensor_tensor(oh_b[:, at % 2, :, :], iota_b[:, :].unsqueeze(1).to_broadcast([P, 8, PK]),
                                          c_slot[:, 1, toks].unsqueeze(2).to_broadcast([P, 8, PK]), ALU.is_equal)
                        for r in range(8):
                            k = (at % 8) * 8 + r
                            for part in range(2):
                                last = dve.tensor_scalar(oh_a[:, at % 2, r, part, :], iota_b[:, :], c_slot[:, 0, k:k + 1],
                                                         c_slot[:, 2 + part, k:k + 1], ALU.is_equal, ALU.mult)
                        last.then_inc(oh_done, 1)
            dve.wait_ge(g_out, 4 + 2 * 64)
            with dve.Fori(0, N_V // 4) as i:
                for c in range(4):
                    dve.wait_ge(ga_ld[c % 2], 16 * (2 * i + c // 2 + 1))
                    dve.wait_ge(g_ld[c % 2], 16 * (2 * i + c // 2 + 1))
                    for j in range(2):
                        by_group = lambda v: v[:, 0:7 * (T // 8)].rearrange("p (g t) -> p g t", g=7)
                        dve.tensor_tensor(by_group(h_f[:, c % 2, j, :]), by_group(ga_in[:, c % 2, j, :]), g_in[:, c % 2, :, j, :], ALU.mult)
                    last_t = slice(7 * (T // 8), T)
                    dve.tensor_tensor(h_f[:, c % 2, :, last_t], ga_in[:, c % 2, :, last_t], g_st[:, 1, bass.ds(8 * i + 2 * c, 2), :], ALU.mult).then_inc(h_mul, 1)
                    dve.wait_ge(h_hi_done, 4 * i + c + 1)
                    dve.tensor_tensor(h_lo[:, c % 2, :, :], h_f[:, c % 2, :, :], h_hi[:, c % 2, :, :], ALU.subtract).then_inc(h_lo_done, 1)
                    lo_in_loop(c, C_V + 4 * i + c + AHEAD)
            split[0] = C_CONV + AHEAD
            for t in range(TB + 1):
                if t < TB:
                    normalise(2, t, res, res2_done, ps[:, 2 * t:2 * t + 2, :].rearrange("p b n -> p (b n)"))
                if t >= 1:
                    normalise(3, t - 1)
                if t >= 2:
                    transposed(3, blocks=[t - 2])
            dve.memset(cum_b, 0.0)
            dve.tensor_tensor(head_b[:, :], ident_b[:, 0:AH], ident_b[:, 32:32 + AH], ALU.add)
            dve.drain()
            dve.tensor_tensor(head_b[:, :], head_b[:, :], ident_b[:, 64:64 + AH], ALU.add)
            dve.memset(f_one[0:AH, :], 1.0)
            dve.memset(z_s[:, 0:4], 0.0)
            transposed(3, blocks=[TB - 1])
            dve.wait_ge(f_mm, 1)
            dve.tensor_scalar(f_x[0:AH, :], ps[0:AH, 2, :], col("b_forget")[0:AH, :], None, ALU.add).then_inc(f_xs, 1)
            dve.wait_ge(f_ln, 1)
            dve.scalar_tensor_tensor(f_x[0:AH, :], f_x[0:AH, :], 0.0, f_e[0:AH, :], ALU.min, ALU.subtract)
            dve.drain()
            dve.tensor_tensor_scan(n_cum[0:AH, :], f_one[0:AH, :], f_x[0:AH, :], 0.0, ALU.mult, ALU.subtract)
            dve.drain()
            parts = [cum_b[32 * a:32 * a + AH, :] for a in range(3)]
            dve.tensor_copy(parts[0], n_cum[0:AH, :])
            dve.drain()
            dve.tensor_tensor(c_rest[0:AH, 0, :], n_cum[0:AH, :], parts[0], ALU.subtract)
            dve.drain()
            dve.tensor_copy(c_rest[0:AH, 1, 0:T // 2].bitcast(BF16), c_rest[0:AH, 0, :])
            dve.tensor_copy(parts[1], c_rest[0:AH, 0, :])
            dve.drain()
            dve.tensor_tensor(parts[2], c_rest[0:AH, 0, :], c_rest[0:AH, 1, 0:T // 2].bitcast(BF16), ALU.subtract).then_inc(f_cum, 1)
            dve.drain()

            def conv_low(j):
                dve.wait_ge(cv_hi, j + 1)
                dve.tensor_tensor(c_lo[:, j, :], cv_s[:, j % 2, :], c_hi[:, j, :], ALU.subtract).then_inc(cv_lo, 1)

            for j in range(KT):
                for a in range(3):
                    ahead(C_CONV + (3 * j + a) // 2)
                dve.wait_ge(ft_out, F_CONV + 3 * j + 2)
                dve.tensor_tensor(z_s[:, 4:], cu_s[:, j % 2, :], cc_s[:, j % 2, :], ALU.mult)
                dve.drain()
                dve.tensor_scalar(acc_s, z_s[:, 2:2 + T], col("conv_w2", j * CONVW), col("conv_b2", j), ALU.mult, ALU.add)
                for k in range(1, CONVW):
                    dve.drain()
                    dve.scalar_tensor_tensor(acc_s, z_s[:, 2 + k:2 + k + T], col("conv_w2", j * CONVW + k), acc_s, ALU.mult, ALU.add)
                dve.drain()
                dve.wait_ge(ft_out, F_CONV + 3 * j + 3)
                dve.tensor_tensor(cv_s[:, j % 2, :], acc_s, cb_s[:, j % 2, :], ALU.mult).then_inc(cv_mul, 1)
                if j:
                    conv_low(j - 1)
            conv_low(KT - 1)

            def conv_branch(j):
                dve.wait_ge(sg_done, j + 1)
                dve.wait_ge(ft_done, f_of(CHUNK_CO(j)) + 2)
                dve.tensor_tensor(m1[:, j, :], ps[:, 7, :], sg_s[:, j % 2, :], ALU.mult).then_inc(m1_done, 1)

            for g in range(2):
                ahead(C_V2 + 2 * g)
                ahead(C_V2 + 2 * g + 1)

            def low_queries(j):
                dve.wait_ge(qk_hi, 2 * j + 1)
                for hh in range(2):
                    rows, others = (slice(n * ADH, (n + 1) * ADH) for n in (hh, 1 - hh))
                    last = dve.scalar_tensor_tensor(q_s[others, j % 2, hh, :], ps[rows, 6, :], ADH ** -0.5, q_s[rows, j % 2, hh, :], ALU.mult, ALU.subtract)
                last.then_inc(qk_out, 1)

            def low_keys(j):
                dve.wait_ge(qk_hi, 2 * j + 2)
                for hh in range(2):
                    rows = slice(hh * ADH, (hh + 1) * ADH)
                    for half in range(2):
                        last = dve.tensor_tensor(k_lo[half * ADH:(half + 1) * ADH, j % 2, hh, :], ps[rows, 7, :], k_hi[rows, j % 2, hh, :], ALU.subtract)
                last.then_inc(qk_out, 1)

            low_queries(0)
            low_keys(0)
            for u in range(len(UNITS) + 3):
                if u < len(UNITS):
                    h, qb = UNITS[u]
                    dve.wait_ge(at_s, u + 1)
                    if u >= 3:
                        dve.wait_ge(at_p, u - 2)
                    dve.tensor_reduce(n_max[:, u % 3:u % 3 + 1], ps[:, (0, 1, 5)[u % 3], 0:(qb + 1) * P], AX_X, ALU.max, negate=True).then_inc(at_max, 1)
                    j, at = h // 2, u % 8
                    if at == 0:
                        ahead(CHUNK_QK(j + 1) if j + 1 < AH // 2 else CHUNK_CO(j))
                    if at == 1 and j:
                        conv_branch(j - 1)
                if 2 <= u < len(UNITS) + 2:
                    v = u - 2
                    n = UNITS[v][1] + 1
                    dve.wait_ge(at_t, v + 1)
                    if v >= 2:
                        dve.wait_ge(at_o, v - 1)
                    dve.tensor_copy(pT_s[:, v % 2, 0:n, :], ps[:, 2 + v % 2, 0:n * P].rearrange("p (k q) -> p k q", k=n)).then_inc(at_tc, 1)
                if u >= 3:
                    v = u - 3
                    h, qb = UNITS[v]
                    dve.reciprocal(r_inv[:, v % 2:v % 2 + 1], r_sum[:, v % 4:v % 4 + 1])
                    dve.drain()
                    dve.wait_ge(at_o, v + 1)
                    last = dve.tensor_scalar(xn[:, qb, h * ADH:(h + 1) * ADH], ps[:, 4, 0:ADH], r_inv[:, v % 2:v % 2 + 1], None, ALU.mult)
                    last.then_inc(at_out, 1)
                if u < len(UNITS) and j + 1 < AH // 2:
                    if at == 2:
                        low_queries(j + 1)
                    if at == 4:
                        low_keys(j + 1)
                    if at == 5:
                        ahead(CHUNK_CO(j))
            conv_branch(KT - 1)
            dve.drain().then_inc(xn_done, TB)
            transposed(4, None, c_hi, c_lo)

            def mix_low(j):
                dve.wait_ge(mix_hi, j + 1)
                dve.tensor_tensor(m_split[:, j, 1, :], mix_s[:, j % 2, :], m_split[:, j, 0, :], ALU.subtract).then_inc(mix_lo, 1)

            for j in range(KT):
                ahead(C_AO + j)
                dve.wait_ge(sg_done, KT + j + 1)
                dve.wait_ge(ft_done, ao_out(j))
                dve.tensor_tensor(prod_s[:, j % 2, :], ps[:, 7 - 2 * (j % 2), :], sg_s[:, j % 2, :], ALU.mult)
                dve.drain()
                dve.tensor_tensor(mix_s[:, j % 2, :], prod_s[:, j % 2, :], m1[:, j, :], ALU.add).then_inc(mix_done, 1)
                if j:
                    mix_low(j - 1)
            mix_low(KT - 1)
            for g in range(2):
                ahead(C_WO2 + 2 * g)
                ahead(C_WO2 + 2 * g + 1)
                for tb in range(TB):
                    dve.wait_ge(tok_done, TB * (G_WO2 + g) + tb + 1)
                    s = slice(g * 512, (g + 1) * 512)
                    last = dve.tensor_tensor(res[:, tb, s], res[:, tb, s], ps[:, 4 * g + tb, :], ALU.add)
                    if g == 1:
                        last.then_inc(res_done, 1)
                        if tb:
                            normalise(4, tb - 1)
            transposed(5, blocks=[0])
            normalise(4, TB - 1)

            transposed(5, blocks=range(1, TB))

            def rows_of_pass(r):
                if not isinstance(r, int):
                    dve.tensor_scalar(now, now, 1.0, None, ALU.add)
                    dve.drain()
                for s in range(2):
                    dve.scalar_tensor_tensor(tok_now[:, s, :], blk_f[:, 0, s, :], now, tok_f[:, :], ALU.is_equal, ALU.mult)
                dve.drain()
                dve.tensor_tensor(tok_e.rearrange("p s t e -> p (s t) e"), e_one.rearrange("p s t e -> p (s t) e"),
                                  tok_now.rearrange("p s t -> p (s t)").unsqueeze(2).to_broadcast([P, 2 * TB, NE]), ALU.mult).then_inc(rt_tok, 1)

            def lo_of(r, i, k):
                s = k % RING
                dve.wait_ge(w_hi_done, r * PASS + 12 * i + (C_MOE + k + 1))
                dve.tensor_tensor(w_lo[:, s, :], moe_st[k % MOE_RING], w_hi[:, s, :], ALU.subtract).then_inc(w_lo_done, 1)

            dve.memset(lr_g, LOWEST)
            dve.wait_ge(rt_mm, 1)
            dve.tensor_copy(lr, ps[:, 2, 0:TB * SM_R].rearrange("p (t n) -> p t n", t=TB))
            dve.drain()
            dve.tensor_copy(lr_g[:, :, 0:EG], lr[:, :, 0:EG])
            dve.drain()
            for tb in range(TB):
                dve.max(g_max[:, tb, :], lr_g[:, tb, :])
            dve.drain()
            for tb in range(TB):
                dve.max_index(g_idx[:, tb, :], g_max[:, tb, :], lr_g[:, tb, :])
            dve.tensor_tensor(r_exp[:, :, 0:EG], lr[:, :, 0:EG], g_max[:, :, 0:1].to_broadcast([P, TB, EG]), ALU.subtract)
            dve.drain()
            dve.tensor_copy(g_num, g_idx[:, :, 0])
            dve.drain()
            dve.tensor_tensor(g_one, g_num.unsqueeze(2).to_broadcast([P, TB, EG]), iota_f[:, 0:EG].unsqueeze(1).to_broadcast([P, TB, EG]), ALU.is_equal)
            dve.drain()
            dve.tensor_tensor(le_all, lr[:, :, EG:].rearrange("p t (g e) -> p t g e", g=EG), g_one.unsqueeze(3).to_broadcast([P, TB, EG, EPG]), ALU.mult)
            dve.drain()
            dve.tensor_reduce(le_sel, le_all.rearrange("p t g e -> p t e g"), AX_X, ALU.add)
            dve.drain()
            for tb in range(TB):
                dve.max(e_max[:, tb, :], le_sel[:, tb, :])
            dve.drain()
            for tb in range(TB):
                dve.max_index(e_idx[:, tb, :], e_max[:, tb, :], le_sel[:, tb, :])
            dve.tensor_tensor(r_exp[:, :, EG:EG + 1], e_max[:, :, 1:2], e_max[:, :, 0:1], ALU.subtract).then_inc(rt_x, 1)
            dve.drain()
            for s in range(2):
                dve.tensor_copy(e_num[:, s, :], e_idx[:, :, s])
            dve.drain()
            for s in range(2):
                dve.scalar_tensor_tensor(e_of[:, s, :], g_num, float(EPG), e_num[:, s, :], ALU.mult, ALU.add)
            dve.drain()
            for s in range(2):
                dve.tensor_tensor(e_one[:, s, :, :], e_of[:, s, :].unsqueeze(2).to_broadcast([P, TB, NE]),
                                  iota_f[:, 0:NE].unsqueeze(1).to_broadcast([P, TB, NE]), ALU.is_equal)
            dve.drain()
            dve.tensor_tensor(e_any, e_one[:, 0, :, :], e_one[:, 1, :, :], ALU.add).then_inc(rt_pick, 1)
            lo_of(0, 0, 0)
            dve.wait_ge(rt_rank, 1)
            up_to = ps[:, 3, 0:TB * NE].rearrange("p (t e) -> p t e", t=TB)
            for s in range(2):
                dve.tensor_tensor(e_rank[:, s, :, :], e_one[:, s, :, :], up_to, ALU.mult)
            dve.drain()
            dve.tensor_reduce(rank_f, e_rank, AX_X, ALU.add)
            dve.drain()
            dve.tensor_scalar(rank_u, rank_f, -1.0, None, ALU.add)
            dve.drain()
            dve.tensor_scalar(blk_u[:, 0, :, :], rank_u, CAP.bit_length() - 1, None, ALU.logical_shift_right)
            dve.tensor_scalar(blk_u[:, 1, :, :], rank_u, CAP - 1, None, ALU.bitwise_and)
            dve.drain()
            dve.tensor_copy(blk_f, blk_u)
            dve.memset(now, 0.0)
            dve.drain()
            dve.tensor_tensor(row_one.rearrange("p s t c -> p (s t) c"), blk_f[:, 1, :, :].rearrange("p s t -> p (s t)").unsqueeze(2).to_broadcast([P, 2 * TB, CAP]),
                              iota_f[:, 0:CAP].unsqueeze(1).to_broadcast([P, 2 * TB, CAP]), ALU.is_equal)
            rows_of_pass(0)
            dve.scalar_tensor_tensor(e_blk, blk_f[:, 0, :, :], float(NE), e_of, ALU.mult, ALU.add)
            dve.drain()
            dve.scalar_tensor_tensor(to_y, e_blk, float(CAP), blk_f[:, 1, :, :], ALU.mult, ALU.add)
            dve.wait_ge(rt_all, 1)
            dve.tensor_reduce(n_rows, ps[:, 4, 0:NE], AX_X, ALU.max)
            dve.drain()
            dve.tensor_copy(n_rows_i, n_rows).then_inc(rt_dest, 1)
            dve.wait_ge(rt_e, 1)
            dve.tensor_reduce(g_sum, r_exp[:, :, 0:EG], AX_X, ALU.add)
            dve.drain()
            dve.scalar_tensor_tensor(w_den, r_exp[:, :, EG], 1.0, g_sum, ALU.add, ALU.mult)
            dve.drain()
            dve.reciprocal(w_tok[:, 0, :], w_den)
            dve.drain()
            dve.tensor_tensor(w_tok[:, 1, :], w_tok[:, 0, :], r_exp[:, :, EG], ALU.mult)

            def rows_lo(r, i, c):
                dve.wait_ge(xe_tp, 2 * moe(r, i, c) + 6)
                dve.tensor_copy(xeT[:, c % 2, 1, :, :].rearrange("p k t -> p (k t)"), ps[:, 7, 0:KT * CAP]).then_inc(xe_lo, 1)

            def hidden(r, i, c, k):
                dve.wait_ge(sil_done, moe(r, i, c) + 1)
                dve.wait_ge(moe_mm, r * PASS + 12 * i + (k + 2 + RING))
                dve.tensor_tensor(hid_f[0:CAP, :], sil[0:CAP, :], ps[0:CAP, 1, :], ALU.mult).then_inc(hid_mul, 1)

            def hidden_lo(r, i, c):
                dve.wait_ge(hid_hi, moe(r, i, c) + 1)
                dve.tensor_tensor(hid_b[0:CAP, 1, :], hid_f[0:CAP, :], hid_b[0:CAP, 0, :], ALU.subtract).then_inc(hid_lo, 1)

            def first(r):
                if not isinstance(r, int):
                    rows_of_pass(r)
                dve.wait_ge(rt_sum, r + 1)
                dve.tensor_copy(row_i[0:CAP, 0:NE], ps[0:CAP, 5, 0:NE]).then_inc(rt_row, 1)
                if not isinstance(r, int):
                    lo_of(r, 0, 0)
                lo_of(r, 0, 1)
                rows_lo(r, 0, 0)
                for k in range(2, 5):
                    lo_of(r, 0, k)
                rows_lo(r, 0, 1)
                lo_of(r, 0, 5)
                hidden(r, 0, 0, 2)
                lo_of(r, 0, 6)

            def step(r, i, c, more=True):
                k = 6 * c - 2
                hidden_lo(r, i, c - 1)
                lo_of(r, i, k + 3)
                lo_of(r, i, k + 4)
                if more:
                    rows_lo(r, i, c + 1)
                lo_of(r, i, k + 5)
                lo_of(r, i, k + 6)
                if more:
                    lo_of(r, i, k + 7)
                hidden(r, i, c, k + 4)
                lo_of(r, i, k + 8 if more else k + 7)

            def last(r):
                step(r, 0, NE - 1, more=False)
                hidden_lo(r, 0, NE - 1)

            one_pass = every_expert(first, step, last)
            one_pass(dve, 0)
            more_passes(dve, one_pass)

            for tb in range(TB):
                dve.wait_ge(yg_ld[tb], 32)
                for s in range(2):
                    last = dve.scalar_tensor_tensor(res[:, tb, :], y_g[:, tb, s, :], w_tok[:, s, tb:tb + 1], res[:, tb, :], ALU.mult, ALU.add)
                    if s == 0:
                        dve.drain()
                last.then_inc(res_done, 1)
                if tb:
                    normalise(5, tb - 1, done=end_done)
            normalise(5, TB - 1, done=end_done)


def _features(w):
    n = w.shape[1] // P
    return w.reshape(KT, P, n, P).transpose(2, 1, 0, 3).reshape(n, P, D)


def _pairs(tiles):
    n = tiles.shape[0] // 2
    return tiles.reshape(n, 2, P, -1).transpose(0, 2, 1, 3).reshape(n, P, CW)


def _tokens(w):
    n, k = w.shape[1] // 512, w.shape[0] // 512
    return w.reshape(k, 4, P, n, 512).transpose(3, 0, 2, 1, 4).reshape(n * k, P, CW)


def _column(v):
    return v.reshape(-1, P).T


def _rows(v, at=0):
    out = np.zeros((P, 1), np.float32)
    out[at:at + v.shape[0], 0] = v
    return out


def lay_out(a):
    w_in = a["w_in"][0]
    ends = np.cumsum([GQK, GQK, GW, GRANK, GW, SW, XBC, SH])
    q, k, v, rank, gate, z, xbc, dt = np.split(w_in, ends[:-1], axis=1)
    f = np.float32
    w = np.empty((N_CHUNKS, P, CW), f)

    def put(at, n, chunks):
        assert chunks.shape == (n, P, CW), (at, n, chunks.shape)
        w[at:at + n] = chunks

    put(C_P1F, N_P1F, _pairs(_features(np.concatenate([q, k, xbc], 1))))
    put(C_P1T, N_P1T, _tokens(np.concatenate([v, gate, z], 1)))
    put(C_WOUT, N_WOUT, _tokens(a["w_out"][0]))
    put(C_QUERY, N_QUERY, _pairs(_features(a["peer_w_query"][0])))
    put(C_KEYS, N_KEYS, a["peer_sub_keys"][0].reshape(2 * PH, PK, P).transpose(2, 0, 1).reshape(1, P, CW))
    put(C_U, N_U, _pairs(a["peer_u"][0].reshape(PK, PK, KT, P).transpose(0, 3, 2, 1).reshape(PK, P, D)))
    put(C_V, N_V, _pairs(a["peer_v"][0].reshape(PK, PK, D)))
    sizes = [D] * 6 + [AH, D, D]
    cb, cc, cu, q2, k2, v2, fl, gc, ga = np.split(a["w_in_2"], np.cumsum(sizes)[:-1], axis=1)
    mix = lambda *ws: _pairs(np.stack([_features(x) for x in ws], 1).reshape(-1, P, D))
    put(C_CONV, N_CONV, mix(cu, cc, cb))
    put(C_V2, N_V2, _tokens(v2))
    for j, (qk, co) in enumerate(zip(mix(q2, k2), mix(gc, a["w_conv_out_2"]))):
        w[CHUNK_QK(j)], w[CHUNK_CO(j)] = qk, co
    put(C_AO, N_AO, mix(ga, a["w_att_out_2"]))
    put(C_WO2, N_WO2, _tokens(a["w_out_2"]))
    gates = a["w_e_gate_2"].reshape(NE, 2, 4, P, DE).transpose(0, 1, 3, 2, 4).reshape(NE, 2, P, CW)
    ups = a["w_e_up_2"].reshape(NE, 2, 4, P, DE).transpose(0, 1, 3, 2, 4).reshape(NE, 2, P, CW)
    downs = a["w_e_down_2"].reshape(NE, 2, 2, P, D).transpose(0, 1, 3, 2, 4).reshape(NE, 2, P, CW)
    for e in range(NE):
        w[MOE_GATE(e):MOE_GATE(e) + 2] = gates[e]
        w[MOE_UP(e):MOE_UP(e) + 2] = ups[e]
        w[MOE_DOWN(e):MOE_DOWN(e) + 2] = downs[e]
    small_in = np.zeros((KT, P, SM_IN), f)
    small_in[:, :, 0:GRANK] = rank.reshape(KT, P, GRANK)
    small_in[:, :, DT0:DT0 + SH] = dt.reshape(KT, P, SH)
    router = np.concatenate([a["w_router_group_2"], a["w_router_expert_2"].transpose(1, 0, 2).reshape(D, NE)], 1)
    gate2 = np.zeros((P, GQK), f)
    gate2[0:GRANK] = a["gla_w_gate2"][0]
    by_part = lambda x: x.reshape(KT, P, -1).transpose(1, 0, 2).reshape(P, -1)
    small = np.concatenate([by_part(small_in), by_part(fl), by_part(router), gate2], 1)
    taps = lambda x: x.reshape(x.shape[0], -1, P).transpose(2, 1, 0).reshape(P, -1)
    table = np.concatenate([
        _column(a["gla_b_gate"][0]), _column(a["gla_norm_w"][0]), taps(a["ssd_conv_w"][0]),
        _column(a["ssd_conv_b"][0]), _rows(a["ssd_dt_bias"][0], DT0), _rows(a["ssd_a_log"][0], DT0),
        np.broadcast_to(a["ssd_d"][0], (P, SH)), _column(a["ssd_norm_w"][0]),
        taps(a["conv_w_2"]), _column(a["conv_b_2"]), _rows(a["b_forget_2"]),
    ], 1)
    return {
        "w_all": w, "x": np.ascontiguousarray(a["x"][0]), "cols": np.ascontiguousarray(table), "small": np.ascontiguousarray(small),
        "rows": np.stack([a["norm_mix_w"][0], a["norm_ffn_w"][0], a["norm_final_w"], a["norm_mix_g_2"], a["norm_ffn_g_2"], a["norm_final_g_2"]])[:, None],
    }


def kernel(**inputs):
    import concourse.bacc as bacc
    from concourse.bass_utils import run_bass_kernel_spmd

    arrays = lay_out({k: np.asarray(v) for k, v in inputs.items()})
    nc = bacc.Bacc("TRN2", target_bir_lowering=False, num_devices=1)
    args = [nc.dram_tensor("in_" + k, v.shape, mybir.dt.from_np(v.dtype), kind="ExternalInput").ap() for k, v in arrays.items()]
    out = nc.dram_tensor("out", (T, D), F32, kind="ExternalOutput").ap()
    build_program(nc, *args, out)
    r = run_bass_kernel_spmd(nc, [{"in_" + k: v for k, v in arrays.items()}], core_ids=[0])
    return r.results[0]["out"].reshape(1, T, D)
```
